# Optimizing a Trainium2 kernel written in Bass

```python
import math
import jax, jax.numpy as jnp
from jax import lax
import numpy as np

D_MODEL = 1024
BATCH = 1
SEQ = 256
DEPTH = 2

CTX_LEN = 256
GRID_W = 64
EPS = 1e-6

BR_WIDTH = D_MODEL // 2
N_BRANCH = 3

DA_SUB = 64
DA_VDIM = 2 * DA_SUB
DA_HEADS = BR_WIDTH // DA_VDIM
DA_QK = DA_HEADS * 2 * DA_SUB
BLOCK_Q = 128
ROPE_BASE = 10000.0
ROPE_NF = DA_SUB // 4

HY_WIDTH = BR_WIDTH
HY_SHORT = 3
HY_BANDS = 16
HY_EMB = 1 + 2 * HY_BANDS
HY_HIDDEN = 64
HY_TARGET = 1e-2
HY_FAST_DECAY = 0.3
HY_SLOW_DECAY = 1.5
HY_MIN_DECAY = math.log(HY_TARGET) / HY_SLOW_DECAY
HY_MAX_DECAY = math.log(HY_TARGET) / HY_FAST_DECAY

GM_WIDTH = BR_WIDTH
GM_GROUPS = 8
GM_CHUNK = 128

COL_K = 0
COL_V = COL_K + DA_QK
COL_Q = COL_V + BR_WIDTH
COL_GA = COL_Q + DA_QK
COL_HY = COL_GA + BR_WIDTH
COL_GB = COL_HY + 3 * HY_WIDTH
COL_GM = COL_GB + BR_WIDTH
COL_GC = COL_GM + 2 * GM_WIDTH
COL_MG = COL_GC + BR_WIDTH
COL_END = COL_MG + N_BRANCH * D_MODEL


def rms_norm(x, g):
    xf = x.astype(jnp.float32)
    y = xf * lax.rsqrt(jnp.mean(xf * xf, axis=-1, keepdims=True) + EPS)
    return (y * g.astype(jnp.float32)).astype(x.dtype)

def layer_norm(x, g, b):
    xf = x.astype(jnp.float32)
    mu = jnp.mean(xf, axis=-1, keepdims=True)
    var = jnp.mean(jnp.square(xf - mu), axis=-1, keepdims=True)
    y = (xf - mu) * lax.rsqrt(var + EPS)
    return (y * g.astype(jnp.float32) + b.astype(jnp.float32)).astype(x.dtype)

def modulation(cond, w, b):
    m = jax.nn.silu(cond) @ w + b
    return jnp.split(m, 3, axis=-1)

def axial_rope(row, col):
    inv = ROPE_BASE ** (-jnp.arange(ROPE_NF, dtype=jnp.float32) / ROPE_NF)
    ang = jnp.stack([row[:, None] * inv, col[:, None] * inv], axis=1)
    return jnp.cos(ang), jnp.sin(ang)

def apply_rope(x, cos, sin):
    xr = x.reshape(*x.shape[:-1], 2, 2, ROPE_NF)
    x1, x2 = xr[..., 0, :], xr[..., 1, :]
    cs, sn = cos.astype(x.dtype), sin.astype(x.dtype)
    out = jnp.stack([x1 * cs - x2 * sn, x2 * cs + x1 * sn], axis=-2)
    return out.reshape(x.shape)

def qk_heads(zs):
    b, n, _ = zs.shape
    return zs.reshape(b, n, DA_HEADS, 2, DA_SUB).transpose(0, 2, 3, 1, 4)

def v_heads(zs):
    b, n, _ = zs.shape
    return zs.reshape(b, n, DA_HEADS, DA_VDIM).transpose(0, 2, 1, 3)

def diff_attend(q, k, v, lam):
    b, h, _, n, _ = q.shape
    nb = n // BLOCK_Q
    qb = q.reshape(b, h, 2, nb, BLOCK_Q, DA_SUB).transpose(3, 0, 1, 2, 4, 5)
    scale = DA_SUB ** -0.5

    def one(qi):
        s = jnp.einsum('bhmqd,bhmkd->bhmqk', qi, k).astype(jnp.float32) * scale
        p = jax.nn.softmax(s, axis=-1)
        w = p[:, :, 0] - lam * p[:, :, 1]
        return jnp.einsum('bhqk,bhkd->bhqd', w.astype(v.dtype), v)

    o = lax.map(one, qb)
    return o.transpose(1, 2, 0, 3, 4).reshape(b, h, n, DA_VDIM)

def diff_head_out(o, g, lam_init):
    o = rms_norm(o, g) * (1.0 - lam_init)
    b, _, n, _ = o.shape
    return o.transpose(0, 2, 1, 3).reshape(b, n, BR_WIDTH)

def hyena_filter(L, w1, b1, w2, b2, w3, freq):
    f32 = jnp.float32
    t = jnp.linspace(0.0, 1.0, L, dtype=f32)[:, None]
    wpos = (2.0 * math.pi / L) * jnp.arange(L, dtype=f32)[:, None]
    bands = jnp.linspace(1e-4, HY_BANDS - 1, HY_BANDS, dtype=f32)[None, :]
    z = jnp.concatenate([t, jnp.cos(bands * wpos), -jnp.sin(bands * wpos)], axis=-1)
    hid = jnp.sin(freq[0].astype(f32) * (z @ w1.astype(f32) + b1.astype(f32)))
    hid = jnp.sin(freq[1].astype(f32) * (hid @ w2.astype(f32) + b2.astype(f32)))
    h = (hid @ w3.astype(f32)).reshape(L, 2, HY_WIDTH)
    deltas = jnp.abs(jnp.linspace(HY_MIN_DECAY, HY_MAX_DECAY, HY_WIDTH, dtype=f32))
    return h * jnp.exp(-t * deltas)[:, None, :]

def long_conv_bidir(u, h, bias):
    L = u.shape[1]
    f32 = jnp.float32
    k = jnp.concatenate([h[:, 0], jnp.zeros((1, HY_WIDTH), f32), h[:0:-1, 1]], axis=0)
    k = k * lax.rsqrt(jnp.sum(k * k, axis=0, keepdims=True))
    kf = jnp.fft.rfft(k, n=2 * L, axis=0)
    uf = jnp.fft.rfft(u.astype(f32), n=2 * L, axis=1)
    y = jnp.fft.irfft(uf * kf[None], n=2 * L, axis=1)[:, :L]
    return (y + u.astype(f32) * bias.astype(f32)).astype(u.dtype)

def short_conv(z, w, b):
    n = z.shape[1]
    pad = HY_SHORT // 2
    zp = jnp.pad(z, ((0, 0), (pad, pad), (0, 0)))
    return sum(zp[:, j:j + n] * w[j] for j in range(HY_SHORT)) + b

def hyena_branch(zb, sw, sb, filt, bias):
    zb = short_conv(zb, sw, sb)
    x0, x1, v = jnp.split(zb, 3, axis=-1)
    return x0 * long_conv_bidir(x1 * v, filt, bias)

def gmlp_branch(zg, ln_g, ln_b, ws, bs):
    u, v = jnp.split(jax.nn.gelu(zg, approximate=False), 2, axis=-1)
    v = layer_norm(v, ln_g, ln_b)
    b, n, _ = v.shape
    vr = v.reshape(b, n // GM_CHUNK, GM_CHUNK, GM_GROUPS, GM_WIDTH // GM_GROUPS)
    vm = jnp.einsum('gpq,bcqgd->bcpgd', ws, vr) + bs.T[:, :, None]
    return u * vm.reshape(b, n, GM_WIDTH)

def merge_branches(z, ys, wb, wo):
    out = None
    for i, (y, g0) in enumerate(zip(ys, (COL_GA, COL_GB, COL_GC))):
        gated = y * jax.nn.silu(z[..., g0:g0 + BR_WIDTH])
        sel = jax.nn.sigmoid(z[..., COL_MG + i * D_MODEL:COL_MG + (i + 1) * D_MODEL])
        term = sel * (gated @ wb[i])
        out = term if out is None else out + term
    return out @ wo

def first_inputs(seed: int = 0) -> dict:
    key = jax.random.key(seed)
    ks = jax.random.split(key, 26)
    f32 = jnp.float32
    nrm = lambda k, shape, s: jax.random.normal(k, shape, f32) * s
    D = D_MODEL
    return {
        "x": nrm(ks[0], (BATCH, SEQ, D), 1.0),
        "c": nrm(ks[1], (BATCH, D), 1.0),
        "ctx": nrm(ks[2], (BATCH, CTX_LEN, D), 1.0),
        "c_ctx": nrm(ks[3], (D,), 1.0),
        "ada_w": nrm(ks[4], (DEPTH, D, 3 * D), 0.5 * D ** -0.5),
        "ada_b": nrm(ks[5], (DEPTH, 3 * D), 0.01),
        "norm_pre": 1.0 + nrm(ks[6], (DEPTH, D), 0.05),
        "norm_post": 1.0 + nrm(ks[7], (DEPTH, D), 0.05),
        "w_in": nrm(ks[8], (DEPTH, D, COL_END), D ** -0.5),
        "da_lambda": nrm(ks[9], (DEPTH, 4, DA_SUB), 0.1),
        "da_subln": 1.0 + nrm(ks[10], (DEPTH, DA_VDIM), 0.05),
        "hy_short_w": nrm(ks[11], (DEPTH, HY_SHORT, 3 * HY_WIDTH), HY_SHORT ** -0.5),
        "hy_short_b": nrm(ks[12], (DEPTH, 3 * HY_WIDTH), 0.02),
        "hy_f_w1": nrm(ks[13], (DEPTH, HY_EMB, HY_HIDDEN), HY_EMB ** -0.5),
        "hy_f_b1": nrm(ks[14], (DEPTH, HY_HIDDEN), 0.1),
        "hy_f_w2": nrm(ks[15], (DEPTH, HY_HIDDEN, HY_HIDDEN), HY_HIDDEN ** -0.5),
        "hy_f_b2": nrm(ks[16], (DEPTH, HY_HIDDEN), 0.1),
        "hy_f_w3": nrm(ks[17], (DEPTH, HY_HIDDEN, 2 * HY_WIDTH), HY_HIDDEN ** -0.5),
        "hy_f_freq": 1.0 + nrm(ks[18], (DEPTH, 2, HY_HIDDEN), 0.1),
        "hy_bias": nrm(ks[19], (DEPTH, HY_WIDTH), 0.5),
        "gm_ln_g": 1.0 + nrm(ks[20], (DEPTH, GM_WIDTH), 0.05),
        "gm_ln_b": nrm(ks[21], (DEPTH, GM_WIDTH), 0.02),
        "gm_ws": nrm(ks[22], (DEPTH, GM_GROUPS, GM_CHUNK, GM_CHUNK), 0.5 * GM_CHUNK ** -0.5),
        "gm_bs": 1.0 + nrm(ks[23], (DEPTH, GM_GROUPS, GM_CHUNK), 0.1),
        "w_branch": nrm(ks[24], (DEPTH, N_BRANCH, BR_WIDTH, D), BR_WIDTH ** -0.5),
        "w_out": nrm(ks[25], (DEPTH, D, D), D ** -0.5),
    }

def first_block(x, c, ctx, c_ctx, ada_w, ada_b, norm_pre, norm_post, w_in, da_lambda, da_subln,
              hy_short_w, hy_short_b, hy_f_w1, hy_f_b1, hy_f_w2, hy_f_b2, hy_f_w3, hy_f_freq, hy_bias,
              gm_ln_g, gm_ln_b, gm_ws, gm_bs, w_branch, w_out):
    n = x.shape[1]
    n_ctx = ctx.shape[1]
    rows = n // GRID_W
    row = jnp.repeat(jnp.arange(rows, dtype=jnp.float32), GRID_W)
    col = jnp.tile(jnp.arange(GRID_W, dtype=jnp.float32), rows)
    cos, sin = axial_rope(row, col)
    xc = ctx
    for l in range(DEPTH):
        last = l == DEPTH - 1
        lam_init = 0.8 - 0.6 * math.exp(-0.3 * l)
        lp = da_lambda[l].astype(jnp.float32)
        lam = jnp.exp(jnp.sum(lp[0] * lp[1])) - jnp.exp(jnp.sum(lp[2] * lp[3])) + lam_init

        sh, sc, gt = modulation(c, ada_w[l], ada_b[l])
        shc, scc, gtc = modulation(c_ctx, ada_w[l], ada_b[l])
        h = rms_norm(x, norm_pre[l]) * (1.0 + sc[:, None]) + sh[:, None]
        hc = rms_norm(xc, norm_pre[l]) * (1.0 + scc) + shc

        z = h @ w_in[l]
        zc = hc @ (w_in[l][:, :COL_Q] if last else w_in[l])
        kc = qk_heads(zc[..., COL_K:COL_V])
        vc = v_heads(zc[..., COL_V:COL_Q])

        q = apply_rope(qk_heads(z[..., COL_Q:COL_GA]), cos, sin)
        k = apply_rope(qk_heads(z[..., COL_K:COL_V]), cos, sin)
        v = v_heads(z[..., COL_V:COL_Q])
        k_all = jnp.concatenate([k, kc], axis=3)
        v_all = jnp.concatenate([v, vc], axis=2)
        y_a = diff_head_out(diff_attend(q, k_all, v_all, lam), da_subln[l], lam_init)
        filt = hyena_filter(n, hy_f_w1[l], hy_f_b1[l], hy_f_w2[l], hy_f_b2[l], hy_f_w3[l], hy_f_freq[l])
        y_b = hyena_branch(z[..., COL_HY:COL_GB], hy_short_w[l], hy_short_b[l], filt, hy_bias[l])
        y_c = gmlp_branch(z[..., COL_GM:COL_GC], gm_ln_g[l], gm_ln_b[l], gm_ws[l], gm_bs[l])
        out = merge_branches(z, (y_a, y_b, y_c), w_branch[l], w_out[l])
        x_new = x + gt[:, None] * rms_norm(out, norm_post[l])

        if not last:
            qc = qk_heads(zc[..., COL_Q:COL_GA])
            yc_a = diff_head_out(diff_attend(qc, kc, vc, lam), da_subln[l], lam_init)
            filt_c = hyena_filter(n_ctx, hy_f_w1[l], hy_f_b1[l], hy_f_w2[l], hy_f_b2[l], hy_f_w3[l], hy_f_freq[l])
            yc_b = hyena_branch(zc[..., COL_HY:COL_GB], hy_short_w[l], hy_short_b[l], filt_c, hy_bias[l])
            yc_c = gmlp_branch(zc[..., COL_GM:COL_GC], gm_ln_g[l], gm_ln_b[l], gm_ws[l], gm_bs[l])
            outc = merge_branches(zc, (yc_a, yc_b, yc_c), w_branch[l], w_out[l])
            xc = xc + gtc * rms_norm(outc, norm_post[l])
        x = x_new
    return x


N_HEADS = 16
HEAD_DIM = 64
ATTN_DIM = N_HEADS * HEAD_DIM
ROT_DIM = HEAD_DIM // 4
ROPE_THETA = 500000.0
D_FF = 2816
FFN_RESIDUAL_WEIGHT = 0.5
N_A_LAYERS = DEPTH // 2
N_B_LAYERS = DEPTH - N_A_LAYERS
DILATION_PAIRS = ((128, 1), (512, 4), (2048, 16))
MOBA_BLOCK = 256
MOBA_TOPK = 3
MOBA_Q_CHUNK = 32
RMS_EPS = 1e-6


def rmsnorm(x, g):
    xf = x.astype(jnp.float32)
    y = xf * lax.rsqrt(jnp.mean(xf * xf, axis=-1, keepdims=True) + RMS_EPS)
    return (y * g.astype(jnp.float32)).astype(x.dtype)

def swiglu(h, w_gate, w_up, w_down):
    return (jax.nn.silu(h @ w_gate) * (h @ w_up)) @ w_down

def partial_rotary(t, pos):
    half = ROT_DIM // 2
    inv_freq = ROPE_THETA ** (-jnp.arange(half, dtype=jnp.float32) / half)
    ang = pos.astype(jnp.float32)[:, None] * inv_freq[None, :]
    cos, sin = jnp.cos(ang), jnp.sin(ang)
    tf = t.astype(jnp.float32)
    x1, x2 = tf[..., :half], tf[..., half:ROT_DIM]
    out = jnp.concatenate([x1 * cos - x2 * sin, x1 * sin + x2 * cos, tf[..., ROT_DIM:]], axis=-1)
    return out.astype(t.dtype)

def dilated_branch(q, k, v, window, dil):
    B, H, S, Dh = q.shape
    blk = window // dil
    span = blk * dil
    s_pad = -(-S // span) * span
    L = s_pad // dil
    nb = L // blk

    def to_sub(t):
        t = jnp.pad(t, ((0, 0), (0, 0), (0, s_pad - S), (0, 0)))
        t = t.reshape(B, H, L, dil, Dh).transpose(0, 1, 3, 2, 4)
        return t.reshape(B, H, dil, nb, blk, Dh)

    qs, ks, vs = to_sub(q), to_sub(k), to_sub(v)

    def with_prev(t):
        prev = jnp.pad(t, ((0, 0), (0, 0), (0, 0), (1, 0), (0, 0), (0, 0)))[:, :, :, :-1]
        return jnp.concatenate([prev, t], axis=4)

    kk, vv = with_prev(ks), with_prev(vs)
    s = jnp.einsum('bhrnqd,bhrnkd->bhrnqk', qs, kk).astype(jnp.float32) * (HEAD_DIM ** -0.5)
    qi = jnp.arange(blk)[:, None]
    kj = jnp.arange(2 * blk)[None, :]
    diff = blk + qi - kj
    band = (diff >= 0) & (diff <= blk)
    has_prev = (jnp.arange(nb)[:, None, None] > 0) | (kj[None] >= blk)
    mask = band[None] & has_prev
    s = jnp.where(mask, s, -jnp.inf)
    m = jnp.max(s, axis=-1, keepdims=True)
    p = jnp.exp(s - m)
    l = jnp.sum(p, axis=-1, keepdims=True)
    o = jnp.einsum('bhrnqk,bhrnkd->bhrnqd', (p / l).astype(v.dtype), vv)
    lse = m + jnp.log(l)

    def from_sub(t):
        X = t.shape[-1]
        t = t.reshape(B, H, dil, L, X).transpose(0, 1, 3, 2, 4).reshape(B, H, s_pad, X)
        return t[:, :, :S]

    return from_sub(o), from_sub(lse)[..., 0]

def mixer_a(h, w_qkv, w_o, pos):
    B, S, _ = h.shape
    qkv = (h @ w_qkv).reshape(B, S, 3, N_HEADS, HEAD_DIM).transpose(2, 0, 3, 1, 4)
    q, k, v = partial_rotary(qkv[0], pos), partial_rotary(qkv[1], pos), qkv[2]
    outs, lses = [], []
    for window, dil in DILATION_PAIRS:
        o_i, lse_i = dilated_branch(q, k, v, window, dil)
        outs.append(o_i)
        lses.append(lse_i)
    wts = jax.nn.softmax(jnp.stack(lses, axis=0), axis=0)
    o = jnp.sum(wts[..., None] * jnp.stack(outs, axis=0).astype(jnp.float32), axis=0).astype(h.dtype)
    return o.transpose(0, 2, 1, 3).reshape(B, S, ATTN_DIM) @ w_o

def shared_kv(h_stream, kv_norm, kv_w, pos):
    B, S, _ = h_stream.shape
    hn = rmsnorm(h_stream, kv_norm)
    kv = (hn @ kv_w).reshape(B, S, 2, N_HEADS, HEAD_DIM).transpose(2, 0, 3, 1, 4)
    k, v = partial_rotary(kv[0], pos), kv[1]
    s_pad = -(-S // MOBA_BLOCK) * MOBA_BLOCK
    pad = ((0, 0), (0, 0), (0, s_pad - S), (0, 0))
    k_pad, v_pad = jnp.pad(k, pad), jnp.pad(v, pad)
    nb = s_pad // MOBA_BLOCK
    k_mean = jnp.mean(k_pad.reshape(B, N_HEADS, nb, MOBA_BLOCK, HEAD_DIM).astype(jnp.float32), axis=3)
    return k_pad, v_pad, k_mean.astype(k.dtype)

def mixer_b(h, w_q, w_o, k_pad, v_pad, k_mean, pos):
    B, S, _ = h.shape
    q = (h @ w_q).reshape(B, S, N_HEADS, HEAD_DIM).transpose(0, 2, 1, 3)
    q = partial_rotary(q, pos)
    nb = k_mean.shape[2]
    ksel = min(MOBA_TOPK, nb)
    k_blocks = k_pad.reshape(B, N_HEADS, nb, MOBA_BLOCK, HEAD_DIM)
    v_blocks = v_pad.reshape(B, N_HEADS, nb, MOBA_BLOCK, HEAD_DIM)
    n_chunks = S // MOBA_Q_CHUNK
    q_chunks = q.reshape(B, N_HEADS, n_chunks, MOBA_Q_CHUNK, HEAD_DIM).transpose(2, 0, 1, 3, 4)
    gather = jax.vmap(jax.vmap(lambda blocks, idx: blocks[idx]))
    scale = HEAD_DIM ** -0.5

    def chunk_attend(args):
        c, qc = args
        t = c * MOBA_Q_CHUNK + jnp.arange(MOBA_Q_CHUNK)
        own = (c * MOBA_Q_CHUNK) // MOBA_BLOCK
        gate = jnp.einsum('bhqd,bhnd->bhqn', qc, k_mean).astype(jnp.float32)
        gate = jnp.where(jnp.arange(nb) < own, gate, -jnp.inf)
        _, sel = lax.top_k(gate, ksel)
        valid = sel < own
        k_s = gather(k_blocks, sel)
        v_s = gather(v_blocks, sel)
        s_sel = jnp.einsum('bhqd,bhqnkd->bhqnk', qc, k_s).astype(jnp.float32) * scale
        s_sel = jnp.where(valid[..., None], s_sel, -jnp.inf).reshape(B, N_HEADS, MOBA_Q_CHUNK, ksel * MOBA_BLOCK)
        k_o = lax.dynamic_slice_in_dim(k_pad, own * MOBA_BLOCK, MOBA_BLOCK, axis=2)
        v_o = lax.dynamic_slice_in_dim(v_pad, own * MOBA_BLOCK, MOBA_BLOCK, axis=2)
        s_own = jnp.einsum('bhqd,bhkd->bhqk', qc, k_o).astype(jnp.float32) * scale
        causal = (own * MOBA_BLOCK + jnp.arange(MOBA_BLOCK))[None, :] <= t[:, None]
        s_own = jnp.where(causal, s_own, -jnp.inf)
        p = jax.nn.softmax(jnp.concatenate([s_sel, s_own], axis=-1), axis=-1).astype(qc.dtype)
        p_sel = p[..., :ksel * MOBA_BLOCK].reshape(B, N_HEADS, MOBA_Q_CHUNK, ksel, MOBA_BLOCK)
        p_own = p[..., ksel * MOBA_BLOCK:]
        return (jnp.einsum('bhqnk,bhqnkd->bhqd', p_sel, v_s)
                + jnp.einsum('bhqk,bhkd->bhqd', p_own, v_o))

    out = lax.map(chunk_attend, (jnp.arange(n_chunks), q_chunks))
    out = out.transpose(1, 0, 3, 2, 4).reshape(B, S, ATTN_DIM)
    return out @ w_o

def second_inputs(seed: int = 0) -> dict:
    key = jax.random.key(seed)
    ks = jax.random.split(key, 18)
    f32 = jnp.float32

    def w(k, shape, fan_in):
        return jax.random.normal(k, shape, f32) * (fan_in ** -0.5)

    def gain(k, shape):
        return 1.0 + 0.02 * jax.random.normal(k, shape, f32)

    return {
        'x': jax.random.normal(ks[0], (BATCH, SEQ, D_MODEL), f32),
        'ffn1_norm': gain(ks[1], (DEPTH, D_MODEL)),
        'ffn1_w_gate': w(ks[2], (DEPTH, D_MODEL, D_FF), D_MODEL),
        'ffn1_w_up': w(ks[3], (DEPTH, D_MODEL, D_FF), D_MODEL),
        'ffn1_w_down': w(ks[4], (DEPTH, D_FF, D_MODEL), D_FF),
        'mix_norm': gain(ks[5], (DEPTH, D_MODEL)),
        'ffn2_norm': gain(ks[6], (DEPTH, D_MODEL)),
        'ffn2_w_gate': w(ks[7], (DEPTH, D_MODEL, D_FF), D_MODEL),
        'ffn2_w_up': w(ks[8], (DEPTH, D_MODEL, D_FF), D_MODEL),
        'ffn2_w_down': w(ks[9], (DEPTH, D_FF, D_MODEL), D_FF),
        'a_w_qkv': w(ks[10], (N_A_LAYERS, D_MODEL, 3 * ATTN_DIM), D_MODEL),
        'a_w_o': w(ks[11], (N_A_LAYERS, ATTN_DIM, D_MODEL), ATTN_DIM),
        'kv_norm': gain(ks[12], (D_MODEL,)),
        'kv_w': w(ks[13], (D_MODEL, 2 * ATTN_DIM), D_MODEL),
        'b_w_q': w(ks[14], (N_B_LAYERS, D_MODEL, ATTN_DIM), D_MODEL),
        'b_w_o': w(ks[15], (N_B_LAYERS, ATTN_DIM, D_MODEL), ATTN_DIM),
        'final_norm': gain(ks[16], (D_MODEL,)),
    }

def second_block(x, ffn1_norm, ffn1_w_gate, ffn1_w_up, ffn1_w_down, mix_norm,
              ffn2_norm, ffn2_w_gate, ffn2_w_up, ffn2_w_down, a_w_qkv, a_w_o,
              kv_norm, kv_w, b_w_q, b_w_o, final_norm):
    pos = jnp.arange(x.shape[1], dtype=jnp.int32)
    h = x
    shared = None
    for layer in range(DEPTH):
        h = h + FFN_RESIDUAL_WEIGHT * swiglu(rmsnorm(h, ffn1_norm[layer]),
                                             ffn1_w_gate[layer], ffn1_w_up[layer], ffn1_w_down[layer])
        hn = rmsnorm(h, mix_norm[layer])
        if layer < N_A_LAYERS:
            h = h + mixer_a(hn, a_w_qkv[layer], a_w_o[layer], pos)
        else:
            j = layer - N_A_LAYERS
            h = h + mixer_b(hn, b_w_q[j], b_w_o[j], shared[0], shared[1], shared[2], pos)
        h = h + FFN_RESIDUAL_WEIGHT * swiglu(rmsnorm(h, ffn2_norm[layer]),
                                             ffn2_w_gate[layer], ffn2_w_up[layer], ffn2_w_down[layer])
        if layer == N_A_LAYERS - 1:
            shared = shared_kv(h, kv_norm, kv_w, pos)
    return rmsnorm(h, final_norm)


def setup_inputs(seed=0):
    out = dict(first_inputs(seed))
    for name, value in second_inputs(seed + 1).items():
        if name != "x":
            out[name + "_2"] = value
    return out


def reference(
    x, c, ctx, c_ctx, ada_w, ada_b, norm_pre, norm_post, w_in, da_lambda, da_subln, hy_short_w,
    hy_short_b, hy_f_w1, hy_f_b1, hy_f_w2, hy_f_b2, hy_f_w3, hy_f_freq, hy_bias, gm_ln_g,
    gm_ln_b, gm_ws, gm_bs, w_branch, w_out, ffn1_norm_2, ffn1_w_gate_2, ffn1_w_up_2,
    ffn1_w_down_2, mix_norm_2, ffn2_norm_2, ffn2_w_gate_2, ffn2_w_up_2, ffn2_w_down_2,
    a_w_qkv_2, a_w_o_2, kv_norm_2, kv_w_2, b_w_q_2, b_w_o_2, final_norm_2,
):
    x = first_block(
        x, c, ctx, c_ctx, ada_w, ada_b, norm_pre, norm_post, w_in, da_lambda, da_subln,
        hy_short_w, hy_short_b, hy_f_w1, hy_f_b1, hy_f_w2, hy_f_b2, hy_f_w3, hy_f_freq, hy_bias,
        gm_ln_g, gm_ln_b, gm_ws, gm_bs, w_branch, w_out,
    )
    return second_block(
        x, ffn1_norm_2, ffn1_w_gate_2, ffn1_w_up_2, ffn1_w_down_2, mix_norm_2, ffn2_norm_2,
        ffn2_w_gate_2, ffn2_w_up_2, ffn2_w_down_2, a_w_qkv_2, a_w_o_2, kv_norm_2, kv_w_2,
        b_w_q_2, b_w_o_2, final_norm_2,
    )


_drawn_inputs = setup_inputs


def setup_inputs(seed=0):
    import zlib

    import numpy as np

    out = dict(_drawn_inputs(seed))
    spreads = {}
    factors = {'da_lambda': 5.81,
     'da_subln': 4.72,
     'hy_short_b': 3.471,
     'gm_ln_g': 8.0,
     'gm_ln_b': 8.0,
     'gm_bs': 2.708,
     'ffn1_norm_2': 5.003,
     'mix_norm_2': 7.568,
     'ffn2_norm_2': 5.536,
     'kv_norm_2': 8.0,
     'final_norm_2': 2.722}
    for name, (base, spread) in spreads.items():
        noise = np.random.default_rng([zlib.crc32(name.encode()), seed]).standard_normal(out[name].shape)
        drawn = base * np.exp(spread * noise) if base else spread * noise
        out[name] = __import__('jax').numpy.asarray(drawn.astype(out[name].dtype))
    for name, factor in factors.items():
        out[name] = (out[name] * factor).astype(out[name].dtype)
    return out
```

```python
import math
from contextlib import ExitStack

import concourse.bass as bass
import numpy as np
from concourse import mybir

F32 = mybir.dt.float32
F32R = mybir.dt.float32r
ALU = mybir.AluOpType
ACT = mybir.ActivationFunctionType
AX_X = mybir.AxisListType.X

P = 128
T = 256
TT = T // P
D = 1024
KD = D // P
BR = 512
KB = BR // P
DEPTH = 2
FF = 2816
FPAIRS = FF // (2 * P)
HEADS_A, SUB = 4, 64
HEADS_B, HD = 16, 64
SLOT = 1024
RING = 3
SEG = 3 * P
EPS = 1e-6
TWO_PI_HI = 6.28125
TWO_PI_LO = 2 * math.pi - 6.28125
ROUND = 1.5 * 2 ** 23
PI_SAFE = 3.1415925

PASS = [("k", 4), ("q", 4), ("v", 4), ("hy", 12), ("gu", 4), ("gv", 4), ("ga", 4), ("gb", 4),
        ("gc", 4), ("merge", 36), ("wo", 8)]
PASS_SLOTS = sum(n for _, n in PASS)
ADA_SLOTS = 3 * D // P
FFN_SLOTS = 3 * FF // P
SCORES, TURN, HEADS_OUT, MISC = 2, 4, 5, 7

COLUMNS = [("cond", 16)]
for _l in range(DEPTH):
    COLUMNS += [(f"norm_pre{_l}", KD), (f"norm_post{_l}", KD), (f"ada_b{_l}", 24), (f"subln{_l}", 1),
                (f"short_w{_l}", 36), (f"short_b{_l}", 12), (f"conv_bias{_l}", KB),
                (f"filter_b1{_l}", 1), (f"filter_b2{_l}", 1), (f"freq0{_l}", 1), (f"freq1{_l}", 1),
                (f"ffn1{_l}", KD), (f"mix{_l}", KD), (f"ffn2{_l}", KD)]
COLUMNS += [("kv_norm", KD), ("final_norm", KD)]
CONSTS = [("ident", P), ("perm_a", P), ("perm_b", P), ("cos_a", T), ("sin_a", T), ("cos_b", T),
          ("sin_b", T), ("bias_dilated", SEG), ("bias_causal", SEG), ("dft_cos", TT * T),
          ("dft_sin_u", TT * T), ("dft_sin_k", TT * T), ("dft_nyq", TT * P), ("idft", 4 * T),
          ("decay", TT * BR), ("filter_z", T)]
LAYER = [("ln_g", BR), ("ln_b", BR), ("mix_bias", KB * P), ("mix_w", 8 * P)]
FILTER = [("w1", 64), ("w2", 64), ("w3", 2 * BR)]


def places(parts):
    out, at = {}, 0
    for name, n in parts:
        out[name] = (at, at + n)
        at += n
    return out, at


def build(nc, weights, x_in, ctx_in, cols_in, consts_in, layer_in, filter_in, lam_in, out):
    col_at, ncols = places(COLUMNS)
    const_at, nconsts = places(CONSTS)
    layer_at, nlayer = places(LAYER)
    filter_at, nfilter = places(FILTER)

    start = {}
    stretches = []
    at = 0

    def stretch(name, dram, n):
        nonlocal at
        start[name] = at
        stretches.append((at, dram, n))
        at += n

    dram = 0
    dram_pass = {}
    for l in range(DEPTH):
        stretch(f"ada{l}", dram, ADA_SLOTS)
        dram += ADA_SLOTS
        dram_pass[l] = dram
        if l == 0:
            stretch("pass0", dram, PASS_SLOTS)
            stretch("pass1", dram, PASS_SLOTS)
        else:
            stretch("ctx_k", dram, 4)
            stretch("ctx_v", dram + 8, 4)
            stretch("pass2", dram, PASS_SLOTS)
        dram += PASS_SLOTS
    tail = [("ffn0", FFN_SLOTS), ("qkv0", 24), ("wo0", 8), ("ffn1", FFN_SLOTS), ("kv", 16),
            ("ffn2", FFN_SLOTS), ("q1", 8), ("wo1", 8), ("ffn3", FFN_SLOTS)]
    for name, n in tail:
        stretch(name, dram, n)
        dram += n
    TOTAL = at
    part = {}
    a = 0
    for name, n in PASS:
        part[name] = a
        a += n

    ctx = ExitStack()
    with ctx:
        def sb(name, shape, dt=F32):
            return ctx.enter_context(nc.sbuf_tensor(name, shape, dt))

        def sem(name):
            return ctx.enter_context(nc.semaphore(name))

        PS = ctx.enter_context(nc.psum_tensor("PS", [P, 8, 512], F32))
        raw = sb("raw", [P, RING, SLOT])
        w_hi = sb("w_hi", [P, RING, SLOT], F32R)
        w_lo = sb("w_lo", [P, RING, SLOT], F32R)
        x = sb("x", [P, KD, T])
        cx = sb("cx", [P, KD, T])
        h_hi = sb("h_hi", [P, KD, T], F32R)
        h_lo = sb("h_lo", [P, KD, T], F32R)
        g_hi = sb("g_hi", [P, 12, T], F32R)
        g_lo = sb("g_lo", [P, 12, T], F32R)
        q = sb("q", [P, KD, T])
        k = sb("k", [P, KD, T])
        v = sb("v", [P, 4, BR])
        v2 = v[:, :, :].rearrange("p (t a) c -> p t (a c)", a=2)
        cols = sb("cols", [P, ncols])
        consts = sb("consts", [P, nconsts])
        layer = sb("layer", [P, nlayer])
        spec_re = sb("spec_re", [P, 2, BR])
        spec_im = sb("spec_im", [P, 2, BR])
        spec_ny = sb("spec_ny", [P, BR])
        ones = sb("ones", [P, P])
        zeros = sb("zeros", [P, 512], mybir.dt.bfloat16)
        eps = sb("eps", [P, 1])
        c_hi = sb("c_hi", [P, KD, 2], F32R)
        c_lo = sb("c_lo", [P, KD, 2], F32R)
        c_act = sb("c_act", [P, 16])
        mod = sb("mod", [P, 24, 2])
        gain = sb("gain", [P, KD, 2])
        gate = sb("gate", [P, KD, 2])
        stat = sb("stat", [P, 96])
        arena = sb("arena", [P, 10752])

        def col(name, j=0, n=1):
            a = col_at[name][0] + j
            return cols[:, a:a + n]

        def const(name):
            a, b = const_at[name]
            return consts[:, a:b]

        def row(name):
            a, b = layer_at[name]
            return layer[:, a:b]

        def scratch(a, n, **kw):
            return arena[:, a:a + n]

        sq = scratch(0, 2048).rearrange("p (k t) -> p k t", k=KD)
        normed = scratch(2048, 2048).rearrange("p (k t) -> p k t", k=KD)
        rt = scratch(4096, 256)
        rstd = scratch(4352, 256)
        branch_out = scratch(4608, 2048).rearrange("p (k t) -> p k t", k=KD)
        merged = scratch(0, 2048).rearrange("p (k t) -> p k t", k=KD)
        sel = scratch(2048, 1536).rearrange("p (i n) -> p i n", i=3)
        term = scratch(3584, 512)
        rope_raw = scratch(0, 1024).rearrange("p (b n) -> p b n", b=2)
        rope_a = scratch(1024, 512)
        rope_b = scratch(1536, 512)
        probs = scratch(2048, 1024).rearrange("p (m n) -> p m n", m=2)
        mixw = scratch(3072, 512)
        mixw_t = scratch(3584, 2048).rearrange("p (b k t) -> p b k t", b=2, k=4)
        head_y = scratch(5632, 1024).rearrange("p (h q d) -> p h q d", h=4, q=2)
        y = scratch(6656, 1024).rearrange("p (k t) -> p k t", k=KB)
        squared = scratch(6656, 1024).rearrange("p (n d) -> p n d", n=8)
        hy = scratch(7680, 3072).rearrange("p (k t) -> p k t", k=12)
        u = hy[:, 4:8, :]
        gu = scratch(0, 1024).rearrange("p (k t) -> p k t", k=KB)
        gv = scratch(1024, 1024).rearrange("p (t c) -> p t c", t=TT)
        gvc = scratch(2048, 1024).rearrange("p (t c) -> p t c", t=TT)
        lnv = scratch(3584, 1024).rearrange("p (t c) -> p t c", t=TT)
        gate_act = scratch(4608, 1024).rearrange("p (b n) -> p b n", b=2)
        gated = scratch(5632, 512)
        u_tok = v[:, 0:2, :]
        prod = k[:, 0:4, :].rearrange("p (a k) t -> p a (k t)", a=2)
        yspec = q[:, :, :].rearrange("p (a k) t -> p a (k t)", a=4)
        hw = scratch(0, 2048).rearrange("p (d t c) -> p d t c", d=2, t=TT)
        h_sum = scratch(2048, 1024).rearrange("p (t c) -> p t c", t=TT)
        h_dif = scratch(3072, 1024).rearrange("p (t c) -> p t c", t=TT)
        h_sq = scratch(4096, 2048).rearrange("p (d t c) -> p d t c", d=2, t=TT)
        fil = scratch(6144, nfilter)
        arg = scratch(7296, 256)
        turns = scratch(7552, 256)
        hid1 = scratch(7808, 256)
        hid2 = scratch(8064, 256)
        lam_rows = scratch(8320, 256)
        silu = scratch(4608, 1024).rearrange("p (b n) -> p b n", b=2)
        act_f = scratch(5632, 512)
        act_hi = g_hi[:, 0:4, :].rearrange("p (b f) t -> p b f t", b=2)
        act_lo = g_lo[:, 0:4, :].rearrange("p (b f) t -> p b f t", b=2)
        biased = scratch(2048, 2 * SEG).rearrange("p (h n) -> p h n", h=2)
        probs2 = scratch(2816, 2 * SEG).rearrange("p (h n) -> p h n", h=2)
        probs2_t = scratch(3584, 4 * SEG).rearrange("p (b h n) -> p b h n", b=2, h=2)

        def filt(name, rows):
            a, b = filter_at[name]
            return fil[0:rows, a:b]

        neg_max = stat[:, 0:8]
        mx = stat[:, 8:16]
        den = stat[:, 16:24]
        rden = stat[:, 24:32]
        head_ss = stat[:, 32:40]
        head_rt = stat[:, 40:48]
        head_rs = stat[:, 48:56]
        conv_rt = stat[:, 56:60]
        conv_rs = stat[:, 60:64]
        ln_sum = stat[:, 64:66]
        ln_ss = stat[:, 66:68]
        ln_rt = stat[:, 68:70]
        ln_rs = stat[:, 70:72]
        dots = stat[:, 72:74]
        dot_exp = stat[:, 74:76]
        lam = stat[:, 76:77]
        neg_lam = stat[:, 77:78]
        subln_g = stat[:, 78:79]
        wden = stat[:, 80:82]

        raw_loaded = [sem(f"raw_loaded{r}") for r in range(RING)]
        w_hi_ready = sem("w_hi_ready")
        w_lo_ready = sem("w_lo_ready")
        w_used = sem("w_used")
        consts_loaded = sem("consts_loaded")
        x_loaded = sem("x_loaded")
        layer_loaded = sem("layer_loaded")
        ones_ready = sem("ones_ready")
        dve_chain = sem("dve_chain")
        act_chain = sem("act_chain")
        cond_act = sem("cond_act")
        cond_hi = sem("cond_hi")
        cond_ready = sem("cond_ready")
        mod_ready = sem("mod_ready")
        fil_mm = sem("fil_mm")
        fil_arg = sem("fil_arg")
        fil_sin = sem("fil_sin")
        fil_h = sem("fil_h")
        fil_sq = sem("fil_sq")
        fil_rt = sem("fil_rt")
        lam_dots = sem("lam_dots")
        lam_exp = sem("lam_exp")
        src_ready = sem("src_ready")
        sq_ready = sem("sq_ready")
        ms_ready = sem("ms_ready")
        rt_ready = sem("rt_ready")
        norm_v = sem("norm_v")
        norm_hi = sem("norm_hi")
        norm_lo = sem("norm_lo")
        dve_evac = sem("dve_evac")
        act_evac = sem("act_evac")
        rope_in = sem("rope_in")
        rope_rot = sem("rope_rot")
        rope_out = sem("rope_out")
        sc_done = sem("sc_done")
        nm_ready = sem("nm_ready")
        p_ready = sem("p_ready")
        mixw_ready = sem("mixw_ready")
        turned = sem("turned")
        mixw_t_ready = sem("mixw_t_ready")
        pv_done = sem("pv_done")
        head_sq = sem("head_sq")
        head_rt_ready = sem("head_rt_ready")
        head_y_ready = sem("head_y_ready")
        head_t = sem("head_t")
        u_ready = sem("u_ready")
        u_t = sem("u_t")
        u_tok_ready = sem("u_tok_ready")
        dft_done = sem("dft_done")
        yspec_ready = sem("yspec_ready")
        conv_done = sem("conv_done")
        ln_centered = sem("ln_centered")
        ln_rt_ready = sem("ln_rt_ready")
        lnv_ready = sem("lnv_ready")
        mixed = sem("mixed")
        gated_ready = sem("gated_ready")
        merge_free = sem("merge_free")
        merge_added = sem("merge_added")
        sel_ready = sem("sel_ready")
        m_hi = sem("m_hi")
        m_lo = sem("m_lo")
        gu_free = sem("gu_free")
        silu_ready = sem("silu_ready")
        act_raw = sem("act_raw")
        act_hi_ready = sem("act_hi_ready")
        act_ready = sem("act_ready")
        sc2_done = sem("sc2_done")
        nm2_ready = sem("nm2_ready")
        p2_ready = sem("p2_ready")
        p2n_ready = sem("p2n_ready")
        turned2 = sem("turned2")
        p2t_ready = sem("p2t_ready")
        pv2_done = sem("pv2_done")
        o2_hi = sem("o2_hi")
        o2_ready = sem("o2_ready")
        qkv_evac = sem("qkv_evac")
        y_ready = sem("y_ready")
        out_ready = sem("out_ready")
        out_stored = sem("out_stored")

        block = ctx.enter_context(nc.Block())

        def f32(ap):
            return ap.bitcast(F32)

        LAYER_OF = [0, 0, 1]
        ON_CTX = [True, False, False]

        def key_tiles(p):
            return [2, 3] if ON_CTX[p] else [0, 1, 2, 3]

        def sources(p):
            return cx if ON_CTX[p] else x

        def dve_pairs(p, j):
            return 12 * p + j + 1 + (4 if p == 2 else 0)

        def act_pairs(p, j):
            return 10 * p + j + 1

        ROPE_BASE = [0, 0, 4, 8]

        @block.sync
        def _(sp):
            def load(n, d, i=None):
                r = n % RING
                src = weights[d] if i is None else weights[bass.ds(i * RING + d, 1)].rearrange("o p n -> (o p) n")
                if i is not None:
                    sp.wait_ge(w_lo_ready, i * RING + (n - RING + 1))
                elif n >= RING:
                    sp.wait_ge(w_lo_ready, n - RING + 1)
                sp.dma_start(raw[:, r, :], src).then_inc(raw_loaded[r], 16)

            for n0, d0, count in stretches:
                first = RING if n0 == 0 else 0
                for j in range(first):
                    load(n0 + j, d0 + j)
                turns_ = (count - first) // RING
                if turns_ > 1:
                    with sp.Fori(0, turns_) as i:
                        for j in range(RING):
                            load(n0 + first + j, d0 + first + j, i)
                    first += turns_ * RING
                for j in range(first, count):
                    load(n0 + j, d0 + j)

        @block.gpsimd
        def _(pool):
            def load_layer(l):
                pool.dma_start(layer[:, :], layer_in[l]).then_inc(layer_loaded, 16)
                pool.dma_start(fil[0:64, :], filter_in[l]).then_inc(layer_loaded, 16)
                pool.dma_start(lam_rows, lam_in[l]).then_inc(layer_loaded, 16)

            pool.dma_start(cols[:, :], cols_in).then_inc(consts_loaded, 16)
            pool.dma_start(consts[:, :], consts_in).then_inc(consts_loaded, 16)
            load_layer(0)
            pool.dma_start(cx[:, :, :], ctx_in).then_inc(x_loaded, 16)
            pool.dma_start(x[:, :, :], x_in).then_inc(x_loaded, 16)
            pool.wait_ge(src_ready, 16)
            load_layer(1)
            pool.wait_ge(out_ready, KD)
            pool.dma_start(out, normed).then_inc(out_stored, 16)
            pool.wait_ge(out_stored, 16)

        @block.tensor
        def _(pe):
            def mm3(dst, hi, lo, m_hi_, m_lo_, first, last, **kw):
                pe.matmul(dst, hi, m_hi_, start=first, stop=False, **kw)
                pe.matmul(dst, hi, m_lo_, start=False, stop=False, **kw)
                return pe.matmul(dst, lo, m_hi_, start=False, stop=last, **kw)

            def slot_ready(c, i, per):
                pe.wait_ge(w_lo_ready, c + 1 if i is None else i * per + (c + 1))

            def project(c, dst, i=None, per=0, tiles=None, hi=h_hi, lo=h_lo, nk=KD):
                slot_ready(c, i, per)
                r = c % RING
                for kk in range(nk):
                    if tiles is not None:
                        pe.wait_ge(*tiles(kk))
                    w = slice(kk * P, kk * P + P)
                    mm = mm3(dst, w_hi[:, r, w], w_lo[:, r, w], hi[:, kk, :], lo[:, kk, :],
                             kk == 0, kk == nk - 1)
                mm.then_inc(w_used, 1)

            def pair(c, bank, i=None, per=0, tiles=None, hi=h_hi, lo=h_lo):
                project(c, PS[:, bank, 0:T], i, per, tiles, hi, lo)
                project(c + 1, PS[:, bank, T:2 * T], i, per, None, hi, lo)

            def token_pair(c, bank):
                slot_ready(c, None, 0)
                slot_ready(c + 1, None, 0)
                for t in range(TT):
                    dst = PS[:, bank, t * T:(t + 1) * T]
                    tok = slice(t * P, t * P + P)
                    for kk in range(KD):
                        r, j = (c + kk // 4) % RING, kk % 4
                        w = slice(j * T, (j + 1) * T)
                        mm = mm3(dst, h_hi[:, kk, tok], h_lo[:, kk, tok], w_hi[:, r, w], w_lo[:, r, w],
                                 kk == 0, kk == KD - 1)
                mm.then_inc(w_used, 2)

            def norm(nid):
                for c in range(4):
                    pe.wait_ge(sq_ready, 4 * nid + c + 1)
                    for kk in (2 * c, 2 * c + 1):
                        mm = pe.matmul(PS[:, 0, 0:T], ones[:, :], sq[:, kk, :], start=(kk == 0),
                                       stop=(kk == KD - 1))
                mm.then_inc(ms_ready, 1)

            def normed_tiles(nid_lo):
                return lambda kk: (norm_lo, KD * nid_lo + kk + 1)

            def modulation(l):
                c0 = start[f"ada{l}"]
                if l == 0:
                    pe.wait_ge(cond_ready, 1)
                with pe.Fori(0, ADA_SLOTS // RING) as i:
                    for j in range(RING):
                        slot_ready(c0 + j, i, RING)
                        for kk in range(KD):
                            w = slice(kk * P, kk * P + P)
                            r = (c0 + j) % RING
                            mm = mm3(PS[:, 1, bass.ds(i * (2 * RING) + 2 * j, 2)], w_hi[:, r, w], w_lo[:, r, w],
                                     c_hi[:, kk, :], c_lo[:, kk, :], kk == 0, kk == KD - 1)
                        mm.then_inc(w_used, 1)

            def filter_(l):
                pe.wait_ge(consts_loaded, 32)
                pe.wait_ge(layer_loaded, 48 * (l + 1))
                pe.matmul(PS[0:64, 2, 0:T], filt("w1", 33), const("filter_z")[0:33, :], start=True,
                          stop=True).then_inc(fil_mm, 1)
                pe.wait_ge(fil_sin, 2 * l + 1)
                pe.matmul(PS[0:64, 3, 0:T], filt("w2", 64), hid1[0:64, :], start=True,
                          stop=True).then_inc(fil_mm, 1)
                pe.wait_ge(fil_sin, 2 * l + 2)
                for d in range(2):
                    for t in range(TT):
                        mm = pe.matmul(PS[:, 4 + 2 * d + t, :], hid2[0:64, t * P:(t + 1) * P],
                                       filt("w3", 64)[:, d * BR:(d + 1) * BR], start=True, stop=True)
                mm.then_inc(fil_mm, 1)
                pe.wait_ge(fil_sq, l + 1)
                for c in range(KB):
                    for n, (d, t) in enumerate([(0, 0), (0, 1), (1, 0), (1, 1)]):
                        mm = pe.matmul(PS[:, 2, 2 * c:2 * c + 1], h_sq[:, d, t, c * P:(c + 1) * P],
                                       ones[:, 0:1], start=(n == 0), stop=(n == 3))
                mm.then_inc(fil_mm, 1)
                pe.wait_ge(fil_h, l + 1)
                dft_c = const("dft_cos").rearrange("p (t f) -> p t f", t=TT)
                dft_s = const("dft_sin_k").rearrange("p (t f) -> p t f", t=TT)
                dft_n = const("dft_nyq").rearrange("p (t f) -> p t f", t=TT)
                for f in range(2):
                    for t in range(TT):
                        pe.matmul(PS[:, 4 + f, :], dft_c[:, t, f * P:(f + 1) * P], h_sum[:, t, :],
                                  start=(t == 0), stop=(t == 1))
                for f in range(2):
                    for t in range(TT):
                        pe.matmul(PS[:, 6 + f, :], dft_s[:, t, f * P:(f + 1) * P], h_dif[:, t, :],
                                  start=(t == 0), stop=(t == 1))
                for t in range(TT):
                    mm = pe.matmul(PS[:, 3, :], dft_n[:, t, :], h_sum[:, t, :], start=(t == 0), stop=(t == 1))
                mm.then_inc(fil_mm, 1)

            def rotate(n, perm):
                pe.wait_ge(rope_in, n + 1)
                if n >= 1:
                    pe.wait_ge(rope_out, n)
                pe.matmul(PS[:, MISC, :], const(perm), rope_raw[:, n % 2, :], start=True,
                          stop=True).then_inc(rope_rot, 1)

            def scores(p, n):
                h, qt = n // 2, n % 2
                if n >= 1:
                    pe.wait_ge(p_ready, 8 * p + n)
                kt = key_tiles(p)
                for m in range(2):
                    s = slice(SUB * m, SUB * m + SUB)
                    for g in range(len(kt) // 2):
                        base = 0 if kt[2 * g] == 0 else 4
                        mm = pe.matmul(PS[:, SCORES + m, g * T:(g + 1) * T], q[s, h, qt * P:(qt + 1) * P],
                                       k[s, base + h, :], start=True, stop=True)
                mm.then_inc(sc_done, 1)

            def turn(p, n):
                pe.wait_ge(mixw_ready, 8 * p + n + 1)
                if n >= 1:
                    pe.wait_ge(mixw_t_ready, 8 * p + n)
                for j in range(len(key_tiles(p))):
                    mm = pe.transpose(PS[:, TURN, j * P:(j + 1) * P], mixw[:, j * P:(j + 1) * P], const("ident"))
                mm.then_inc(turned, 1)

            def values(p, n):
                h, qt = n // 2, n % 2
                pe.wait_ge(mixw_t_ready, 8 * p + n + 1)
                if n == 0:
                    pe.wait_ge(dve_evac, dve_pairs(p, 5))
                kt = key_tiles(p)
                for j, t in enumerate(kt):
                    mm = pe.matmul(PS[:, HEADS_OUT + qt, h * P:(h + 1) * P], mixw_t[:, h % 2, j, qt * P:(qt + 1) * P],
                                   v[:, t, h * P:(h + 1) * P], start=(j == 0), stop=(j == len(kt) - 1))
                mm.then_inc(pv_done, 1)

            def ctx_keys(nid_lo):
                pair(start["ctx_k"], 0, tiles=normed_tiles(nid_lo))
                pair(start["ctx_k"] + 2, 1)
                for j in range(2):
                    pe.wait_ge(dve_evac, 24 + j + 1)
                    token_pair(start["ctx_v"] + 2 * j, j)

            def run_pass(p, nid, nid_lo):
                c0 = start[f"pass{p}"]
                on_x = not ON_CTX[p]
                rb = ROPE_BASE[p]
                for j in range(4):
                    if j >= 2:
                        pe.wait_ge(dve_evac, dve_pairs(p, j - 2))
                    pair(c0 + 2 * j, j % 2, tiles=normed_tiles(nid_lo) if j == 0 else None)
                    if on_x and j >= 1:
                        rotate(rb + j - 1, "perm_a")
                pe.wait_ge(dve_evac, dve_pairs(p, 2))
                token_pair(c0 + part["v"], 0)
                if on_x:
                    rotate(rb + 3, "perm_a")
                for n in range(8):
                    if n == 0:
                        if on_x:
                            pe.wait_ge(rope_out, rb + 4)
                        else:
                            pe.wait_ge(dve_evac, dve_pairs(p, 3))
                    scores(p, n)
                    if n >= 1:
                        values(p, n - 1)
                    j = 5 + n
                    if j < 12:
                        pe.wait_ge(dve_evac, dve_pairs(p, j - 2))
                        if j == 5:
                            token_pair(c0 + part["v"] + 2, 1)
                        else:
                            pair(c0 + 2 * j, j % 2)
                    else:
                        pe.wait_ge(dve_evac, dve_pairs(p, j - 2))
                        pair(c0 + 2 * j, j % 2)
                    turn(p, n)
                pe.wait_ge(dve_evac, dve_pairs(p, 11))
                pair(c0 + part["gu"] + 2, 1)
                values(p, 7)
                pe.wait_ge(u_ready, p + 1)
                for t in range(TT):
                    for c in range(KB):
                        mm = pe.transpose(PS[:, [TURN, MISC][t], c * P:(c + 1) * P], u[:, c, t * P:(t + 1) * P],
                                          const("ident"))
                mm.then_inc(u_t, 1)
                pe.wait_ge(act_evac, act_pairs(p, 0))
                token_pair(c0 + part["gv"], 0)
                pe.wait_ge(head_y_ready, p + 1)
                for h in range(HEADS_A):
                    for qt in range(TT):
                        mm = pe.transpose(PS[:, SCORES + h // 2, (h % 2) * T + qt * P:(h % 2) * T + (qt + 1) * P],
                                          head_y[:, h, qt, :], const("ident"))
                mm.then_inc(head_t, 1)
                pe.wait_ge(act_evac, act_pairs(p, 1))
                token_pair(c0 + part["gv"] + 2, 1)
                pe.wait_ge(u_tok_ready, p + 1)
                pe.wait_ge(y_ready, p + 1)
                for n, name in enumerate(("dft_cos", "dft_sin_u")):
                    dft = const(name).rearrange("p (t f) -> p t f", t=TT)
                    for f in range(2):
                        for t in range(TT):
                            mm = pe.matmul(PS[:, [SCORES, HEADS_OUT][n] + f, :], dft[:, t, f * P:(f + 1) * P],
                                           u_tok[:, t, :], start=(t == 0), stop=(t == 1))
                mm.then_inc(dft_done, 1)
                for j in range(2):
                    pe.wait_ge(act_evac, act_pairs(p, 2 + j))
                    pair(c0 + part["ga"] + 2 * j, j)
                pe.wait_ge(yspec_ready, p + 1)
                idft = const("idft").rearrange("p (a t) -> p a t", a=4)
                for c in range(KB):
                    for a_ in range(4):
                        mm = pe.matmul(PS[:, [TURN, MISC][c // 2], (c % 2) * T:(c % 2 + 1) * T],
                                       yspec[:, a_, c * P:(c + 1) * P], idft[:, a_, :], start=(a_ == 0), stop=(a_ == 3))
                mm.then_inc(conv_done, 1)
                for j in range(2):
                    pe.wait_ge(act_evac, act_pairs(p, 4 + j))
                    pair(c0 + part["gb"] + 2 * j, j)
                pe.wait_ge(lnv_ready, p + 1)
                mixw_g = row("mix_w").rearrange("p (g t) -> p g t", g=8)
                for g in range(8):
                    for c in range(TT):
                        o = SUB * (g % 2)
                        f = (g // 2) * T + c * P
                        mm = pe.matmul(PS[o:o + SUB, SCORES + f // 512, f % 512:f % 512 + P],
                                       lnv[:, c, g * SUB:(g + 1) * SUB], mixw_g[:, g, :], start=True, stop=True)
                mm.then_inc(mixed, 1)
                for j in range(2):
                    pe.wait_ge(act_evac, act_pairs(p, 6 + j))
                    pair(c0 + part["gc"] + 2 * j, j)
                with pe.Fori(0, 4) as i:
                    for b in range(3):
                        c = c0 + part["merge"] + 3 * b
                        pe.wait_ge(merge_free, i * 3 + (15 * p + b + 1))
                        slot_ready(c, i, 9)
                        r = c % RING
                        for o in range(2):
                            for kk in range(KB):
                                w = slice(kk * T + o * P, kk * T + (o + 1) * P)
                                mm = mm3(PS[:, 2 * b, o * T:(o + 1) * T], w_hi[:, r, w], w_lo[:, r, w],
                                         g_hi[:, KB * b + kk, :], g_lo[:, KB * b + kk, :], kk == 0, kk == KB - 1)
                        mm.then_inc(w_used, 1)
                        pair(c + 1, 2 * b + 1, i, 9)
                for j in range(4):
                    if j >= 2:
                        pe.wait_ge(src_ready, 4 * OUT_EVENT[p] + j - 1)
                    pair(c0 + part["wo"] + 2 * j, 4 + j % 2,
                         tiles=(lambda kk: (m_lo, KD * p + kk + 1)) if j == 0 else None)
                norm(nid)

            def down(c, s, f, i, per, last):
                slot_ready(c, i, per)
                r = c % RING
                for o in range(KD):
                    w = slice(o * P, o * P + P)
                    mm = mm3(PS[:, 4 + o // 2, (o % 2) * T:(o % 2 + 1) * T], w_hi[:, r, w], w_lo[:, r, w],
                             act_hi[:, s, f, :], act_lo[:, s, f, :], False, last, skip_group_check=True)
                mm.then_inc(w_used, 1)

            def ffn(n, nid_lo):
                c0 = start[f"ffn{n}"]
                for b in range(4):
                    pe.matmul(PS[:, 4 + b, :], zeros[:, 0:P], zeros[:, :], start=True, stop=False,
                              skip_group_check=True)

                def gate_up(c, s, i, base, tiles=None):
                    pe.wait_ge(gu_free, base if i is None else i * 2 + base)
                    pair(c, 2 * s, i, 12, tiles)
                    pair(c + 2, 2 * s + 1, i, 12)

                def downs(c, s, i, base, last=False):
                    pe.wait_ge(act_ready, base if i is None else i * 2 + base)
                    for f in range(2):
                        down(c + f, s, f, i, 12, last)

                g, a_ = 13 * n, FPAIRS * n
                gate_up(c0, 0, None, g + 1, normed_tiles(nid_lo))
                with pe.Fori(0, 4) as i:
                    for e in range(2):
                        c = c0 + 4 + 6 * e
                        gate_up(c, (1 + e) % 2, i, g + 2 + e)
                        downs(c + 4, e % 2, i, a_ + 1 + e)
                for pr in (9, 10):
                    c = c0 + 4 + 6 * (pr - 1)
                    gate_up(c, pr % 2, None, g + pr + 1)
                    downs(c + 4, (pr - 1) % 2, None, a_ + pr)
                downs(c0 + FFN_SLOTS - 2, 10 % 2, None, a_ + 11, True)

            def scores2(n, unit):
                if unit >= 1 or n >= 1:
                    pe.wait_ge(p2n_ready, 8 * n + unit)
                for h in range(2):
                    s = slice(HD * h, HD * h + HD)
                    pe.matmul(PS[:, SCORES + h, 0:P], q[s, unit, 0:P], k[s, unit, 0:P], start=True, stop=True)
                    mm = pe.matmul(PS[:, SCORES + h, P:SEG], q[s, unit, P:T], k[s, unit, :], start=True, stop=True)
                mm.then_inc(sc2_done, 1)

            def turn2(n, unit):
                pe.wait_ge(p2n_ready, 8 * n + unit + 1)
                if unit >= 1 or n >= 1:
                    pe.wait_ge(p2t_ready, 8 * n + unit)
                for h in range(2):
                    for j in range(3):
                        mm = pe.transpose(PS[:, TURN + h, j * P:(j + 1) * P], probs2[:, h, j * P:(j + 1) * P],
                                          const("ident"))
                mm.then_inc(turned2, 1)

            def values2(n, unit):
                pe.wait_ge(p2t_ready, 8 * n + unit + 1)
                if unit >= 1 or n >= 1:
                    pe.wait_ge(o2_ready, 8 * n + unit)
                for h in range(2):
                    o, c = HD * h, unit * P + HD * h
                    pe.matmul(PS[o:o + HD, 6, 0:T], v2[:, 0, c:c + HD], probs2_t[:, unit % 2, h, 0:T],
                              start=True, stop=False)
                    mm = pe.matmul(PS[o:o + HD, 6, P:T], v2[:, 1, c:c + HD], probs2_t[:, unit % 2, h, T:SEG],
                                   start=False, stop=True)
                mm.then_inc(pv2_done, 1)

            def out_proj(n, event, name):
                c0 = start[name]
                for j in range(4):
                    if j >= 2:
                        pe.wait_ge(src_ready, 4 * event + j - 1)
                    pair(c0 + 2 * j, 4 + j % 2, hi=g_hi, lo=g_lo,
                         tiles=(lambda kk: (o2_ready, 8 * n + kk + 1)) if j == 0 else None)

            pe.wait_ge(ones_ready, 1)
            modulation(0)
            filter_(0)
            norm(0)
            run_pass(0, 1, 0)
            norm(2)
            run_pass(1, 3, 1)
            modulation(1)
            filter_(1)
            norm(4)
            ctx_keys(2)
            norm(5)
            run_pass(2, 6, 3)
            norm(7)
            ffn(0, 4)
            norm(8)
            c0 = start["qkv0"]
            for j in range(8):
                if j >= 2:
                    pe.wait_ge(qkv_evac, j - 1)
                pair(c0 + 2 * j, j % 2, tiles=normed_tiles(5) if j == 0 else None)
                if j >= 1:
                    rotate(8 + j - 1, "perm_b")
            rotate(8 + 7, "perm_b")
            pe.wait_ge(rope_out, 16)
            for n in range(8):
                scores2(0, n)
                if n >= 1:
                    values2(0, n - 1)
                if n < 4:
                    pe.wait_ge(qkv_evac, 7 + n)
                    token_pair(c0 + 16 + 2 * n, n % 2)
                if n == 0:
                    pe.wait_ge(qkv_evac, 8)
                turn2(0, n)
                if n < 4:
                    pe.wait_ge(qkv_evac, 9 + n)
            values2(0, 7)
            out_proj(0, 7, "wo0")
            norm(9)
            ffn(1, 6)
            norm(10)
            c0 = start["kv"]
            for j in range(4):
                if j >= 2:
                    pe.wait_ge(qkv_evac, 12 + j - 1)
                pair(c0 + 2 * j, j % 2, tiles=normed_tiles(7) if j == 0 else None)
                if j >= 1:
                    rotate(16 + j - 1, "perm_b")
            for j in range(4):
                pe.wait_ge(qkv_evac, 12 + 3 + j)
                token_pair(c0 + 8 + 2 * j, j % 2)
                if j == 0:
                    rotate(16 + 3, "perm_b")
            pe.wait_ge(qkv_evac, 20)
            norm(11)
            ffn(2, 8)
            norm(12)
            c0 = start["q1"]
            for j in range(4):
                if j >= 2:
                    pe.wait_ge(qkv_evac, 20 + j - 1)
                pair(c0 + 2 * j, j % 2, tiles=normed_tiles(9) if j == 0 else None)
                if j >= 1:
                    rotate(20 + j - 1, "perm_b")
            rotate(20 + 3, "perm_b")
            pe.wait_ge(rope_out, 24)
            for n in range(8):
                scores2(1, n)
                if n >= 1:
                    values2(1, n - 1)
                turn2(1, n)
            values2(1, 7)
            out_proj(1, 10, "wo1")
            norm(13)
            ffn(3, 10)
            norm(14)

        @block.scalar
        def _(act):
            chain = [0]

            def link(ins):
                chain[0] += 1
                ins.then_inc(act_chain, 1)
                act.wait_ge(act_chain, chain[0])

            def split(c, i=None, per=0):
                if i is None and c >= TOTAL:
                    return
                r = c % RING
                if i is None:
                    act.wait_ge(raw_loaded[r], 16 * (c // RING + 1))
                    if c >= RING:
                        act.wait_ge(w_used, c - RING + 1)
                else:
                    act.wait_ge(raw_loaded[r], i * (16 * per // RING) + 16 * (c // RING + 1))
                    act.wait_ge(w_used, i * per + (c - RING + 1))
                nc.scalar.activation(w_hi[:, r, :], raw[:, r, :], ACT.Copy).then_inc(w_hi_ready, 1)

            def splits(c, n=2):
                for j in range(n):
                    split(c + j + RING)

            def norm(nid, src, event=None):
                for c in range(4):
                    if event is None:
                        act.wait_ge(x_loaded, 32)
                    else:
                        act.wait_ge(src_ready, 4 * event + c + 1)
                    nc.scalar.activation(sq[:, 2 * c:2 * c + 2, :], src[:, 2 * c:2 * c + 2, :],
                                         ACT.Square).then_inc(sq_ready, 1)
                act.wait_ge(ms_ready, nid + 1)
                if nid == 2:
                    act.wait_ge(src_ready, 8)
                nc.scalar.activation(rt, PS[:, 0, 0:T], ACT.Sqrt, bias=eps[:, 0:1]).then_inc(rt_ready, 1)

            def high(nid_lo, shift=None):
                for kk in range(KD):
                    act.wait_ge(norm_v, KD * nid_lo + kk + 1)
                    if shift is None:
                        ins = nc.scalar.activation(h_hi[:, kk, :], normed[:, kk, :], ACT.Copy)
                    else:
                        ins = nc.scalar.activation(h_hi[:, kk, :], normed[:, kk, :], ACT.Identity,
                                                   bias=shift(kk))
                    ins.then_inc(norm_hi, 1)

            def modulation(l):
                c0 = start[f"ada{l}"]
                if l == 0:
                    act.wait_ge(consts_loaded, 32)
                    nc.scalar.activation(c_act[:, :], col("cond", 0, 16), ACT.Silu).then_inc(cond_act, 1)
                    for c in range(RING):
                        split(c)
                with act.Fori(0, ADA_SLOTS // RING) as i:
                    for j in range(RING):
                        split(c0 + RING + j, i, RING)

            def filter_(l):
                for n, hid in enumerate((hid1, hid2)):
                    act.wait_ge(fil_arg, 2 * l + n + 1)
                    nc.scalar.activation(hid[0:64, :], arg[0:64, :], ACT.Sin).then_inc(fil_sin, 1)
                act.wait_ge(lam_dots, l + 1)
                nc.scalar.activation(dot_exp, dots, ACT.Exp).then_inc(lam_exp, 1)
                act.wait_ge(fil_h, l + 1)
                nc.scalar.activation(h_sq[:, :, :, :], hw[:, :, :, :], ACT.Square).then_inc(fil_sq, 1)
                act.wait_ge(fil_mm, 5 * l + 4)
                nc.scalar.activation(conv_rt, PS[:, 2, 0:8:2], ACT.Sqrt, scale=float(D)).then_inc(fil_rt, 1)

            def exps(p, n):
                nk = P * len(key_tiles(p))
                act.wait_ge(nm_ready, 8 * p + n + 1)
                for m in range(2):
                    ins = nc.scalar.activation(probs[:, m, 0:nk], PS[:, SCORES + m, 0:nk], ACT.Exp,
                                               bias=neg_max[:, m:m + 1], scale=SUB ** -0.5,
                                               accum_out=den[:, m:m + 1])
                ins.then_inc(p_ready, 1)

            def squares(p, n):
                h, qt = n // 2, n % 2
                act.wait_ge(pv_done, 8 * p + n + 1)
                ins = nc.scalar.activation(squared[:, n, :], PS[:, HEADS_OUT + qt, h * P:(h + 1) * P], ACT.Square,
                                           accum_out=head_ss[:, 2 * h + qt:2 * h + qt + 1])
                if n == 7:
                    link(ins)

            def run_pass(p, nid):
                c0 = start[f"pass{p}"]
                splits(c0, 8)
                splits(c0 + part["v"])
                for n in range(8):
                    exps(p, n)
                    splits(c0 + part["v"] + 2 + 2 * n)
                    if n >= 1:
                        squares(p, n - 1)
                splits(c0 + part["gu"] + 2)
                squares(p, 7)
                nc.scalar.activation(head_rt, head_ss, ACT.Sqrt, scale=1.0 / P,
                                     bias=eps[:, 0:1]).then_inc(head_rt_ready, 1)
                for j in range(2):
                    act.wait_ge(w_used, c0 + part["gu"] + 2 * j + 2)
                    nc.scalar.activation(gu[:, 2 * j:2 * j + 2, :], PS[:, j, :], ACT.Gelu).then_inc(act_evac, 1)
                for j in range(2):
                    act.wait_ge(w_used, c0 + part["gv"] + 2 * j + 2)
                    nc.scalar.activation(gv[:, :, j * T:(j + 1) * T], PS[:, j, :].rearrange("p (t c) -> p t c", t=TT),
                                         ACT.Gelu).then_inc(act_evac, 1)
                    splits(c0 + part["gv"] + 2 * j)

                def gates(name, b):
                    for j in range(2):
                        c = c0 + part[name] + 2 * j
                        act.wait_ge(w_used, c + 2)
                        if b >= 1:
                            act.wait_ge(gated_ready, 6 * p + 2 * (b - 1) + j + 1)
                        nc.scalar.activation(gate_act[:, j, :], PS[:, j, :], ACT.Silu).then_inc(act_evac, 1)
                        splits(c)

                gates("ga", 0)
                act.wait_ge(ln_centered, p + 1)
                for t in range(TT):
                    ins = nc.scalar.activation(lnv[:, t, :], gvc[:, t, :], ACT.Square,
                                               accum_out=ln_ss[:, t:t + 1])
                link(ins)
                nc.scalar.activation(ln_rt, ln_ss, ACT.Sqrt, scale=1.0 / BR,
                                     bias=eps[:, 0:1]).then_inc(ln_rt_ready, 1)
                gates("gb", 1)
                gates("gc", 2)
                with act.Fori(0, 4) as i:
                    for b in range(3):
                        c = c0 + part["merge"] + 3 * b
                        split(c + RING, i, 9)
                        split(c + 1 + RING, i, 9)
                        act.wait_ge(merge_free, i * 3 + (15 * p + b + 1))
                        act.wait_ge(w_used, i * 9 + (c + 3))
                        nc.scalar.activation(sel[:, b, :], PS[:, 2 * b + 1, :], ACT.Sigmoid).then_inc(sel_ready, 1)
                        split(c + 2 + RING, i, 9)
                act.wait_ge(merge_added, 8 * (p + 1))
                act.wait_ge(w_used, c0 + part["wo"])
                for kk in range(KD):
                    nc.scalar.activation(h_hi[:, kk, :], merged[:, kk, :], ACT.Copy).then_inc(m_hi, 1)
                splits(c0 + part["wo"], 8)
                norm(nid, branch_out, OUT_EVENT[p])

            def ffn(n):
                c0 = start[f"ffn{n}"]

                def post(c, s, i, base, sbase):
                    for j in range(3):
                        split(c + j + RING, i, 12)
                    act.wait_ge(gu_free, base if i is None else i * 2 + base)
                    act.wait_ge(w_used, c + 4 if i is None else i * 12 + (c + 4))
                    nc.scalar.activation(silu[:, s, :], PS[:, 2 * s, :], ACT.Silu).then_inc(silu_ready, 1)
                    split(c + 3 + RING, i, 12)

                def downs(c, i):
                    for f in range(2):
                        split(c + f + RING, i, 12)

                g = 13 * n
                post(c0, 0, None, g + 1, 0)
                with act.Fori(0, 4) as i:
                    for e in range(2):
                        c = c0 + 4 + 6 * e
                        post(c, (1 + e) % 2, i, g + 2 + e, 0)
                        downs(c + 4, i)
                for pr in (9, 10):
                    c = c0 + 4 + 6 * (pr - 1)
                    post(c, pr % 2, None, g + pr + 1, 0)
                    downs(c + 4, None)
                downs(c0 + FFN_SLOTS - 2, None)

            def exps2(n, unit):
                act.wait_ge(nm2_ready, 8 * n + unit + 1)
                for h in range(2):
                    nc.scalar.activation(probs2[:, h, 0:P], biased[:, h, 0:P], ACT.Exp,
                                         bias=neg_max[:, h:h + 1], accum_out=den[:, h:h + 1])
                    ins = nc.scalar.activation(probs2[:, h, P:SEG], biased[:, h, P:SEG], ACT.Exp,
                                               bias=neg_max[:, 2 + h:3 + h], accum_out=den[:, 2 + h:3 + h])
                ins.then_inc(p2_ready, 1)

            act.wait_ge(ones_ready, 1)
            modulation(0)
            filter_(0)
            norm(0, cx)
            high(0, lambda kk: mod[:, kk, 1:2])
            run_pass(0, 1)
            norm(2, x)
            high(1, lambda kk: mod[:, kk, 0:1])
            run_pass(1, 3)
            modulation(1)
            filter_(1)
            norm(4, cx, 1)
            high(2, lambda kk: mod[:, kk, 1:2])
            splits(start["ctx_k"], 8)
            norm(5, x, 3)
            high(3, lambda kk: mod[:, kk, 0:1])
            run_pass(2, 6)
            norm(7, x, 5)
            high(4)
            ffn(0)
            norm(8, x, 6)
            high(5)
            splits(start["qkv0"], 16)
            for n in range(8):
                exps2(0, n)
                if n < 4:
                    splits(start["qkv0"] + 16 + 2 * n)
            splits(start["wo0"], 8)
            norm(9, x, 7)
            high(6)
            ffn(1)
            norm(10, x, 8)
            high(7)
            splits(start["kv"], 16)
            norm(11, x, 8)
            high(8)
            ffn(2)
            norm(12, x, 9)
            high(9)
            splits(start["q1"], 8)
            for n in range(8):
                exps2(1, n)
            splits(start["wo1"], 8)
            norm(13, x, 10)
            high(10)
            ffn(3)
            norm(14, x, 11)

        @block.vector
        def _(dve):
            V = nc.vector
            chain = [0]

            def link(ins):
                chain[0] += 1
                ins.then_inc(dve_chain, 1)
                dve.wait_ge(dve_chain, chain[0])

            def split(c, i=None, per=0):
                if i is None and c >= TOTAL:
                    return
                r = c % RING
                dve.wait_ge(w_hi_ready, c + 1 if i is None else i * per + (c + 1))
                V.tensor_tensor(w_lo[:, r, :], raw[:, r, :], f32(w_hi[:, r, :]), ALU.subtract).then_inc(w_lo_ready, 1)

            def splits(c, n=2):
                for j in range(n):
                    split(c + j + RING)

            def norm_rstd(nid):
                dve.wait_ge(rt_ready, nid + 1)
                link(V.reciprocal(rstd, rt))

            def norm_split(nid, nid_lo, src, g, shift=None):
                norm_rstd(nid)

                def scale_(kk):
                    V.scalar_tensor_tensor(normed[:, kk, :], src[:, kk, :], g(kk), rstd, ALU.mult,
                                           ALU.mult).then_inc(norm_v, 1)

                def low(kk):
                    dve.wait_ge(norm_hi, KD * nid_lo + kk + 1)
                    if shift is None:
                        ins = V.tensor_tensor(h_lo[:, kk, :], normed[:, kk, :], f32(h_hi[:, kk, :]), ALU.subtract)
                    else:
                        ins = V.scalar_tensor_tensor(h_lo[:, kk, :], normed[:, kk, :], shift(kk), f32(h_hi[:, kk, :]),
                                                     ALU.add, ALU.subtract)
                    ins.then_inc(norm_lo, 1)

                scale_(0)
                scale_(1)
                for kk in range(KD):
                    if kk + 2 < KD:
                        scale_(kk + 2)
                    low(kk)

            def post_norm(p, nid):
                dst = sources(p)
                w = 1 if ON_CTX[p] else 0
                norm_rstd(nid)
                for kk in range(KD):
                    ins = V.scalar_tensor_tensor(branch_out[:, kk, :], branch_out[:, kk, :], gate[:, kk, w:w + 1], rstd,
                                                 ALU.mult, ALU.mult)
                link(ins)
                for c in range(4):
                    s = slice(2 * c, 2 * c + 2)
                    V.tensor_tensor(dst[:, s, :], dst[:, s, :], branch_out[:, s, :], ALU.add).then_inc(src_ready, 1)

            def modulation(l):
                c0 = start[f"ada{l}"]
                if l == 0:
                    dve.wait_ge(cond_act, 1)
                    V.tensor_copy(c_hi[:, :, :], c_act[:, :].rearrange("p (k w) -> p k w", w=2)).then_inc(cond_hi, 1)
                    dve.wait_ge(cond_hi, 1)
                    V.tensor_tensor(c_lo[:, :, :], c_act[:, :].rearrange("p (k w) -> p k w", w=2), f32(c_hi[:, :, :]),
                                    ALU.subtract).then_inc(cond_ready, 1)
                    for c in range(RING):
                        split(c)
                with dve.Fori(0, ADA_SLOTS // RING) as i:
                    for j in range(RING):
                        split(c0 + RING + j, i, RING)

            def mod_vectors(l):
                dve.wait_ge(w_used, start[f"ada{l}"] + ADA_SLOTS)
                m = PS[:, 1, 0:48].rearrange("p (f w) -> p f w", w=2)
                for w in range(2):
                    ins = V.tensor_tensor(mod[:, :, w], m[:, :, w], col(f"ada_b{l}", 0, 24), ALU.add)
                link(ins)
                for w in range(2):
                    V.scalar_tensor_tensor(gain[:, :, w], mod[:, KD:2 * KD, w], 1.0, col(f"norm_pre{l}", 0, KD),
                                           ALU.add, ALU.mult)
                    ins = V.tensor_tensor(gate[:, :, w], mod[:, 2 * KD:3 * KD, w], col(f"norm_post{l}", 0, KD),
                                          ALU.mult)
                link(ins)

            def filter_(l):
                lam_init = 0.8 - 0.6 * math.exp(-0.3 * l)
                for n in range(2):
                    dve.wait_ge(fil_mm, 5 * l + n + 1)
                    a_ = arg[0:64, :]
                    t_ = turns[0:64, :]
                    link(V.tensor_scalar(a_, PS[0:64, 2 + n, 0:T], col(f"filter_b{n + 1}{l}")[0:64, :],
                                         col(f"freq{n}{l}")[0:64, :], ALU.add, ALU.mult))
                    link(V.tensor_scalar(t_, a_, 1 / (2 * math.pi), ROUND, ALU.mult, ALU.add))
                    link(V.tensor_scalar(t_, t_, -ROUND, None, ALU.add))
                    link(V.scalar_tensor_tensor(a_, t_, -TWO_PI_HI, a_, ALU.mult, ALU.add))
                    link(V.scalar_tensor_tensor(a_, t_, -TWO_PI_LO, a_, ALU.mult, ALU.add))
                    V.tensor_scalar(a_, a_, PI_SAFE, -PI_SAFE, ALU.min, ALU.max).then_inc(fil_arg, 1)
                dve.wait_ge(layer_loaded, 48 * (l + 1))
                lp = lam_rows.rearrange("p (a b d) -> p a b d", a=2, b=2)
                link(V.tensor_tensor(turns[:, 0:2 * SUB].rearrange("p (a d) -> p a d", a=2), lp[:, :, 0, :], lp[:, :, 1, :],
                                     ALU.mult))
                V.reduce_sum(dots, turns[:, 0:2 * SUB].rearrange("p (a d) -> p a d", a=2), AX_X).then_inc(lam_dots, 1)
                dve.wait_ge(lam_exp, l + 1)
                link(V.tensor_tensor(lam, dot_exp[:, 0:1], dot_exp[:, 1:2], ALU.subtract))
                link(V.tensor_scalar(neg_lam, lam, -1.0, -lam_init, ALU.mult, ALU.add))
                link(V.tensor_scalar(subln_g, col(f"subln{l}"), 1.0 - lam_init, None, ALU.mult))
                dve.wait_ge(fil_mm, 5 * l + 3)
                dec = const("decay").rearrange("p (t c) -> p t c", t=TT)
                for d in range(2):
                    ins = V.tensor_tensor(hw[:, d, :, :], PS[:, 4 + 2 * d:6 + 2 * d, :], dec, ALU.mult)
                link(ins)
                link(V.memset(hw[0:1, 1, 0, :], 0.0))
                V.tensor_tensor(h_sum[:, :, :], hw[:, 0, :, :], hw[:, 1, :, :], ALU.add)
                V.tensor_tensor(h_dif[:, :, :], hw[:, 0, :, :], hw[:, 1, :, :], ALU.subtract).then_inc(fil_h, 1)
                dve.wait_ge(fil_rt, l + 1)
                V.reciprocal(conv_rs, conv_rt)
                dve.wait_ge(fil_mm, 5 * l + 5)
                V.tensor_copy(spec_re[:, :, :], PS[:, 4:6, :])
                V.tensor_copy(spec_im[:, :, :], PS[:, 6:8, :])
                link(V.tensor_copy(spec_ny[:, :], PS[:, 3, :]))

            def rope_turn(n, dst, cos, sin):
                def two(t):
                    return const(t).rearrange("p (o t) -> p o t", o=1).to_broadcast([P, 2, T])
                dve.wait_ge(rope_rot, n + 1)
                V.tensor_tensor(rope_a.rearrange("p (k t) -> p k t", k=2), rope_raw[:, n % 2, :].rearrange("p (k t) -> p k t", k=2),
                                two(cos), ALU.mult)
                link(V.tensor_tensor(rope_b.rearrange("p (k t) -> p k t", k=2),
                                     PS[:, MISC, :].rearrange("p (k t) -> p k t", k=2), two(sin), ALU.mult))
                V.tensor_tensor(dst, rope_a.rearrange("p (k t) -> p k t", k=2), rope_b.rearrange("p (k t) -> p k t", k=2),
                                ALU.add).then_inc(rope_out, 1)

            def take_values(c, bank, dst, done):
                dve.wait_ge(w_used, c + 2)
                V.tensor_copy(dst, PS[:, bank, :].rearrange("p (t c) -> p t c", t=TT)).then_inc(done, 1)

            def softmax_max(p, n):
                nk = P * len(key_tiles(p))
                dve.wait_ge(sc_done, 8 * p + n + 1)
                link(V.reduce_max(mx[:, 0:2], PS[:, SCORES:SCORES + 2, 0:nk], AX_X))
                V.tensor_scalar(neg_max[:, 0:2], mx[:, 0:2], -(SUB ** -0.5), None, ALU.mult).then_inc(nm_ready, 1)

            def softmax_mix(p, n):
                nk = P * len(key_tiles(p))
                dve.wait_ge(p_ready, 8 * p + n + 1)
                link(V.reciprocal(rden[:, 0:2], den[:, 0:2]))
                V.tensor_tensor(wden[:, 0:1], rden[:, 1:2], neg_lam, ALU.mult)
                link(V.tensor_scalar(mixw[:, 0:nk], probs[:, 0, 0:nk], rden[:, 0:1], None, ALU.mult))
                V.scalar_tensor_tensor(mixw[:, 0:nk], probs[:, 1, 0:nk], wden[:, 0:1], mixw[:, 0:nk], ALU.mult,
                                       ALU.add).then_inc(mixw_ready, 1)

            def take_turned(p, n):
                h, qt = n // 2, n % 2
                nt = len(key_tiles(p))
                dve.wait_ge(turned, 8 * p + n + 1)
                V.tensor_copy(mixw_t[:, h % 2, 0:nt, qt * P:(qt + 1) * P],
                              PS[:, TURN, 0:nt * P].rearrange("p (k t) -> p k t", k=nt)).then_inc(mixw_t_ready, 1)

            def short_conv(l, c, bank, tile):
                dve.wait_ge(w_used, c + 2)

                def tap(j, f):
                    return col(f"short_w{l}", 12 * j + f)
                for a_ in range(2):
                    f = tile + a_
                    z = PS[:, bank, a_ * T:(a_ + 1) * T]
                    ins = V.tensor_scalar(hy[:, f, :], z, tap(1, f), col(f"short_b{l}", f), ALU.mult, ALU.add)
                link(ins)
                for a_ in range(2):
                    f = tile + a_
                    z = PS[:, bank, a_ * T:(a_ + 1) * T]
                    ins = V.scalar_tensor_tensor(hy[:, f, 1:T], z[:, 0:T - 1], tap(0, f), hy[:, f, 1:T], ALU.mult,
                                                 ALU.add)
                link(ins)
                for a_ in range(2):
                    f = tile + a_
                    z = PS[:, bank, a_ * T:(a_ + 1) * T]
                    ins = V.scalar_tensor_tensor(hy[:, f, 0:T - 1], z[:, 1:T], tap(2, f), hy[:, f, 0:T - 1], ALU.mult,
                                                 ALU.add)
                ins.then_inc(dve_evac, 1)

            def gating(p, b, c0):
                name = ("ga", "gb", "gc")[b]
                for j in range(2):
                    s = slice(KB * b + 2 * j, KB * b + 2 * j + 2)
                    dve.wait_ge(act_evac, act_pairs(p, 4 + 2 * b + j))
                    gd = gated.rearrange("p (k t) -> p k t", k=2)
                    link(V.tensor_tensor(gd, y[:, 2 * j:2 * j + 2, :],
                                         gate_act[:, j, :].rearrange("p (k t) -> p k t", k=2), ALU.mult))
                    link(V.tensor_copy(g_hi[:, s, :], gd))
                    V.tensor_tensor(g_lo[:, s, :], gd, f32(g_hi[:, s, :]), ALU.subtract).then_inc(gated_ready, 1)
                    splits(c0 + part[name] + 2 * j)

            def run_pass(p, nid):
                l = LAYER_OF[p]
                c0 = start[f"pass{p}"]
                on_x = not ON_CTX[p]
                rb = ROPE_BASE[p]
                base = 0 if on_x else 4
                dsts = [k[:, base:base + 2, :], k[:, base + 2:base + 4, :], q[:, 0:2, :], q[:, 2:4, :]]
                for j in range(4):
                    c = c0 + 2 * j
                    if on_x:
                        rope_copy(rb + j, j % 2, c, dve_evac)
                        splits(c)
                        if j >= 1:
                            rope_turn(rb + j - 1, dsts[j - 1], "cos_a", "sin_a")
                    else:
                        dve.wait_ge(w_used, c + 2)
                        V.tensor_copy(dsts[j], PS[:, j % 2, :].rearrange("p (k t) -> p k t", k=2)).then_inc(dve_evac, 1)
                        splits(c)
                kt = 0 if on_x else 2
                take_values(c0 + part["v"], 0, v[:, kt:kt + 2, 0:T], dve_evac)
                if on_x:
                    rope_turn(rb + 3, dsts[3], "cos_a", "sin_a")
                splits(c0 + part["v"])
                for n in range(8):
                    softmax_max(p, n)
                    if n == 1:
                        take_values(c0 + part["v"] + 2, 1, v[:, kt:kt + 2, T:2 * T], dve_evac)
                    elif n >= 2:
                        short_conv(l, c0 + part["hy"] + 2 * (n - 2), n % 2, 2 * (n - 2))
                    softmax_mix(p, n)
                    splits(c0 + part["v"] + 2 + 2 * n)
                    take_turned(p, n)
                V.tensor_tensor(u, u, hy[:, 8:12, :], ALU.mult).then_inc(u_ready, 1)
                splits(c0 + part["gu"] + 2)
                dve.wait_ge(head_rt_ready, p + 1)
                link(V.reciprocal(head_rs, head_rt))
                for h in range(HEADS_A):
                    for qt in range(TT):
                        ins = V.tensor_scalar(head_y[:, h, qt, :], PS[:, HEADS_OUT + qt, h * P:(h + 1) * P],
                                              head_rs[:, 2 * h + qt:2 * h + qt + 1], None, ALU.mult)
                ins.then_inc(head_y_ready, 1)
                dve.wait_ge(u_t, p + 1)
                V.tensor_copy(u_tok[:, 0, :], PS[:, TURN, :])
                V.tensor_copy(u_tok[:, 1, :], PS[:, MISC, :]).then_inc(u_tok_ready, 1)
                splits(c0 + part["gv"])
                dve.wait_ge(head_t, p + 1)
                V.tensor_scalar(y[:, :, :], PS[:, SCORES:SCORES + 2, :].rearrange("p b (k t) -> p (b k) t", t=T),
                                subln_g, None, ALU.mult).then_inc(y_ready, 1)
                dve.wait_ge(y_ready, p + 1)
                splits(c0 + part["gv"] + 2)
                dve.wait_ge(act_evac, act_pairs(p, 3))
                link(V.reduce_sum(ln_sum, gv[:, :, :], AX_X))
                for t in range(TT):
                    ins = V.scalar_tensor_tensor(gvc[:, t, :], ln_sum[:, t:t + 1].to_broadcast([P, BR]), -1.0 / BR, gv[:, t, :],
                                                 ALU.mult, ALU.add)
                ins.then_inc(ln_centered, 1)
                dve.wait_ge(dft_done, p + 1)
                ur, ui = PS[:, SCORES:SCORES + 2, :], PS[:, HEADS_OUT:HEADS_OUT + 2, :]
                yr, yi = yspec[:, 0:2, :], yspec[:, 2:4, :]
                V.tensor_tensor(yr, ur, spec_re[:, :, :], ALU.mult)
                link(V.tensor_tensor(prod, ui, spec_im[:, :, :], ALU.mult))
                link(V.tensor_tensor(yr, yr, prod, ALU.subtract))
                V.tensor_tensor(yi, ur, spec_im[:, :, :], ALU.mult)
                V.tensor_tensor(prod[:, 0, :], ui[:, 0, :], spec_ny[:, :], ALU.mult)
                link(V.tensor_tensor(prod[:, 1, :], ui[:, 1, :], spec_re[:, 1, :], ALU.mult))
                V.tensor_tensor(yi, yi, prod, ALU.add).then_inc(yspec_ready, 1)
                gating(p, 0, c0)
                dve.wait_ge(ln_rt_ready, p + 1)
                link(V.reciprocal(ln_rs, ln_rt))
                for t in range(TT):
                    ins = V.scalar_tensor_tensor(gvc[:, t, :], gvc[:, t, :], ln_rs[:, t:t + 1], row("ln_g"), ALU.mult,
                                                 ALU.mult)
                link(ins)
                for t in range(TT):
                    ins = V.tensor_tensor(lnv[:, t, :], gvc[:, t, :], row("ln_b"), ALU.add)
                ins.then_inc(lnv_ready, 1)
                dve.wait_ge(conv_done, p + 1)
                for c in range(KB):
                    ins = V.tensor_scalar(u[:, c, :], u[:, c, :], col(f"conv_bias{l}", c), None, ALU.mult)
                link(ins)
                for c in range(KB):
                    ins = V.scalar_tensor_tensor(y[:, c, :], PS[:, [TURN, MISC][c // 2], (c % 2) * T:(c % 2 + 1) * T],
                                                 conv_rs[:, c:c + 1], u[:, c, :], ALU.mult, ALU.add)
                link(ins)
                link(V.tensor_tensor(y[:, :, :], y[:, :, :], hy[:, 0:4, :], ALU.mult))
                gating(p, 1, c0)
                dve.wait_ge(mixed, p + 1)
                bias = row("mix_bias").rearrange("p (k o t) -> p k o t", k=KB, o=1).to_broadcast([P, KB, TT, P])
                link(V.tensor_tensor(y[:, :, :].rearrange("p k (c t) -> p k c t", c=TT),
                                     PS[:, SCORES:SCORES + 2, :].rearrange("p b (k c t) -> p (b k) c t", c=TT, t=P),
                                     bias, ALU.add))
                link(V.tensor_tensor(y[:, :, :], y[:, :, :], gu[:, :, :], ALU.mult))
                gating(p, 2, c0)
                for b in range(3):
                    V.memset(stat[:, 90 + b:91 + b], 0.0).then_inc(merge_free, 1)
                with dve.Fori(0, 4) as i:
                    for b in range(3):
                        c = c0 + part["merge"] + 3 * b
                        split(c + RING, i, 9)
                        split(c + 1 + RING, i, 9)
                        dve.wait_ge(sel_ready, i * 3 + (12 * p + b + 1))
                        m = merged.rearrange("p k t -> p (k t)")[:, bass.ds(i * 512, 512)]
                        V.tensor_tensor(m if b == 0 else term, sel[:, b, :], PS[:, 2 * b, :], ALU.mult).then_inc(merge_free, 1)
                        if b >= 1:
                            dve.wait_ge(merge_free, i * 3 + (15 * p + 3 + b + 1))
                            if b == 2:
                                dve.wait_ge(merge_added, i * 2 + (8 * p + 1))
                            V.tensor_tensor(m, m, term, ALU.add).then_inc(merge_added, 1)
                        split(c + 2 + RING, i, 9)
                for kk in range(KD):
                    dve.wait_ge(m_hi, KD * p + kk + 1)
                    V.tensor_tensor(h_lo[:, kk, :], merged[:, kk, :], f32(h_hi[:, kk, :]), ALU.subtract).then_inc(m_lo, 1)
                for j in range(4):
                    c = c0 + part["wo"] + 2 * j
                    dve.wait_ge(w_used, c + 2)
                    V.tensor_copy(branch_out[:, 2 * j:2 * j + 2, :],
                                  PS[:, 4 + j % 2, :].rearrange("p (k t) -> p k t", k=2)).then_inc(src_ready, 1)
                    splits(c)
                post_norm(p, nid)

            def rope_copy(n, bank, c, done):
                dve.wait_ge(w_used, c + 2)
                if n >= 2:
                    dve.wait_ge(rope_rot, n - 1)
                V.tensor_copy(rope_raw[:, n % 2, :], PS[:, bank, :]).then_inc(rope_in, 1)
                dve.wait_ge(rope_in, n + 1)
                V.memset(stat[:, 94:95], 0.0).then_inc(done, 1)

            def ffn(n):
                c0 = start[f"ffn{n}"]
                for b in range(2):
                    V.memset(stat[:, 90 + b:91 + b], 0.0).then_inc(gu_free, 1)

                def at_(v_, i, per):
                    return v_ if i is None else i * per + v_

                def post(c, s, i, pr):
                    split(c + RING, i, 12)
                    split(c + 1 + RING, i, 12)
                    split(c + 2 + RING, i, 12)
                    b = FPAIRS * n + pr + 1
                    dve.wait_ge(silu_ready, at_(b, i, 2))
                    V.tensor_tensor(act_f, silu[:, s, :], PS[:, 2 * s + 1, :], ALU.mult).then_inc(gu_free, 1)
                    dve.wait_ge(gu_free, at_(13 * n + 2 + pr + 1, i, 2))
                    hi = act_hi[:, s, :, :].rearrange("p f t -> p (f t)")
                    lo = act_lo[:, s, :, :].rearrange("p f t -> p (f t)")
                    V.tensor_copy(hi, act_f).then_inc(act_hi_ready, 1)
                    dve.wait_ge(act_hi_ready, at_(b, i, 2))
                    V.tensor_tensor(lo, act_f, f32(hi), ALU.subtract).then_inc(act_ready, 1)
                    split(c + 3 + RING, i, 12)

                def downs(c, i):
                    for f in range(2):
                        split(c + f + RING, i, 12)

                post(c0, 0, None, 0)
                with dve.Fori(0, 4) as i:
                    for e in range(2):
                        c = c0 + 4 + 6 * e
                        post(c, (1 + e) % 2, i, 1 + e)
                        downs(c + 4, i)
                for pr in (9, 10):
                    c = c0 + 4 + 6 * (pr - 1)
                    post(c, pr % 2, None, pr)
                    downs(c + 4, None)
                downs(c0 + FFN_SLOTS - 2, None)
                dve.wait_ge(w_used, c0 + FFN_SLOTS)
                for j in range(4):
                    s = slice(2 * j, 2 * j + 2)
                    V.scalar_tensor_tensor(x[:, s, :], PS[:, 4 + j, :].rearrange("p (k t) -> p k t", k=2), 0.5, x[:, s, :],
                                           ALU.mult, ALU.add).then_inc(src_ready, 1)

            def softmax2(n, unit, table):
                dve.wait_ge(sc2_done, 8 * n + unit + 1)
                bias = const(table).rearrange("p (o s) -> p o s", o=1).to_broadcast([P, 2, SEG])
                link(V.scalar_tensor_tensor(biased[:, :, :], PS[:, SCORES:SCORES + 2, 0:SEG], HD ** -0.5, bias, ALU.mult, ALU.add))
                V.reduce_max(mx[:, 0:2], biased[:, :, 0:P], AX_X)
                link(V.reduce_max(mx[:, 2:4], biased[:, :, P:SEG], AX_X))
                V.tensor_scalar(neg_max[:, 0:4], mx[:, 0:4], -1.0, None, ALU.mult).then_inc(nm2_ready, 1)

            def normalize2(n, unit):
                dve.wait_ge(p2_ready, 8 * n + unit + 1)
                link(V.reciprocal(rden[:, 0:4], den[:, 0:4]))
                for h in range(2):
                    V.tensor_scalar(probs2[:, h, 0:P], probs2[:, h, 0:P], rden[:, h:h + 1], None, ALU.mult)
                    ins = V.tensor_scalar(probs2[:, h, P:SEG], probs2[:, h, P:SEG], rden[:, 2 + h:3 + h], None, ALU.mult)
                ins.then_inc(p2n_ready, 1)

            def take_turned2(n, unit):
                dve.wait_ge(turned2, 8 * n + unit + 1)
                V.tensor_copy(probs2_t[:, unit % 2, :, :], PS[:, TURN:TURN + 2, 0:SEG]).then_inc(p2t_ready, 1)

            def take_heads2(n, unit):
                dve.wait_ge(pv2_done, 8 * n + unit + 1)
                V.tensor_copy(g_hi[:, unit, :], PS[:, 6, 0:T]).then_inc(o2_hi, 1)
                dve.wait_ge(o2_hi, 8 * n + unit + 1)
                V.tensor_tensor(g_lo[:, unit, :], PS[:, 6, 0:T], f32(g_hi[:, unit, :]), ALU.subtract).then_inc(o2_ready, 1)

            def rope_phase(c0, n0, dsts, extra=None):
                for j, dst in enumerate(dsts):
                    c = c0 + 2 * j
                    rope_copy(n0 + j, j % 2, c, qkv_evac)
                    splits(c)
                    if j >= 1:
                        rope_turn(n0 + j - 1, dsts[j - 1], "cos_b", "sin_b")

            def out_proj(name):
                c0 = start[name]
                for j in range(4):
                    s = slice(2 * j, 2 * j + 2)
                    dve.wait_ge(w_used, c0 + 2 * j + 2)
                    V.tensor_tensor(x[:, s, :], x[:, s, :], PS[:, 4 + j % 2, :].rearrange("p (k t) -> p k t", k=2),
                                    ALU.add).then_inc(src_ready, 1)
                    splits(c0 + 2 * j)

            def pairs_of(t):
                return [t[:, 2 * j:2 * j + 2, :] for j in range(4)]

            V.memset(ones[:, :], 1.0 / D)
            V.memset(zeros[:, :], 0.0)
            V.memset(eps[:, :], EPS).then_inc(ones_ready, 1)
            modulation(0)
            mod_vectors(0)
            filter_(0)
            norm_split(0, 0, cx, lambda kk: gain[:, kk, 1:2], lambda kk: mod[:, kk, 1:2])
            run_pass(0, 1)
            norm_split(2, 1, x, lambda kk: gain[:, kk, 0:1], lambda kk: mod[:, kk, 0:1])
            run_pass(1, 3)
            modulation(1)
            mod_vectors(1)
            filter_(1)
            norm_split(4, 2, cx, lambda kk: gain[:, kk, 1:2], lambda kk: mod[:, kk, 1:2])
            for j in range(2):
                c = start["ctx_k"] + 2 * j
                dve.wait_ge(w_used, c + 2)
                V.tensor_copy(k[:, 4 + 2 * j:6 + 2 * j, :], PS[:, j, :].rearrange("p (k t) -> p k t", k=2)).then_inc(dve_evac, 1)
                splits(c)
            for j in range(2):
                c = start["ctx_v"] + 2 * j
                take_values(c, j, v[:, 2:4, j * T:(j + 1) * T], dve_evac)
                splits(c)
            norm_split(5, 3, x, lambda kk: gain[:, kk, 0:1], lambda kk: mod[:, kk, 0:1])
            run_pass(2, 6)
            norm_split(7, 4, x, lambda kk: col("ffn10", kk))
            ffn(0)
            norm_split(8, 5, x, lambda kk: col("mix0", kk))
            rope_phase(start["qkv0"], 8, pairs_of(q) + pairs_of(k))
            rope_turn(15, pairs_of(k)[3], "cos_b", "sin_b")
            for n in range(8):
                softmax2(0, n, "bias_dilated")
                if n >= 1:
                    take_heads2(0, n - 1)
                if n < 4:
                    c = start["qkv0"] + 16 + 2 * n
                    take_values(c, n % 2, v2[:, :, n * T:(n + 1) * T], qkv_evac)
                    splits(c)
                normalize2(0, n)
                take_turned2(0, n)
            take_heads2(0, 7)
            out_proj("wo0")
            norm_split(9, 6, x, lambda kk: col("ffn20", kk))
            ffn(1)
            norm_split(10, 7, x, lambda kk: col("kv_norm", kk))
            rope_phase(start["kv"], 16, pairs_of(k))
            for j in range(4):
                c = start["kv"] + 8 + 2 * j
                take_values(c, j % 2, v2[:, :, j * T:(j + 1) * T], qkv_evac)
                splits(c)
                if j == 0:
                    rope_turn(19, pairs_of(k)[3], "cos_b", "sin_b")
            norm_split(11, 8, x, lambda kk: col("ffn11", kk))
            ffn(2)
            norm_split(12, 9, x, lambda kk: col("mix1", kk))
            rope_phase(start["q1"], 20, pairs_of(q))
            rope_turn(23, pairs_of(q)[3], "cos_b", "sin_b")
            for n in range(8):
                softmax2(1, n, "bias_causal")
                if n >= 1:
                    take_heads2(1, n - 1)
                normalize2(1, n)
                take_turned2(1, n)
            take_heads2(1, 7)
            out_proj("wo1")
            norm_split(13, 10, x, lambda kk: col("ffn21", kk))
            ffn(3)
            norm_rstd(14)
            for kk in range(KD):
                V.scalar_tensor_tensor(normed[:, kk, :], x[:, kk, :], col("final_norm", kk), rstd, ALU.mult,
                                       ALU.mult).then_inc(out_ready, 1)


OUT_EVENT = [0, 2, 4]


def constants():
    f = np.float32
    t = np.arange(T)
    out = {"ident": np.eye(P)}

    def rotary(width, ang_of, perm_name, cos_name, sin_name):
        cos, sin, perm = np.ones((P, T)), np.zeros((P, T)), np.zeros((P, P))
        for i in range(P):
            found = ang_of(i % width)
            if found is None:
                continue
            ang, first, half = found
            cos[i], sin[i] = np.cos(ang), np.sin(ang)
            if first:
                perm[i + half, i] = -1.0
            else:
                perm[i - half, i] = 1.0
        out[perm_name], out[cos_name], out[sin_name] = perm, cos, sin

    nf = SUB // 4

    def axial(i):
        axis, rest = divmod(i, 2 * nf)
        half, fr = divmod(rest, nf)
        inv = f(10000.0) ** (-np.arange(nf, dtype=f) / f(nf))
        pos = (t // 64 if axis == 0 else t % 64).astype(f)
        return (pos * inv[fr]).astype(f), half == 0, nf

    def partial(i):
        half_dim = HD // 8
        if i >= 2 * half_dim:
            return None
        half, fr = divmod(i, half_dim)
        inv = f(500000.0) ** (-np.arange(half_dim, dtype=f) / f(half_dim))
        return (t.astype(f) * inv[fr]).astype(f), half == 0, half_dim

    rotary(SUB, axial, "perm_a", "cos_a", "sin_a")
    rotary(HD, partial, "perm_b", "cos_b", "sin_b")

    diff = t[:, None] - t[None, :]
    causal = diff >= 0
    count = sum((causal & (diff <= w) & (diff % d == 0)).astype(int) for w, d in ((128, 1), (512, 4), (2048, 16)))
    for name, n in (("bias_dilated", count), ("bias_causal", causal.astype(int))):
        b = np.where(n > 0, np.log(np.maximum(n, 1)), -1e30)
        out[name] = np.concatenate([b[0:P, 0:P], b[P:T, :]], axis=1)

    def tiled(m):
        return m.reshape(-1, P, m.shape[1]).transpose(1, 0, 2).reshape(P, -1)

    w = np.pi * np.outer(t, t) / T
    sign = np.where(t % 2 == 0, 1.0, -1.0)
    out["dft_cos"] = tiled(np.cos(w))
    s = -np.sin(w)
    out["dft_sin_k"] = tiled(s)
    s = s.copy()
    s[:, 0] = sign
    out["dft_sin_u"] = tiled(s)
    ny = np.cos(w)[:, 0:P].copy()
    ny[:, 0] = sign
    out["dft_nyq"] = tiled(ny)
    weight = np.where(t == 0, 1.0, 2.0)[:, None] / (2 * T)
    re, im = weight * np.cos(w), -weight * np.sin(w)
    im[0, :] = sign / (2 * T)
    out["idft"] = tiled(np.concatenate([re, im], axis=0))
    lin = np.linspace(0.0, 1.0, T)
    lo, hi = math.log(1e-2) / 1.5, math.log(1e-2) / 0.3
    out["decay"] = tiled(np.exp(-lin[:, None] * np.abs(np.linspace(lo, hi, BR))[None, :]))
    wpos = (2.0 * math.pi / T) * t[None, :]
    bands = np.linspace(1e-4, 15, 16)[:, None]
    z = np.concatenate([lin[None, :], np.cos(bands * wpos), -np.sin(bands * wpos)], axis=0)
    out["filter_z"] = np.concatenate([z, np.zeros((P - 33, T))], axis=0)
    return np.ascontiguousarray(np.concatenate([out[n].astype(f) for n, _ in CONSTS], axis=1))


def pack(inputs):
    g = {n: np.asarray(a) for n, a in inputs.items()}
    slots = []

    def tiles(w, lo=0, hi=None):
        w = w[:, lo:hi]
        for c in range(0, w.shape[1], P):
            slots.append(w[:, c:c + P].reshape(KD, P, P).transpose(1, 0, 2).reshape(P, SLOT))

    def token(w, lo=0, hi=None):
        w = w[:, lo:hi]
        for c in range(0, w.shape[1], T):
            for r in range(0, D, D // 2):
                slots.append(w[r:r + D // 2, c:c + T].reshape(4, P, T).transpose(1, 0, 2).reshape(P, SLOT))

    for l in range(DEPTH):
        tiles(g["ada_w"][l])
        w = g["w_in"][l]
        tiles(w, 0, 512)
        tiles(w, 1024, 1536)
        token(w, 512, 1024)
        tiles(w, 2048, 3584)
        tiles(w, 4096, 4608)
        token(w, 4608, 5120)
        tiles(w, 1536, 2048)
        tiles(w, 3584, 4096)
        tiles(w, 5120, 5632)
        for c in range(0, D, T):
            for b in range(3):
                slots.append(g["w_branch"][l, b][:, c:c + T].reshape(KB, P, T).transpose(1, 0, 2).reshape(P, SLOT))
                tiles(w, 5632 + b * D + c, 5632 + b * D + c + T)
        tiles(g["w_out"][l])

    def ffn(n, l):
        gate, up, down = (g[f"ffn{n}_w_{x}_2"][l] for x in ("gate", "up", "down"))
        for p in range(FPAIRS + 1):
            if p < FPAIRS:
                tiles(gate, 2 * P * p, 2 * P * (p + 1))
                tiles(up, 2 * P * p, 2 * P * (p + 1))
            if p >= 1:
                for f in (2 * p - 2, 2 * p - 1):
                    slots.append(down[f * P:(f + 1) * P, :])

    ffn(1, 0)
    tiles(g["a_w_qkv_2"][0], 0, 2 * D)
    token(g["a_w_qkv_2"][0], 2 * D, 3 * D)
    tiles(g["a_w_o_2"][0])
    ffn(2, 0)
    tiles(g["kv_w_2"], 0, D)
    token(g["kv_w_2"], D, 2 * D)
    ffn(1, 1)
    tiles(g["b_w_q_2"][0])
    tiles(g["b_w_o_2"][0])
    ffn(2, 1)
    weights = np.stack(slots)

    def column(v):
        return v.reshape(-1, P).T

    def padded(v, rows):
        return np.concatenate([v, np.zeros((rows - v.shape[0], v.shape[1]), v.dtype)], axis=0)

    cols = {"cond": np.stack([column(g["c"][0]), column(g["c_ctx"])], axis=2).reshape(P, 16),
            "kv_norm": column(g["kv_norm_2"]), "final_norm": column(g["final_norm_2"])}
    layers, filters, lams = [], [], []
    for l in range(DEPTH):
        cols[f"norm_pre{l}"] = column(g["norm_pre"][l])
        cols[f"norm_post{l}"] = column(g["norm_post"][l])
        cols[f"ada_b{l}"] = column(g["ada_b"][l])
        cols[f"subln{l}"] = column(g["da_subln"][l])
        cols[f"short_w{l}"] = column(g["hy_short_w"][l].reshape(-1))
        cols[f"short_b{l}"] = column(g["hy_short_b"][l])
        cols[f"conv_bias{l}"] = column(g["hy_bias"][l])
        cols[f"filter_b1{l}"] = padded(g["hy_f_b1"][l][:, None], P)
        cols[f"filter_b2{l}"] = padded(g["hy_f_b2"][l][:, None], P)
        cols[f"freq0{l}"] = padded(g["hy_f_freq"][l, 0][:, None], P)
        cols[f"freq1{l}"] = padded(g["hy_f_freq"][l, 1][:, None], P)
        cols[f"ffn1{l}"] = column(g["ffn1_norm_2"][l])
        cols[f"mix{l}"] = column(g["mix_norm_2"][l])
        cols[f"ffn2{l}"] = column(g["ffn2_norm_2"][l])
        mix_bias = np.repeat(g["gm_bs"][l].reshape(KB, 2, 1, P), SUB, axis=2).reshape(KB, P, P)
        layers.append(np.concatenate([np.broadcast_to(g["gm_ln_g"][l], (P, BR)), np.broadcast_to(g["gm_ln_b"][l], (P, BR)),
                                      mix_bias.transpose(1, 0, 2).reshape(P, -1),
                                      g["gm_ws"][l].transpose(2, 0, 1).reshape(P, -1)], axis=1))
        filters.append(np.concatenate([padded(g["hy_f_w1"][l], 64), g["hy_f_w2"][l], g["hy_f_w3"][l]], axis=1))
        lams.append(np.broadcast_to(g["da_lambda"][l].reshape(-1), (P, 4 * SUB)))

    def stream(a):
        return np.ascontiguousarray(a[0].T.reshape(KD, P, T).transpose(1, 0, 2))

    return {"weights": weights, "x_in": stream(g["x"]), "ctx_in": stream(g["ctx"]),
            "cols_in": np.ascontiguousarray(np.concatenate([cols[n] for n, _ in COLUMNS], axis=1)),
            "consts_in": constants(), "layer_in": np.stack(layers), "filter_in": np.stack(filters),
            "lam_in": np.stack(lams)}


def kernel(**inputs):
    import concourse.bacc as bacc
    from concourse.bass_utils import run_bass_kernel_spmd

    nc = bacc.Bacc("TRN2", target_bir_lowering=False, num_devices=1)
    arrays = pack(inputs)
    aps = {n: nc.dram_tensor(n, a.shape, mybir.dt.from_np(a.dtype), kind="ExternalInput").ap()
           for n, a in arrays.items()}
    out = nc.dram_tensor("out", (P, KD, T), F32, kind="ExternalOutput").ap()
    build(nc, out=out, **aps)
    r = run_bass_kernel_spmd(nc, [arrays], core_ids=[0])
    res = np.asarray(r.results[0]["out"])
    return np.ascontiguousarray(res.transpose(2, 1, 0).reshape(1, T, D))
```

```python
import math
from contextlib import ExitStack

import concourse.bass as bass
import numpy as np
from concourse import mybir

F32 = mybir.dt.float32
F32R = mybir.dt.float32r
ALU = mybir.AluOpType
ACT = mybir.ActivationFunctionType
AX_X = mybir.AxisListType.X

P = 128
T = 256
TT = T // P
D = 1024
KD = D // P
BR = 512
KB = BR // P
DEPTH = 2
FF = 2816
FPAIRS = FF // (2 * P)
HEADS_A, SUB = 4, 64
HEADS_B, HD = 16, 64
SLOT = 1024
RING = 3
SEG = 3 * P
EPS = 1e-6
TWO_PI_HI = 6.28125
TWO_PI_LO = 2 * math.pi - 6.28125
ROUND = 1.5 * 2 ** 23
PI_SAFE = 3.1415925

PASS = [("k", 4), ("q", 4), ("v", 4), ("hy", 12), ("gu", 4), ("gv", 4), ("ga", 4), ("gb", 4),
        ("gc", 4), ("merge", 36), ("wo", 8)]
PASS_SLOTS = sum(n for _, n in PASS)
MERGE_SLOTS = dict(PASS)["merge"]
MERGE_TURN = 3 * (3 + 2)
MERGE_AT = PASS_SLOTS - MERGE_SLOTS - dict(PASS)["wo"]
ADA_SLOTS = 3 * D // P
ADA_TURN = 6
ADA_TURNS = ADA_SLOTS // ADA_TURN
FFN_SLOTS = 3 * FF // P
SCORES, TURN, HEADS_OUT, MISC = 2, 4, 5, 7

COLUMNS = [("cond", 16), ("ada_sum", 2)]
for _l in range(DEPTH):
    COLUMNS += [(f"norm_pre{_l}", KD), (f"norm_post{_l}", KD), (f"ada_b{_l}", 24), (f"subln{_l}", 1),
                (f"short_w{_l}", 36), (f"short_b{_l}", 12), (f"conv_bias{_l}", KB),
                (f"ffn1{_l}", KD), (f"mix{_l}", KD), (f"ffn2{_l}", KD)]
COLUMNS += [("kv_norm", KD), ("final_norm", KD)]
COLUMNS += [("filter_b1", 1), ("filter_b2", 1), ("freq0", 1), ("freq1", 1)]
CONSTS = [("ident", P), ("perm_a", P), ("perm_b", P), ("cos_a", T), ("sin_a", T), ("cos_b", T),
          ("sin_b", T), ("bias_dilated", SEG), ("bias_causal", SEG), ("dft_cos", TT * T),
          ("dft_sin_u", TT * T), ("idft", 4 * T)]
FILTER_CONSTS = [("dft_sin_k", TT * T), ("dft_nyq", TT * P), ("decay", TT * BR), ("filter_z", T)]
LAYER = [("ln_g", BR), ("ln_b", BR), ("mix_bias", KB * P), ("mix_w", 8 * P)]
FILTER = [("w1", 64), ("w2", 64), ("w3", 2 * BR)]


def places(parts):
    out, at = {}, 0
    for name, n in parts:
        out[name] = (at, at + n)
        at += n
    return out, at


def build(nc, weights, x_in, ctx_in, cols_in, consts_in, filter_consts_in, layer_in, filter_in, lam_in, out):
    col_at, ncols = places(COLUMNS)
    const_at, nconsts = places(CONSTS)
    fconst_at, nfconsts = places(FILTER_CONSTS)
    layer_at, nlayer = places(LAYER)
    filter_at, nfilter = places(FILTER)

    start = {}
    stretches = []
    stream_len = 0

    def stretch(name, dram, n):
        nonlocal stream_len
        start[name] = stream_len
        stretches.append((stream_len, dram, n))
        stream_len += n

    dram_pass = [ADA_SLOTS, 2 * ADA_SLOTS + PASS_SLOTS]
    stretch("pass0", dram_pass[0], PASS_SLOTS)
    stretch("pass1", dram_pass[0], MERGE_AT)
    stretch("pass1_merge", None, MERGE_SLOTS + ADA_SLOTS)
    stretch("pass1_wo", dram_pass[0] + MERGE_AT + MERGE_SLOTS, 8)
    stretch("ctx_k", dram_pass[1], 4)
    stretch("ctx_v", dram_pass[1] + 8, 4)
    stretch("pass2", dram_pass[1], PASS_SLOTS)
    dram = dram_pass[1] + PASS_SLOTS
    for p in (0, 2):
        start[f"pass{p}_merge"] = start[f"pass{p}"] + MERGE_AT
        start[f"pass{p}_wo"] = start[f"pass{p}"] + MERGE_AT + MERGE_SLOTS
    tail = [("ffn0", FFN_SLOTS), ("qkv0", 24), ("wo0", 8), ("ffn1", FFN_SLOTS), ("kv", 16),
            ("ffn2", FFN_SLOTS), ("q1", 8), ("wo1", 8), ("ffn3", FFN_SLOTS)]
    for name, n in tail:
        stretch(name, dram, n)
        dram += n
    TOTAL = stream_len
    part = {}
    a = 0
    for name, n in PASS:
        part[name] = a
        a += n

    ctx = ExitStack()
    with ctx:
        def sb(name, shape, dt=F32):
            return ctx.enter_context(nc.sbuf_tensor(name, shape, dt))

        def sem(name):
            return ctx.enter_context(nc.semaphore(name))

        PS = ctx.enter_context(nc.psum_tensor("PS", [P, 8, 512], F32))
        raw = sb("raw", [P, RING, SLOT])
        w_hi = sb("w_hi", [P, RING, SLOT], F32R)
        w_lo = sb("w_lo", [P, RING, SLOT], F32R)
        x = sb("x", [P, KD, T])
        cx = sb("cx", [P, KD, T])
        h_hi = sb("h_hi", [P, KD, T], F32R)
        h_lo = sb("h_lo", [P, KD, T], F32R)
        g_hi = sb("g_hi", [P, 12, T], F32R)
        g_lo = sb("g_lo", [P, 12, T], F32R)
        q = sb("q", [P, KD, T])
        k = sb("k", [P, KD, T])
        v = sb("v", [P, 4, BR])
        v2 = v[:, :, :].rearrange("p (t a) c -> p t (a c)", a=2)
        cols = sb("cols", [P, ncols])
        consts = sb("consts", [P, nconsts])
        layer = sb("layer", [P, nlayer])
        spec_re = sb("spec_re", [P, DEPTH, 2, BR])
        spec_im = sb("spec_im", [P, DEPTH, 2, BR])
        spec_ny = sb("spec_ny", [P, DEPTH, BR])
        ones = sb("ones", [P, P])
        zeros = sb("zeros", [P, P], mybir.dt.bfloat16)
        eps = sb("eps", [P, 1])
        c_parts = sb("c_parts", [P, KD, 4], F32R)
        c_act = sb("c_act", [P, 16])
        mod_raw = sb("mod_raw", [P, 48])
        mod = sb("mod", [P, DEPTH, 24, 2])
        gain = sb("gain", [P, DEPTH, KD, 2])
        gate = sb("gate", [P, DEPTH, KD, 2])
        stat = sb("stat", [P, 88])
        arena = sb("arena", [P, 10752])

        def col(name, j=0, n=1):
            a = col_at[name][0] + j
            return cols[:, a:a + n]

        def const(name):
            a, b = const_at[name]
            return consts[:, a:b]

        def row(name):
            a, b = layer_at[name]
            return layer[:, a:b]

        def scratch(a, n, **kw):
            return arena[:, a:a + n]

        sq = scratch(0, 2048).rearrange("p (k t) -> p k t", k=KD)
        sq_behind = scratch(7680, 2048).rearrange("p (k t) -> p k t", k=KD)
        normed = scratch(2048, 2048).rearrange("p (k t) -> p k t", k=KD)
        rt = scratch(10240, 256)
        rstd = scratch(10496, 256)
        branch_out = scratch(4608, 2048).rearrange("p (k t) -> p k t", k=KD)
        merged = scratch(0, 2048).rearrange("p (k t) -> p k t", k=KD)
        sel = scratch(2048, 1536).rearrange("p (i n) -> p i n", i=3)
        term = scratch(3584, 512)
        rope_raw = scratch(0, 1024).rearrange("p (b n) -> p b n", b=2)
        rope_a = scratch(1024, 512)
        rope_b = scratch(1536, 512)
        probs = scratch(2048, 1024).rearrange("p (m n) -> p m n", m=2)
        mixw = scratch(3072, 512)
        mixw_t = scratch(3584, 2048).rearrange("p (b k t) -> p b k t", b=2, k=4)
        head_y = scratch(5632, 1024).rearrange("p (h q d) -> p h q d", h=4, q=2)
        y = scratch(6656, 1024).rearrange("p (k t) -> p k t", k=KB)
        squared = scratch(6656, 1024).rearrange("p (n d) -> p n d", n=8)
        hy = scratch(7680, 3072).rearrange("p (k t) -> p k t", k=12)
        u = hy[:, 4:8, :]
        gu = scratch(0, 1024).rearrange("p (k t) -> p k t", k=KB)
        gv = scratch(1024, 1024).rearrange("p (t c) -> p t c", t=TT)
        gvc = scratch(2048, 1024).rearrange("p (t c) -> p t c", t=TT)
        lnv = scratch(3584, 1024).rearrange("p (t c) -> p t c", t=TT)
        gate_act = scratch(4608, 1024).rearrange("p (b n) -> p b n", b=2)
        gated = scratch(5632, 1024).rearrange("p (b k t) -> p b k t", b=2, k=2)
        u_tok = v[:, 0:2, :]
        prod = k[:, 0:4, :].rearrange("p (a k) t -> p a (k t)", a=2)
        yspec = q[:, :, :].rearrange("p (a k) t -> p a (k t)", a=4)
        hw = q[:, :, :].rearrange("p (d t a) c -> p d t (a c)", d=2, t=TT)
        h_sum = k[:, 0:4, :].rearrange("p (t a) c -> p t (a c)", t=TT)
        h_dif = k[:, 4:8, :].rearrange("p (t a) c -> p t (a c)", t=TT)
        h_sq = v[:, :, :].rearrange("p (d t) c -> p d t c", d=2)
        fil = scratch(0, nfilter)
        arg = scratch(2304, T)
        turns = scratch(2816, T)
        hid1 = scratch(3328, T)
        hid2 = scratch(3840, T)
        lam_rows = scratch(4608, 512).rearrange("p (l n) -> p l n", l=DEPTH)
        fconsts = scratch(5120, nfconsts)
        conv_rt = scratch(7168, BR)
        conv_rs = conv_rt
        ada_rows = scratch(9728, 3 * T)
        ada_raw = [raw[:, 0, :], raw[:, 1, :], raw[:, 2, :], scratch(8192, SLOT)]
        ada_raw += [x[:, 4 * j:4 * j + 4, :].rearrange("p k t -> p (k t)") for j in range(2)]
        silu = scratch(4608, 1024).rearrange("p (b n) -> p b n", b=2)
        act_f = scratch(5632, 512)
        act_hi = g_hi[:, 0:4, :].rearrange("p (b f) t -> p b f t", b=2)
        act_lo = g_lo[:, 0:4, :].rearrange("p (b f) t -> p b f t", b=2)
        biased = scratch(2048, 4 * SEG).rearrange("p (b h n) -> p b h n", b=2, h=2)
        probs2 = scratch(3584, 4 * SEG).rearrange("p (b h n) -> p b h n", b=2, h=2)
        probs2_t = scratch(5120, 4 * SEG).rearrange("p (b h n) -> p b h n", b=2, h=2)

        def filt(l, name):
            a, b = filter_at[name]
            return fil[64 * l:64 * l + 64, a:b]

        def fconst(name):
            a, b = fconst_at[name]
            return fconsts[:, a:b]

        neg_max = stat[:, 0:8]
        mx = stat[:, 8:16]
        den = stat[:, 16:24]
        rden = stat[:, 24:32]
        head_ss = stat[:, 32:40]
        head_rt = stat[:, 40:48]
        head_rs = stat[:, 48:56]
        ln_sum = stat[:, 64:66]
        ln_ss = stat[:, 66:68]
        ln_rt = stat[:, 68:70]
        ln_rs = stat[:, 70:72]
        dots = stat[:, 72:74]
        dot_exp = stat[:, 74:76]
        lam = stat[:, 76:77]
        wden = stat[:, 80:82]
        signal = stat[:, 82:83]
        by_layer = stat[:, 84:88].rearrange("p (l n) -> p l n", l=DEPTH)
        neg_lam = by_layer[:, :, 0:1]
        subln_g = by_layer[:, :, 1:2]

        ada_loaded = [sem(f"ada_loaded{j}") for j in range(ADA_TURN)]
        ada_used = sem("ada_used")
        raw_loaded = [sem(f"raw_loaded{r}") for r in range(RING)]
        w_hi_ready = sem("w_hi_ready")
        w_lo_ready = sem("w_lo_ready")
        w_used = sem("w_used")
        consts_loaded = sem("consts_loaded")
        x_loaded = sem("x_loaded")
        ctx_loaded = sem("ctx_loaded")
        layer_loaded = sem("layer_loaded")
        filter_loaded = sem("filter_loaded")
        lam_loaded = sem("lam_loaded")
        ones_ready = sem("ones_ready")
        dve_chain = sem("dve_chain")
        act_chain = sem("act_chain")
        cond_act = sem("cond_act")
        cond_hi = sem("cond_hi")
        cond_ready = sem("cond_ready")
        ada_rows_ready = sem("ada_rows_ready")
        ada_turned = sem("ada_turned")
        ada_taken = sem("ada_taken")
        fil_mm = sem("fil_mm")
        fil_arg = sem("fil_arg")
        fil_sin = sem("fil_sin")
        fil_h = sem("fil_h")
        fil_sq = sem("fil_sq")
        fil_rt = sem("fil_rt")
        fil_taken = sem("fil_taken")
        cols_loaded = sem("cols_loaded")
        lam_dots = sem("lam_dots")
        lam_exp = sem("lam_exp")
        src_ready = sem("src_ready")
        sq_ready = sem("sq_ready")
        ms_ready = sem("ms_ready")
        rt_ready = sem("rt_ready")
        norm_v = sem("norm_v")
        norm_hi = sem("norm_hi")
        norm_lo = sem("norm_lo")
        dve_evac = sem("dve_evac")
        act_evac = sem("act_evac")
        tap_ready = sem("tap_ready")
        rope_in = sem("rope_in")
        rope_rot = sem("rope_rot")
        rope_out = sem("rope_out")
        sc_done = sem("sc_done")
        nm_ready = sem("nm_ready")
        p_ready = sem("p_ready")
        mixw_ready = sem("mixw_ready")
        turned = sem("turned")
        mixw_t_ready = sem("mixw_t_ready")
        pv_done = sem("pv_done")
        head_sq = sem("head_sq")
        head_rt_ready = sem("head_rt_ready")
        head_y_ready = sem("head_y_ready")
        head_t = sem("head_t")
        u_ready = sem("u_ready")
        u_t = sem("u_t")
        u_tok_ready = sem("u_tok_ready")
        dft_done = sem("dft_done")
        yspec_ready = sem("yspec_ready")
        conv_done = sem("conv_done")
        ln_centered = sem("ln_centered")
        ln_rt_ready = sem("ln_rt_ready")
        lnv_ready = sem("lnv_ready")
        mixed = sem("mixed")
        gated_ready = sem("gated_ready")
        merge_free = sem("merge_free")
        merge_added = sem("merge_added")
        sel_ready = sem("sel_ready")
        m_hi = sem("m_hi")
        m_lo = sem("m_lo")
        gu_free = sem("gu_free")
        silu_ready = sem("silu_ready")
        act_raw = sem("act_raw")
        act_hi_ready = sem("act_hi_ready")
        act_ready = sem("act_ready")
        sc2_done = sem("sc2_done")
        nm2_ready = sem("nm2_ready")
        biased_ready = sem("biased_ready")
        p2_ready = sem("p2_ready")
        p2n_ready = sem("p2n_ready")
        turned2 = sem("turned2")
        p2t_ready = sem("p2t_ready")
        pv2_done = sem("pv2_done")
        o2_hi = sem("o2_hi")
        o2_ready = sem("o2_ready")
        qkv_evac = sem("qkv_evac")
        y_ready = sem("y_ready")
        out_ready = sem("out_ready")
        out_stored = sem("out_stored")

        block = ctx.enter_context(nc.Block())

        def at(value, i, per):
            return value if i is None else i * per + value

        def f32(ap):
            return ap.bitcast(F32)

        LAYER_OF = [0, 0, 1]
        ON_CTX = [True, False, False]

        def key_tiles(p):
            return [2, 3] if ON_CTX[p] else [0, 1, 2, 3]

        def sources(p):
            return cx if ON_CTX[p] else x

        ROPE_BASE = [0, 0, 4]
        TAKEN_BASE = [0, 12, 24]
        CTX_TAKEN = 20

        def taken(p, j):
            if ON_CTX[p]:
                return dve_evac, TAKEN_BASE[p] + j + 1
            if j < 4:
                return rope_in, ROPE_BASE[p] + j + 1
            return dve_evac, TAKEN_BASE[p] + j - 4 + 1

        def act_pairs(p, j):
            return 10 * p + j + 1

        def NORM_BANK(nid):
            return 0 if nid == 0 else 2

        def normed_of(nid_lo):
            return sq_behind if nid_lo == 0 else normed

        def squares_of(nid):
            return sq_behind if nid in (0, 1) else sq

        @block.sync
        def _(sp):
            for turn in range(ADA_TURNS):
                for j in range(ADA_TURN):
                    n = turn * ADA_TURN + j
                    if turn >= 1:
                        sp.wait_ge(ada_used, n - ADA_TURN + 1)
                    sp.dma_start(ada_raw[j], weights[n]).then_inc(ada_loaded[j], 16)

            def load(n, d, i=None, per=RING, dper=RING):
                r = n % RING
                if i is not None:
                    src = weights[bass.ds(i * dper + d, 1)].rearrange("o p n -> (o p) n")
                    sp.wait_ge(w_lo_ready, i * per + (n - RING + 1))
                else:
                    src = weights[d]
                    if n >= RING:
                        sp.wait_ge(w_lo_ready, n - RING + 1)
                    else:
                        sp.wait_ge(ada_used, ADA_SLOTS - ADA_TURN + n + 1)
                sp.dma_start(raw[:, r, :], src).then_inc(raw_loaded[r], 16)

            for n0, d0, count in stretches:
                if d0 is None:
                    dm, da = dram_pass[0] + MERGE_AT, dram_pass[1] - ADA_SLOTS
                    with sp.Fori(0, 4) as i:
                        for b in range(3):
                            for j in range(2):
                                load(n0 + 5 * b + j, da + 2 * b + j, i, 15, ADA_TURN)
                            for j in range(3):
                                load(n0 + 5 * b + 2 + j, dm + 3 * b + j, i, 15, 9)
                    continue
                first = RING if n0 == 0 else 0
                for j in range(first):
                    load(n0 + j, d0 + j)
                turns_ = (count - first) // RING
                if turns_ > 1:
                    with sp.Fori(0, turns_) as i:
                        for j in range(RING):
                            load(n0 + first + j, d0 + first + j, i)
                    first += turns_ * RING
                for j in range(first, count):
                    load(n0 + j, d0 + j)

        @block.gpsimd
        def _(pool):
            pool.dma_start(cols[:, :], cols_in).then_inc(cols_loaded, 16)
            pool.dma_start(fil, filter_in).then_inc(filter_loaded, 16)
            pool.dma_start(fconsts, filter_consts_in).then_inc(filter_loaded, 16)
            pool.wait_ge(ada_used, ADA_TURN)
            pool.dma_start(consts[:, :], consts_in).then_inc(consts_loaded, 16)
            for l in range(DEPTH):
                pool.dma_start(lam_rows[:, l, :], lam_in[l]).then_inc(lam_loaded, 16)
            pool.wait_ge(ada_used, 2 * ADA_TURN)
            pool.dma_start(cx[:, :, :], ctx_in).then_inc(ctx_loaded, 16)
            pool.wait_ge(ada_used, ADA_SLOTS)
            pool.dma_start(x[:, :, :], x_in).then_inc(x_loaded, 16)
            pool.dma_start(layer[:, :], layer_in[0]).then_inc(layer_loaded, 16)
            pool.wait_ge(src_ready, 16)
            pool.dma_start(layer[:, :], layer_in[1]).then_inc(layer_loaded, 16)
            pool.wait_ge(out_ready, KD)
            pool.dma_start(out, normed).then_inc(out_stored, 16)
            pool.wait_ge(out_stored, 16)

        @block.tensor
        def _(pe):
            def mm3(dst, hi, lo, m_hi_, m_lo_, first, last, **kw):
                pe.matmul(dst, hi, m_hi_, start=first, stop=False, **kw)
                pe.matmul(dst, hi, m_lo_, start=False, stop=False, **kw)
                return pe.matmul(dst, lo, m_hi_, start=False, stop=last, **kw)

            def slot_ready(c, i, per):
                pe.wait_ge(w_lo_ready, at(c + 1, i, per))

            def project(c, dst, i=None, per=0, tiles=None, hi=h_hi, lo=h_lo, nk=KD):
                slot_ready(c, i, per)
                r = c % RING
                for kk in range(nk):
                    if tiles is not None:
                        pe.wait_ge(*tiles(kk))
                    w = slice(kk * P, kk * P + P)
                    mm = mm3(dst, w_hi[:, r, w], w_lo[:, r, w], hi[:, kk, :], lo[:, kk, :],
                             kk == 0, kk == nk - 1)
                mm.then_inc(w_used, 1)

            def pair(c, bank, i=None, per=0, tiles=None, hi=h_hi, lo=h_lo):
                project(c, PS[:, bank, 0:T], i, per, tiles, hi, lo)
                project(c + 1, PS[:, bank, T:2 * T], i, per, None, hi, lo)

            def token_pair(c, bank, hi=h_hi, lo=h_lo):
                for half in range(2):
                    slot_ready(c + half, None, 0)
                    r = (c + half) % RING
                    for t in range(TT):
                        tok = slice(t * P, t * P + P)
                        for j in range(4):
                            kk, w = 4 * half + j, slice(j * T, (j + 1) * T)
                            mm = mm3(PS[:, bank, t * T:(t + 1) * T], hi[:, kk, tok], lo[:, kk, tok], w_hi[:, r, w], w_lo[:, r, w],
                                     kk == 0 and t == 0, kk == KD - 1, skip_group_check=True)
                    mm.then_inc(w_used, 1)

            def norm(nid):
                bank = NORM_BANK(nid)
                for c in range(4):
                    pe.wait_ge(sq_ready, 4 * MS_ORDER.index(nid) + c + 1)
                    for kk in (2 * c, 2 * c + 1):
                        mm = pe.matmul(PS[:, bank, 0:T], ones[:, :], squares_of(nid)[:, kk, :], start=(kk == 0),
                                       stop=(kk == KD - 1))
                mm.then_inc(ms_ready, 1)

            def normed_tiles(nid_lo):
                return lambda kk: (norm_lo, KD * nid_lo + kk + 1)

            def ada(c, turn, m, banks, i=None):
                per = 0 if i is None else MERGE_TURN
                if m == 1 and turn > 0:
                    pe.wait_ge(ada_taken, at(turn, i, 1))
                if m == 2:
                    pe.wait_ge(ada_rows_ready, at(3 * turn + 1, i, 3))
                dst = PS[0:4, banks[m % 2], 0:T]
                for half in range(2):
                    slot_ready(c + half, i, per)
                    r = (c + half) % RING
                    for j in range(4):
                        kk, w = 4 * half + j, slice(j * T, (j + 1) * T)
                        pe.matmul(dst, c_parts[:, kk, :], w_hi[:, r, w], start=(kk == 0), stop=False)
                        mm = pe.matmul(dst, c_parts[:, kk, :], w_lo[:, r, w], start=False, stop=(kk == KD - 1))
                    mm.then_inc(w_used, 1)

            def ada_turn(turn, bank, i=None):
                rows = 2 if i is None else 4
                pe.wait_ge(ada_rows_ready, at(3 * turn + 3, i, 3))
                for j in range(6):
                    mm = pe.matmul(PS[:, bank, 2 * j:2 * j + 2], ada_rows[0:rows, j * P:(j + 1) * P],
                                   col("ada_sum", 0, 2)[0:rows, :],
                                   start=True, stop=True)
                mm.then_inc(ada_turned, 1)

            def modulation(turn):
                for m in range(3):
                    if m == 1 and turn > 0:
                        pe.wait_ge(ada_taken, turn)
                    if m == 2:
                        pe.wait_ge(ada_rows_ready, 3 * turn + 1)
                    for half in range(2):
                        pe.wait_ge(ada_loaded[2 * m + half], 16 * (turn + 1))
                        for j in range(4):
                            kk = 4 * half + j
                            mm = pe.matmul(PS[0:2, m % 2, 0:T], c_act[:, 2 * kk:2 * kk + 2],
                                           ada_raw[2 * m + half][:, j * T:(j + 1) * T], start=(kk == 0), stop=(kk == KD - 1))
                        mm.then_inc(ada_used, 1)

            def filter_hidden(n):
                for l in range(DEPTH):
                    rows = slice(64 * l, 64 * l + 64)
                    if n == 0:
                        lhs, rhs = filt(l, "w1"), fconst("filter_z")[rows, :]
                    else:
                        pe.wait_ge(fil_sin, 1)
                        lhs, rhs = filt(l, "w2"), hid1[rows, :]
                    mm = pe.matmul(PS[rows, 2 + n, 0:T], lhs, rhs, start=True, stop=True)
                mm.then_inc(fil_mm, 1)

            def filter_taps(l):
                pe.wait_ge(fil_sin, 2)
                if l == 1:
                    pe.wait_ge(fil_taken, 1)
                for d in range(2):
                    for t in range(TT):
                        mm = pe.matmul(PS[:, 4 + 2 * d + t, :], hid2[64 * l:64 * l + 64, t * P:(t + 1) * P],
                                       filt(l, "w3")[:, d * BR:(d + 1) * BR], start=True, stop=True)
                mm.then_inc(fil_mm, 1)

            def filter_energy(l):
                pe.wait_ge(fil_sq, l + 1)
                for n, (d, t) in enumerate([(0, 0), (0, 1), (1, 0), (1, 1)]):
                    mm = pe.matmul(PS[:, 2, :], ones[:, :], h_sq[:, d, t, :], start=(n == 0), stop=(n == 3))
                mm.then_inc(fil_mm, 1)

            def filter_spectrum(l):
                pe.wait_ge(fil_h, l + 1)
                dft_c = const("dft_cos").rearrange("p (t f) -> p t f", t=TT)
                dft_s = fconst("dft_sin_k").rearrange("p (t f) -> p t f", t=TT)
                dft_n = fconst("dft_nyq").rearrange("p (t f) -> p t f", t=TT)
                for f in range(2):
                    for t in range(TT):
                        pe.matmul(PS[:, 4 + f, :], dft_c[:, t, f * P:(f + 1) * P], h_sum[:, t, :],
                                  start=(t == 0), stop=(t == 1))
                for f in range(2):
                    for t in range(TT):
                        pe.matmul(PS[:, 6 + f, :], dft_s[:, t, f * P:(f + 1) * P], h_dif[:, t, :],
                                  start=(t == 0), stop=(t == 1))
                for t in range(TT):
                    mm = pe.matmul(PS[:, 3, :], dft_n[:, t, :], h_sum[:, t, :], start=(t == 0), stop=(t == 1))
                mm.then_inc(fil_mm, 1)

            def rotate(n, perm):
                pe.wait_ge(rope_in, n + 1)
                if n >= 1:
                    pe.wait_ge(rope_out, n)
                pe.matmul(PS[:, MISC, :], const(perm), rope_raw[:, n % 2, :], start=True,
                          stop=True).then_inc(rope_rot, 1)

            def scores(p, n):
                h, qt = n // 2, n % 2
                if n >= 1:
                    pe.wait_ge(p_ready, 8 * p + n)
                kt = key_tiles(p)
                for m in range(2):
                    s = slice(SUB * m, SUB * m + SUB)
                    for g in range(len(kt) // 2):
                        base = 0 if kt[2 * g] == 0 else 4
                        mm = pe.matmul(PS[:, SCORES + m, g * T:(g + 1) * T], q[s, h, qt * P:(qt + 1) * P],
                                       k[s, base + h, :], start=True, stop=True)
                mm.then_inc(sc_done, 1)

            def turn(p, n):
                pe.wait_ge(mixw_ready, 8 * p + n + 1)
                if n >= 1:
                    pe.wait_ge(mixw_t_ready, 8 * p + n)
                for j in range(len(key_tiles(p))):
                    mm = pe.transpose(PS[:, TURN, j * P:(j + 1) * P], mixw[:, j * P:(j + 1) * P], const("ident"))
                mm.then_inc(turned, 1)

            def values(p, n):
                h, qt = n // 2, n % 2
                pe.wait_ge(mixw_t_ready, 8 * p + n + 1)
                if n == 0:
                    pe.wait_ge(*taken(p, 5))
                kt = key_tiles(p)
                for j, t in enumerate(kt):
                    mm = pe.matmul(PS[:, HEADS_OUT + qt, h * P:(h + 1) * P], mixw_t[:, h % 2, j, qt * P:(qt + 1) * P],
                                   v[:, t, h * P:(h + 1) * P], start=(j == 0), stop=(j == len(kt) - 1))
                mm.then_inc(pv_done, 1)

            def keys_queries(p, nid_lo, behind_second=None):
                c0 = start[f"pass{p}"]
                on_x = not ON_CTX[p]
                rb = ROPE_BASE[p]
                for j in range(4):
                    if j >= 2:
                        pe.wait_ge(*taken(p, j - 2))
                    pair(c0 + 2 * j, j % 2, tiles=normed_tiles(nid_lo) if j == 0 else None)
                    if on_x and j >= 1:
                        rotate(rb + j - 1, "perm_a")
                    if j == 1 and behind_second is not None:
                        norm(behind_second)
                pe.wait_ge(*taken(p, 2))
                token_pair(c0 + part["v"], 0)
                if on_x:
                    rotate(rb + 3, "perm_a")

            def run_pass(p):
                c0 = start[f"pass{p}"]
                on_x = not ON_CTX[p]
                rb = ROPE_BASE[p]
                for n in range(8):
                    if n == 0:
                        if on_x:
                            pe.wait_ge(rope_out, rb + 4)
                        else:
                            pe.wait_ge(*taken(p, 3))
                    scores(p, n)
                    j = 5 + n
                    pe.wait_ge(*taken(p, j - 2))
                    if j == 5:
                        token_pair(c0 + part["v"] + 2, 1)
                    else:
                        project(c0 + 2 * j, PS[:, j % 2, 0:T])
                        values(p, n - 1)
                        project(c0 + 2 * j + 1, PS[:, j % 2, T:2 * T])
                    turn(p, n)
                pe.wait_ge(*taken(p, 11))
                pair(c0 + part["gu"] + 2, 1)
                values(p, 7)
                pe.wait_ge(u_ready, p + 1)
                for t in range(TT):
                    for c in range(KB):
                        mm = pe.transpose(PS[:, [TURN, MISC][t], c * P:(c + 1) * P], u[:, c, t * P:(t + 1) * P],
                                          const("ident"))
                mm.then_inc(u_t, 1)
                pe.wait_ge(p_ready, 8 * (p + 1))
                token_pair(c0 + part["gv"], 2)
                pe.wait_ge(u_tok_ready, p + 1)
                pe.wait_ge(act_evac, act_pairs(p, 1))
                pe.wait_ge(head_y_ready, p + 1)
                for n, name in enumerate(("dft_cos", "dft_sin_u")):
                    dft = const(name).rearrange("p (t f) -> p t f", t=TT)
                    for f in range(2):
                        for t in range(TT):
                            mm = pe.matmul(PS[:, [0, HEADS_OUT][n] + f, :], dft[:, t, f * P:(f + 1) * P],
                                           u_tok[:, t, :], start=(t == 0), stop=(t == 1))
                mm.then_inc(dft_done, 1)
                token_pair(c0 + part["gv"] + 2, 3)
                for h in range(HEADS_A):
                    for qt in range(TT):
                        mm = pe.transpose(PS[:, [TURN, MISC][h // 2], (h % 2) * T + qt * P:(h % 2) * T + (qt + 1) * P],
                                          head_y[:, h, qt, :], const("ident"))
                mm.then_inc(head_t, 1)
                for j in range(2):
                    pe.wait_ge(act_evac, act_pairs(p, 2 + j))
                    pair(c0 + part["ga"] + 2 * j, 2 + j)
                pe.wait_ge(yspec_ready, p + 1)
                pe.wait_ge(y_ready, p + 1)
                idft = const("idft").rearrange("p (a t) -> p a t", a=4)
                for c in range(KB):
                    for a_ in range(4):
                        mm = pe.matmul(PS[:, [TURN, MISC][c // 2], (c % 2) * T:(c % 2 + 1) * T],
                                       yspec[:, a_, c * P:(c + 1) * P], idft[:, a_, :], start=(a_ == 0), stop=(a_ == 3))
                mm.then_inc(conv_done, 1)
                for j in range(2):
                    pair(c0 + part["gb"] + 2 * j, j)
                pe.wait_ge(lnv_ready, p + 1)
                pe.wait_ge(layer_loaded, 16 * (LAYER_OF[p] + 1))
                pe.wait_ge(act_evac, act_pairs(p, 5))
                mixw_g = row("mix_w").rearrange("p (g t) -> p g t", g=8)
                for g in range(8):
                    for c in range(TT):
                        o = SUB * (g % 2)
                        f = (g // 2) * T + c * P
                        mm = pe.matmul(PS[o:o + SUB, SCORES + f // 512, f % 512:f % 512 + P],
                                       lnv[:, c, g * SUB:(g + 1) * SUB], mixw_g[:, g, :], start=True, stop=True)
                mm.then_inc(mixed, 1)
                for j in range(2):
                    pe.wait_ge(act_evac, act_pairs(p, 6 + j))
                    pair(c0 + part["gc"] + 2 * j, j)
                pe.wait_ge(act_evac, act_pairs(p, 9))
                each, per, ahead = (5, MERGE_TURN, 2) if p == 1 else (3, 9, 0)
                with pe.Fori(0, 4) as i:
                    for b in range(3):
                        c = start[f"pass{p}_merge"] + each * b + ahead
                        if p == 1:
                            ada(c - ahead, ADA_TURNS, b, (6, 7), i)
                        pe.wait_ge(merge_free, i * 3 + (15 * p + b + 1))
                        slot_ready(c, i, per)
                        r = c % RING
                        for o in range(2):
                            for kk in range(KB):
                                w = slice(kk * T + o * P, kk * T + (o + 1) * P)
                                mm = mm3(PS[:, 2 * b, o * T:(o + 1) * T], w_hi[:, r, w], w_lo[:, r, w],
                                         g_hi[:, KB * b + kk, :], g_lo[:, KB * b + kk, :], kk == 0, kk == KB - 1)
                        mm.then_inc(w_used, 1)
                        pair(c + 1, 2 * b + 1, i, per)
                    if p == 1:
                        ada_turn(ADA_TURNS, 7, i)

            def branch_sum(p, j):
                if j >= 2:
                    pe.wait_ge(src_ready, 4 * OUT_EVENT[p] + j - 1)
                pair(start[f"pass{p}_wo"] + 2 * j, 4 + j % 2,
                     tiles=(lambda kk: (m_lo, KD * p + kk + 1)) if j == 0 else None)

            def ctx_keys(nid_lo):
                for j in range(2):
                    pair(start["ctx_k"] + 2 * j, j, tiles=normed_tiles(nid_lo) if j == 0 else None, hi=g_hi, lo=g_lo)

            def ctx_values():
                for j in range(2):
                    pe.wait_ge(dve_evac, CTX_TAKEN + j + 1)
                    token_pair(start["ctx_v"] + 2 * j, j, g_hi, g_lo)

            def down(c, s, f, i, per, last):
                slot_ready(c, i, per)
                r = c % RING
                for o in range(KD):
                    w = slice(o * P, o * P + P)
                    mm = mm3(PS[:, 4 + o // 2, (o % 2) * T:(o % 2 + 1) * T], w_hi[:, r, w], w_lo[:, r, w],
                             act_hi[:, s, f, :], act_lo[:, s, f, :], False, last, skip_group_check=True)
                mm.then_inc(w_used, 1)

            def ffn(n, nid_lo):
                c0 = start[f"ffn{n}"]
                for b in range(4):
                    pe.matmul(PS[:, 4 + b, :], zeros[:, :], zeros[:, 0:1].to_broadcast([P, 512]), start=True, stop=False,
                              skip_group_check=True)

                def gate_up(c, s, i, base, tiles=None):
                    pe.wait_ge(gu_free, base if i is None else i * 2 + base)
                    pair(c, 2 * s, i, 12, tiles)
                    pair(c + 2, 2 * s + 1, i, 12)

                def downs(c, s, i, base, last=False):
                    pe.wait_ge(act_ready, base if i is None else i * 2 + base)
                    for f in range(2):
                        down(c + f, s, f, i, 12, last)

                g, a_ = 13 * n, FPAIRS * n
                gate_up(c0, 0, None, g + 1, normed_tiles(nid_lo))
                with pe.Fori(0, 4) as i:
                    for e in range(2):
                        c = c0 + 4 + 6 * e
                        gate_up(c, (1 + e) % 2, i, g + 2 + e)
                        downs(c + 4, e % 2, i, a_ + 1 + e)
                for pr in (9, 10):
                    c = c0 + 4 + 6 * (pr - 1)
                    gate_up(c, pr % 2, None, g + pr + 1)
                    downs(c + 4, (pr - 1) % 2, None, a_ + pr)
                downs(c0 + FFN_SLOTS - 2, 10 % 2, None, a_ + 11, True)

            def scores2(n, unit):
                if unit >= 2:
                    pe.wait_ge(biased_ready, 8 * n + unit - 1)
                for h in range(2):
                    s = slice(HD * h, HD * h + HD)
                    bank = SCORES - 2 * (unit % 2) + h
                    pe.matmul(PS[:, bank, 0:P], q[s, unit, 0:P], k[s, unit, 0:P], start=True, stop=True)
                    mm = pe.matmul(PS[:, bank, P:SEG], q[s, unit, P:T], k[s, unit, :], start=True, stop=True)
                mm.then_inc(sc2_done, 1)

            def turn2(n, unit):
                pe.wait_ge(p2n_ready, 8 * n + unit + 1)
                if unit >= 1 or n >= 1:
                    pe.wait_ge(p2t_ready, 8 * n + unit)
                for h in range(2):
                    for j in range(3):
                        mm = pe.transpose(PS[:, TURN + h, j * P:(j + 1) * P], probs2[:, unit % 2, h, j * P:(j + 1) * P],
                                          const("ident"))
                mm.then_inc(turned2, 1)

            def values2(n, unit):
                pe.wait_ge(p2t_ready, 8 * n + unit + 1)
                if unit >= 1 or n >= 1:
                    pe.wait_ge(o2_ready, 8 * n + unit)
                for h in range(2):
                    o, c = HD * h, unit * P + HD * h
                    pe.matmul(PS[o:o + HD, 6, 0:T], v2[:, 0, c:c + HD], probs2_t[:, unit % 2, h, 0:T],
                              start=True, stop=False)
                    mm = pe.matmul(PS[o:o + HD, 6, P:T], v2[:, 1, c:c + HD], probs2_t[:, unit % 2, h, T:SEG],
                                   start=False, stop=True)
                mm.then_inc(pv2_done, 1)

            def attention2(n):
                scores2(n, 0)
                scores2(n, 1)
                for unit in range(8):
                    turn2(n, unit)
                    if unit + 2 < 8:
                        scores2(n, unit + 2)
                    values2(n, unit)

            def projected(c0, n0, npairs, nid_lo):
                for j in range(npairs):
                    if j >= 2:
                        pe.wait_ge(rope_in, n0 + j - 1)
                    pair(c0 + 2 * j, j % 2, tiles=normed_tiles(nid_lo) if j == 0 else None)
                    if j >= 1:
                        rotate(n0 + j - 1, "perm_b")

            def values_projected(c0, n0, taken_):
                for j in range(4):
                    if j < 2:
                        pe.wait_ge(rope_in, n0 + j)
                    else:
                        pe.wait_ge(qkv_evac, taken_ + j - 1)
                    token_pair(c0 + 2 * j, j % 2)
                    if j == 0:
                        rotate(n0, "perm_b")

            def out_proj(n, event, name):
                c0 = start[name]
                for j in range(4):
                    if j >= 2:
                        pe.wait_ge(src_ready, 4 * event + j - 1)
                    pair(c0 + 2 * j, 4 + j % 2, hi=g_hi, lo=g_lo,
                         tiles=(lambda kk: (o2_ready, 8 * n + kk + 1)) if j == 0 else None)

            pe.wait_ge(ones_ready, 1)
            pe.wait_ge(cond_ready, 1)
            modulation(0)
            pe.wait_ge(filter_loaded, 32)
            filter_hidden(0)
            ada_turn(0, 1)
            modulation(1)
            filter_hidden(1)
            ada_turn(1, 1)
            modulation(2)
            filter_taps(0)
            ada_turn(2, 1)
            modulation(3)
            pe.wait_ge(consts_loaded, 16)
            filter_energy(0)
            filter_spectrum(0)
            ada_turn(3, 1)
            norm(0)
            filter_taps(1)
            filter_energy(1)
            filter_spectrum(1)
            keys_queries(0, 0)
            run_pass(0)
            branch_sum(0, 0)
            norm(2)
            for j in range(1, 4):
                branch_sum(0, j)
            keys_queries(1, 1, behind_second=1)
            run_pass(1)
            branch_sum(1, 0)
            norm(4)
            for j in range(1, 4):
                branch_sum(1, j)
            ctx_keys(2)
            norm(3)
            ctx_values()
            norm(5)
            keys_queries(2, 3)
            run_pass(2)
            for j in range(4):
                branch_sum(2, j)
            norm(6)
            norm(7)
            ffn(0, 4)
            norm(8)
            projected(start["qkv0"], 8, 8, 5)
            values_projected(start["qkv0"] + 16, 15, 0)
            pe.wait_ge(rope_out, 16)
            pe.wait_ge(qkv_evac, 4)
            attention2(0)
            out_proj(0, 7, "wo0")
            norm(9)
            ffn(1, 6)
            norm(10)
            projected(start["kv"], 16, 4, 7)
            values_projected(start["kv"] + 8, 19, 4)
            norm(11)
            ffn(2, 8)
            norm(12)
            projected(start["q1"], 20, 4, 9)
            rotate(23, "perm_b")
            pe.wait_ge(rope_out, 24)
            attention2(1)
            out_proj(1, 10, "wo1")
            norm(13)
            ffn(3, 10)
            norm(14)

        @block.scalar
        def _(act):
            chain = [0]

            def link(ins):
                chain[0] += 1
                ins.then_inc(act_chain, 1)
                act.wait_ge(act_chain, chain[0])

            def split(c, i=None, per=0):
                if i is None and c >= TOTAL:
                    return
                r = c % RING
                if i is None:
                    act.wait_ge(raw_loaded[r], 16 * (c // RING + 1))
                    if c >= RING:
                        act.wait_ge(w_used, c - RING + 1)
                else:
                    act.wait_ge(raw_loaded[r], i * (16 * per // RING) + 16 * (c // RING + 1))
                    act.wait_ge(w_used, i * per + (c - RING + 1))
                nc.scalar.activation(w_hi[:, r, :], raw[:, r, :], ACT.Copy).then_inc(w_hi_ready, 1)

            def splits(c, n=2):
                for j in range(n):
                    split(c + j + RING)

            def squares(nid, src, event=None):
                for c in range(4):
                    if event is None:
                        act.wait_ge(ctx_loaded if src is cx else x_loaded, 16)
                    else:
                        act.wait_ge(src_ready, 4 * event + c + 1)
                    nc.scalar.activation(squares_of(nid)[:, 2 * c:2 * c + 2, :], src[:, 2 * c:2 * c + 2, :],
                                         ACT.Square).then_inc(sq_ready, 1)

            def root(nid):
                act.wait_ge(ms_ready, MS_ORDER.index(nid) + 1)
                nc.scalar.activation(rt, PS[:, NORM_BANK(nid), 0:T], ACT.Sqrt, bias=eps[:, 0:1]).then_inc(rt_ready, 1)

            def norm(nid, src, event=None):
                squares(nid, src, event)
                root(nid)

            def high(nid_lo, shift=None, hi=h_hi):
                for kk in range(KD):
                    act.wait_ge(norm_v, KD * nid_lo + kk + 1)
                    if shift is None:
                        ins = nc.scalar.activation(hi[:, kk, :], normed_of(nid_lo)[:, kk, :], ACT.Copy)
                    else:
                        ins = nc.scalar.activation(hi[:, kk, :], normed_of(nid_lo)[:, kk, :], ACT.Identity, bias=shift(kk))
                    ins.then_inc(norm_hi, 1)

            def sines(n):
                act.wait_ge(fil_arg, n + 1)
                nc.scalar.activation((hid1, hid2)[n], arg, ACT.Sin).then_inc(fil_sin, 1)

            def tap_squares(l):
                act.wait_ge(fil_h, l + 1)
                nc.scalar.activation(h_sq[:, :, :, :], hw[:, :, :, :], ACT.Square).then_inc(fil_sq, 1)

            def tap_roots(l):
                act.wait_ge(fil_mm, [4, 7][l])
                nc.scalar.activation(conv_rt, PS[:, 2, :], ACT.Sqrt, scale=float(D)).then_inc(fil_rt, 1)

            def lambdas():
                for l in range(DEPTH):
                    act.wait_ge(lam_dots, l + 1)
                    nc.scalar.activation(dot_exp, dots, ACT.Exp).then_inc(lam_exp, 1)

            def exps(p, n):
                nk = P * len(key_tiles(p))
                act.wait_ge(nm_ready, 8 * p + n + 1)
                for m in range(2):
                    ins = nc.scalar.activation(probs[:, m, 0:nk], PS[:, SCORES + m, 0:nk], ACT.Exp,
                                               bias=neg_max[:, m:m + 1], scale=SUB ** -0.5,
                                               accum_out=den[:, m:m + 1])
                ins.then_inc(p_ready, 1)

            def head_squares(p, n):
                h, qt = n // 2, n % 2
                act.wait_ge(pv_done, 8 * p + n + 1)
                ins = nc.scalar.activation(squared[:, n, :], PS[:, HEADS_OUT + qt, h * P:(h + 1) * P], ACT.Square,
                                           accum_out=head_ss[:, 2 * h + qt:2 * h + qt + 1])
                if n == 7:
                    link(ins)

            def taps(p, j):
                l = LAYER_OF[p]
                act.wait_ge(w_used, start[f"pass{p}"] + part["hy"] + 2 * j + 2)
                for a_ in range(2):
                    f = 2 * j + a_
                    ins = nc.scalar.activation(hy[:, f, :], PS[:, j % 2, a_ * T:(a_ + 1) * T], ACT.Identity,
                                               scale=col(f"short_w{l}", 12 + f), bias=col(f"short_b{l}", f))
                ins.then_inc(tap_ready, 1)

            def take_turned(p, n):
                h, qt = n // 2, n % 2
                nt = len(key_tiles(p))
                act.wait_ge(turned, 8 * p + n + 1)
                nc.scalar.activation(mixw_t[:, h % 2, 0:nt, qt * P:(qt + 1) * P],
                                     PS[:, TURN, 0:nt * P].rearrange("p (k t) -> p k t", k=nt),
                                     ACT.Copy).then_inc(mixw_t_ready, 1)

            def keys_queries(p, behind_second=None, src=None, event=None):
                c0 = start[f"pass{p}"]
                splits(c0)
                if behind_second is not None:
                    squares(behind_second, src, event)
                splits(c0 + 2)
                if behind_second is not None:
                    root(behind_second)
                splits(c0 + 4, 4)
                splits(c0 + part["v"])

            def run_pass(p):
                c0 = start[f"pass{p}"]
                for n in range(8):
                    if n >= 2:
                        taps(p, n - 2)
                    exps(p, n)
                    splits(c0 + part["v"] + 2 + 2 * n)
                    take_turned(p, n)
                    if n >= 1:
                        head_squares(p, n - 1)
                splits(c0 + part["gu"] + 2)
                head_squares(p, 7)
                nc.scalar.activation(head_rt, head_ss, ACT.Sqrt, scale=1.0 / P,
                                     bias=eps[:, 0:1]).then_inc(head_rt_ready, 1)
                for j in range(2):
                    act.wait_ge(w_used, c0 + part["gu"] + 2 * j + 2)
                    nc.scalar.activation(gu[:, 2 * j:2 * j + 2, :], PS[:, j, :], ACT.Gelu).then_inc(act_evac, 1)
                for j in range(2):
                    split(c0 + part["gv"] + 2 * j + RING)
                    act.wait_ge(w_used, c0 + part["gv"] + 2 * j + 2)
                    nc.scalar.activation(gv[:, :, j * T:(j + 1) * T], PS[:, 2 + j, :].rearrange("p (t c) -> p t c", t=TT),
                                         ACT.Gelu).then_inc(act_evac, 1)
                    split(c0 + part["gv"] + 2 * j + 1 + RING)

                def gates(name, b, bank=0):
                    for j in range(2):
                        c = c0 + part[name] + 2 * j
                        split(c + RING)
                        act.wait_ge(w_used, c + 2)
                        if b >= 1:
                            act.wait_ge(gated_ready, 6 * p + 2 * (b - 1) + j + 1)
                        nc.scalar.activation(gate_act[:, j, :], PS[:, bank + j, :], ACT.Silu).then_inc(act_evac, 1)
                        split(c + 1 + RING)

                gates("ga", 0, 2)
                act.wait_ge(ln_centered, p + 1)
                for t in range(TT):
                    ins = nc.scalar.activation(lnv[:, t, :], gvc[:, t, :], ACT.Square,
                                               accum_out=ln_ss[:, t:t + 1])
                link(ins)
                nc.scalar.activation(ln_rt, ln_ss, ACT.Sqrt, scale=1.0 / BR,
                                     bias=eps[:, 0:1]).then_inc(ln_rt_ready, 1)
                gates("gb", 1)
                gates("gc", 2)
                each, per, ahead = (5, MERGE_TURN, 2) if p == 1 else (3, 9, 0)
                with act.Fori(0, 4) as i:
                    for b in range(3):
                        c = start[f"pass{p}_merge"] + each * b + ahead
                        for j in range(-ahead, 2):
                            split(c + j + RING, i, per)
                        act.wait_ge(merge_free, i * 3 + (15 * p + b + 1))
                        act.wait_ge(w_used, i * per + (c + 3))
                        nc.scalar.activation(sel[:, b, :], PS[:, 2 * b + 1, :], ACT.Sigmoid).then_inc(sel_ready, 1)
                        split(c + 2 + RING, i, per)
                act.wait_ge(merge_added, 8 * (p + 1))
                act.wait_ge(w_used, start[f"pass{p}_wo"])
                for kk in range(KD):
                    nc.scalar.activation(h_hi[:, kk, :], merged[:, kk, :], ACT.Copy).then_inc(m_hi, 1)
                act.wait_ge(m_lo, KD * (p + 1))

            def ffn(n):
                c0 = start[f"ffn{n}"]

                def post(c, s, i, base, sbase):
                    for j in range(3):
                        split(c + j + RING, i, 12)
                    act.wait_ge(gu_free, base if i is None else i * 2 + base)
                    act.wait_ge(w_used, c + 4 if i is None else i * 12 + (c + 4))
                    nc.scalar.activation(silu[:, s, :], PS[:, 2 * s, :], ACT.Silu).then_inc(silu_ready, 1)
                    split(c + 3 + RING, i, 12)

                def downs(c, i):
                    for f in range(2):
                        split(c + f + RING, i, 12)

                g = 13 * n
                post(c0, 0, None, g + 1, 0)
                with act.Fori(0, 4) as i:
                    for e in range(2):
                        c = c0 + 4 + 6 * e
                        post(c, (1 + e) % 2, i, g + 2 + e, 0)
                        downs(c + 4, i)
                for pr in (9, 10):
                    c = c0 + 4 + 6 * (pr - 1)
                    post(c, pr % 2, None, g + pr + 1, 0)
                    downs(c + 4, None)
                downs(c0 + FFN_SLOTS - 2, None)

            def exps2(n, unit):
                b = unit % 2
                act.wait_ge(nm2_ready, 8 * n + unit + 1)
                for h in range(2):
                    m = 4 * b + h
                    nc.scalar.activation(probs2[:, b, h, 0:P], biased[:, b, h, 0:P], ACT.Exp,
                                         bias=neg_max[:, m:m + 1], accum_out=den[:, m:m + 1])
                    ins = nc.scalar.activation(probs2[:, b, h, P:SEG], biased[:, b, h, P:SEG], ACT.Exp,
                                               bias=neg_max[:, m + 2:m + 3], accum_out=den[:, m + 2:m + 3])
                ins.then_inc(p2_ready, 1)

            def take_turned2(n, unit):
                act.wait_ge(turned2, 8 * n + unit + 1)
                nc.scalar.activation(probs2_t[:, unit % 2, :, :], PS[:, TURN:TURN + 2, 0:SEG], ACT.Copy).then_inc(p2t_ready, 1)

            def heads_high(n, unit):
                act.wait_ge(pv2_done, 8 * n + unit + 1)
                nc.scalar.activation(g_hi[:, unit, :], PS[:, 6, 0:T], ACT.Copy).then_inc(o2_hi, 1)

            def attention2(n):
                exps2(n, 0)
                for unit in range(8):
                    if unit + 1 < 8:
                        exps2(n, unit + 1)
                    take_turned2(n, unit)
                    heads_high(n, unit)

            act.wait_ge(ones_ready, 1)
            act.wait_ge(cols_loaded, 16)
            nc.scalar.activation(c_act[:, :], col("cond", 0, 16), ACT.Silu).then_inc(cond_act, 1)
            sines(0)
            sines(1)
            tap_squares(0)
            lambdas()
            tap_roots(0)
            act.wait_ge(ada_rows_ready, 3 * ADA_TURNS)
            squares(0, cx)
            for c in range(RING):
                split(c)
            root(0)
            tap_squares(1)
            tap_roots(1)
            high(0, lambda kk: mod[:, 0, kk, 1:2])
            keys_queries(0)
            run_pass(0)
            squares(2, x)
            splits(start["pass0_wo"])
            root(2)
            splits(start["pass0_wo"] + 2, 6)
            act.wait_ge(w_used, start["pass1"])
            high(1, lambda kk: mod[:, 0, kk, 0:1])
            keys_queries(1, 1, branch_out, OUT_EVENT[0])
            run_pass(1)
            squares(4, cx, 1)
            splits(start["pass1_wo"])
            root(4)
            high(2, lambda kk: mod[:, 1, kk, 1:2], g_hi)
            splits(start["pass1_wo"] + 2, 6)
            squares(3, branch_out, OUT_EVENT[1])
            splits(start["ctx_k"], 4)
            root(3)
            splits(start["ctx_v"], 4)
            norm(5, x, 3)
            high(3, lambda kk: mod[:, 1, kk, 0:1])
            keys_queries(2)
            run_pass(2)
            splits(start["pass2_wo"], 8)
            norm(6, branch_out, OUT_EVENT[2])
            norm(7, x, 5)
            high(4)
            ffn(0)
            norm(8, x, 6)
            high(5)
            splits(start["qkv0"], 24)
            attention2(0)
            splits(start["wo0"], 8)
            norm(9, x, 7)
            high(6)
            ffn(1)
            norm(10, x, 8)
            high(7)
            splits(start["kv"], 16)
            norm(11, x, 8)
            high(8)
            ffn(2)
            norm(12, x, 9)
            high(9)
            splits(start["q1"], 8)
            attention2(1)
            splits(start["wo1"], 8)
            norm(13, x, 10)
            high(10)
            ffn(3)
            norm(14, x, 11)

        @block.vector
        def _(dve):
            V = nc.vector
            chain = [0]

            def link(ins):
                chain[0] += 1
                ins.then_inc(dve_chain, 1)
                dve.wait_ge(dve_chain, chain[0])

            def split(c, i=None, per=0):
                if i is None and c >= TOTAL:
                    return
                r = c % RING
                dve.wait_ge(w_hi_ready, c + 1 if i is None else i * per + (c + 1))
                V.tensor_tensor(w_lo[:, r, :], raw[:, r, :], f32(w_hi[:, r, :]), ALU.subtract).then_inc(w_lo_ready, 1)

            def splits(c, n=2):
                for j in range(n):
                    split(c + j + RING)

            def norm_rstd(nid):
                dve.wait_ge(rt_ready, MS_ORDER.index(nid) + 1)
                link(V.reciprocal(rstd, rt))

            def norm_split(nid, nid_lo, src, g, shift=None, hi=h_hi, lo=h_lo):
                norm_rstd(nid)

                def scale_(kk):
                    V.scalar_tensor_tensor(normed_of(nid_lo)[:, kk, :], src[:, kk, :], g(kk), rstd, ALU.mult,
                                           ALU.mult).then_inc(norm_v, 1)

                def low(kk):
                    dve.wait_ge(norm_hi, KD * nid_lo + kk + 1)
                    if shift is None:
                        ins = V.tensor_tensor(lo[:, kk, :], normed_of(nid_lo)[:, kk, :], f32(hi[:, kk, :]), ALU.subtract)
                    else:
                        ins = V.scalar_tensor_tensor(lo[:, kk, :], normed_of(nid_lo)[:, kk, :], shift(kk), f32(hi[:, kk, :]),
                                                     ALU.add, ALU.subtract)
                    ins.then_inc(norm_lo, 1)

                scale_(0)
                scale_(1)
                for kk in range(KD):
                    if kk + 2 < KD:
                        scale_(kk + 2)
                    low(kk)

            def post_norm(p, nid):
                dst = sources(p)
                l, w = LAYER_OF[p], 1 if ON_CTX[p] else 0
                norm_rstd(nid)
                for kk in range(KD):
                    ins = V.scalar_tensor_tensor(branch_out[:, kk, :], branch_out[:, kk, :], gate[:, l, kk, w:w + 1], rstd,
                                                 ALU.mult, ALU.mult)
                link(ins)
                for c in range(4):
                    s = slice(2 * c, 2 * c + 2)
                    V.tensor_tensor(dst[:, s, :], dst[:, s, :], branch_out[:, s, :], ALU.add).then_inc(src_ready, 1)

            def ada_piece(c, turn, m, banks, i=None):
                if i is None:
                    dve.wait_ge(ada_used, ADA_TURN * turn + 2 * m + 2)
                else:
                    dve.wait_ge(w_used, at(c + 2, i, MERGE_TURN))
                if m == 0 and turn > 0:
                    dve.wait_ge(ada_turned, at(turn, i, 1))
                n = 2 if i is None else 4
                V.tensor_copy(ada_rows[0:n, m * T:(m + 1) * T], PS[0:n, banks[m % 2], 0:T]).then_inc(ada_rows_ready, 1)

            def ada_take(turn, bank, i=None):
                dve.wait_ge(ada_turned, at(turn + 1, i, 1))
                dst = mod_raw[:, 12 * turn:12 * turn + 12] if i is None else mod_raw[:, bass.ds(i * 12, 12)]
                V.tensor_copy(dst, PS[:, bank, 0:12]).then_inc(ada_taken, 1)

            def modulation(turn):
                for m in range(3):
                    ada_piece(None, turn, m, (0, 1))

            def mod_vectors(l):
                dve.wait_ge(ada_taken, ADA_TURNS * (l + 1))
                m = mod_raw[:, :].rearrange("p (f w) -> p f w", w=2)
                for w in range(2):
                    ins = V.tensor_tensor(mod[:, l, :, w], m[:, :, w], col(f"ada_b{l}", 0, 24), ALU.add)
                link(ins)
                for w in range(2):
                    V.scalar_tensor_tensor(gain[:, l, :, w], mod[:, l, KD:2 * KD, w], 1.0, col(f"norm_pre{l}", 0, KD),
                                           ALU.add, ALU.mult)
                    ins = V.tensor_tensor(gate[:, l, :, w], mod[:, l, 2 * KD:3 * KD, w], col(f"norm_post{l}", 0, KD),
                                          ALU.mult)
                link(ins)

            def sine_args(n):
                dve.wait_ge(fil_mm, n + 1)
                link(V.tensor_scalar(arg, PS[:, 2 + n, 0:T], col(f"filter_b{n + 1}"), col(f"freq{n}"), ALU.add, ALU.mult))
                link(V.tensor_scalar(turns, arg, 1 / (2 * math.pi), ROUND, ALU.mult, ALU.add))
                link(V.tensor_scalar(turns, turns, -ROUND, None, ALU.add))
                link(V.scalar_tensor_tensor(arg, turns, -TWO_PI_HI, arg, ALU.mult, ALU.add))
                link(V.scalar_tensor_tensor(arg, turns, -TWO_PI_LO, arg, ALU.mult, ALU.add))
                V.tensor_scalar(arg, arg, PI_SAFE, -PI_SAFE, ALU.min, ALU.max).then_inc(fil_arg, 1)

            def lambdas():
                dve.wait_ge(lam_loaded, 16 * DEPTH)
                for l in range(DEPTH):
                    lam_init = 0.8 - 0.6 * math.exp(-0.3 * l)
                    lp = lam_rows[:, l, :].rearrange("p (a b d) -> p a b d", a=2, b=2)
                    t_ = turns[:, 0:2 * SUB].rearrange("p (a d) -> p a d", a=2)
                    link(V.tensor_tensor(t_, lp[:, :, 0, :], lp[:, :, 1, :], ALU.mult))
                    V.reduce_sum(dots, t_, AX_X).then_inc(lam_dots, 1)
                    dve.wait_ge(lam_exp, l + 1)
                    link(V.tensor_tensor(lam, dot_exp[:, 0:1], dot_exp[:, 1:2], ALU.subtract))
                    V.tensor_scalar(neg_lam[:, l, :], lam, -1.0, -lam_init, ALU.mult, ALU.add)
                    link(V.tensor_scalar(subln_g[:, l, :], col(f"subln{l}"), 1.0 - lam_init, None, ALU.mult))

            def filter_taps(l):
                dve.wait_ge(fil_mm, [3, 6][l])
                dec = fconst("decay").rearrange("p (t c) -> p t c", t=TT)
                for d in range(2):
                    ins = V.tensor_tensor(hw[:, d, :, :], PS[:, 4 + 2 * d:6 + 2 * d, :], dec, ALU.mult)
                link(ins)
                link(V.memset(hw[0:1, 1, 0, :], 0.0))
                V.tensor_tensor(h_sum, hw[:, 0, :, :], hw[:, 1, :, :], ALU.add)
                V.tensor_tensor(h_dif, hw[:, 0, :, :], hw[:, 1, :, :], ALU.subtract).then_inc(fil_h, 1)

            def filter_spectrum(l):
                dve.wait_ge(fil_rt, l + 1)
                link(V.reciprocal(conv_rs, conv_rt))
                dve.wait_ge(fil_mm, [5, 8][l])
                both = conv_rs.rearrange("p (o c) -> p o c", o=1).to_broadcast([P, 2, BR])
                V.tensor_tensor(spec_re[:, l, :, :], PS[:, 4:6, :], both, ALU.mult)
                V.tensor_tensor(spec_im[:, l, :, :], PS[:, 6:8, :], both, ALU.mult)
                V.tensor_tensor(spec_ny[:, l, :], PS[:, 3, :], conv_rs, ALU.mult).then_inc(fil_taken, 1)

            def rope_turn(n, dst, cos, sin):
                def two(t):
                    return const(t).rearrange("p (o t) -> p o t", o=1).to_broadcast([P, 2, T])
                dve.wait_ge(rope_rot, n + 1)
                V.tensor_tensor(rope_a.rearrange("p (k t) -> p k t", k=2), rope_raw[:, n % 2, :].rearrange("p (k t) -> p k t", k=2),
                                two(cos), ALU.mult)
                link(V.tensor_tensor(rope_b.rearrange("p (k t) -> p k t", k=2),
                                     PS[:, MISC, :].rearrange("p (k t) -> p k t", k=2), two(sin), ALU.mult))
                V.tensor_tensor(dst, rope_a.rearrange("p (k t) -> p k t", k=2), rope_b.rearrange("p (k t) -> p k t", k=2),
                                ALU.add).then_inc(rope_out, 1)

            def take_values(c, bank, dst, done):
                dve.wait_ge(w_used, c + 2)
                V.tensor_copy(dst, PS[:, bank, :].rearrange("p (t c) -> p t c", t=TT)).then_inc(done, 1)

            def softmax_max(p, n):
                nk = P * len(key_tiles(p))
                dve.wait_ge(sc_done, 8 * p + n + 1)
                link(V.reduce_max(mx[:, 0:2], PS[:, SCORES:SCORES + 2, 0:nk], AX_X))
                V.tensor_scalar(neg_max[:, 0:2], mx[:, 0:2], -(SUB ** -0.5), None, ALU.mult).then_inc(nm_ready, 1)

            def softmax_mix(p, n):
                nk = P * len(key_tiles(p))
                dve.wait_ge(p_ready, 8 * p + n + 1)
                link(V.reciprocal(rden[:, 0:2], den[:, 0:2]))
                V.tensor_tensor(wden[:, 0:1], rden[:, 1:2], neg_lam[:, LAYER_OF[p], :], ALU.mult)
                link(V.tensor_scalar(mixw[:, 0:nk], probs[:, 0, 0:nk], rden[:, 0:1], None, ALU.mult))
                V.scalar_tensor_tensor(mixw[:, 0:nk], probs[:, 1, 0:nk], wden[:, 0:1], mixw[:, 0:nk], ALU.mult,
                                       ALU.add).then_inc(mixw_ready, 1)

            def short_conv(p, j):
                l = LAYER_OF[p]
                dve.wait_ge(tap_ready, 6 * p + j + 1)

                def outer(tap, out_tokens, in_tokens):
                    for a_ in range(2):
                        f = 2 * j + a_
                        z = PS[:, j % 2, a_ * T:(a_ + 1) * T]
                        ins = V.scalar_tensor_tensor(hy[:, f, out_tokens], z[:, in_tokens], col(f"short_w{l}", 12 * tap + f),
                                                     hy[:, f, out_tokens], ALU.mult, ALU.add)
                    return ins

                link(outer(0, slice(1, T), slice(0, T - 1)))
                outer(2, slice(0, T - 1), slice(1, T)).then_inc(dve_evac, 1)

            def gating(p, b, c0, split_off=0):
                name = ("ga", "gb", "gc")[b]
                for j in range(2):
                    c = c0 + part[name] + 2 * j
                    if j >= split_off:
                        split(c + RING)
                    s = slice(KB * b + 2 * j, KB * b + 2 * j + 2)
                    dve.wait_ge(act_evac, act_pairs(p, 4 + 2 * b + j))
                    gd = gated[:, j, :, :]
                    link(V.tensor_tensor(gd, y[:, 2 * j:2 * j + 2, :],
                                         gate_act[:, j, :].rearrange("p (k t) -> p k t", k=2), ALU.mult))
                    link(V.tensor_copy(g_hi[:, s, :], gd))
                    V.tensor_tensor(g_lo[:, s, :], gd, f32(g_hi[:, s, :]), ALU.subtract).then_inc(gated_ready, 1)
                    if j >= split_off:
                        split(c + 1 + RING)

            def keys_queries(p, behind_second=None):
                c0 = start[f"pass{p}"]
                on_x = not ON_CTX[p]
                rb = ROPE_BASE[p]
                base = 0 if on_x else 4
                dsts = [k[:, base:base + 2, :], k[:, base + 2:base + 4, :], q[:, 0:2, :], q[:, 2:4, :]]
                for j in range(4):
                    c = c0 + 2 * j
                    split(c + RING)
                    if on_x:
                        rope_copy(rb + j, j % 2, c)
                        split(c + 1 + RING)
                        if j >= 1:
                            rope_turn(rb + j - 1, dsts[j - 1], "cos_a", "sin_a")
                        if j == 1 and behind_second is not None:
                            post_norm(*behind_second)
                    else:
                        dve.wait_ge(w_used, c + 2)
                        V.tensor_copy(dsts[j], PS[:, j % 2, :].rearrange("p (k t) -> p k t", k=2)).then_inc(dve_evac, 1)
                        split(c + 1 + RING)
                kt = 0 if on_x else 2
                split(c0 + part["v"] + RING)
                take_values(c0 + part["v"], 0, v[:, kt:kt + 2, 0:T], dve_evac)
                if on_x:
                    rope_turn(rb + 3, dsts[3], "cos_a", "sin_a")
                split(c0 + part["v"] + 1 + RING)

            def run_pass(p):
                l = LAYER_OF[p]
                c0 = start[f"pass{p}"]
                kt = 0 if not ON_CTX[p] else 2
                for n in range(8):
                    softmax_max(p, n)
                    if n == 1:
                        take_values(c0 + part["v"] + 2, 1, v[:, kt:kt + 2, T:2 * T], dve_evac)
                    elif n >= 2:
                        short_conv(p, n - 2)
                    softmax_mix(p, n)
                    splits(c0 + part["v"] + 2 + 2 * n)
                V.tensor_tensor(u, u, hy[:, 8:12, :], ALU.mult).then_inc(u_ready, 1)
                splits(c0 + part["gu"] + 2)
                dve.wait_ge(head_rt_ready, p + 1)
                link(V.reciprocal(head_rs, head_rt))
                for h in range(HEADS_A):
                    for qt in range(TT):
                        ins = V.tensor_scalar(head_y[:, h, qt, :], PS[:, HEADS_OUT + qt, h * P:(h + 1) * P],
                                              head_rs[:, 2 * h + qt:2 * h + qt + 1], None, ALU.mult)
                ins.then_inc(head_y_ready, 1)
                dve.wait_ge(u_t, p + 1)
                V.tensor_copy(u_tok[:, 0, :], PS[:, TURN, :])
                V.tensor_copy(u_tok[:, 1, :], PS[:, MISC, :]).then_inc(u_tok_ready, 1)
                splits(c0 + part["gv"])
                dve.wait_ge(dft_done, p + 1)
                ur, ui = PS[:, 0:2, :], PS[:, HEADS_OUT:HEADS_OUT + 2, :]
                yr, yi = yspec[:, 0:2, :], yspec[:, 2:4, :]
                V.tensor_tensor(yr, ur, spec_re[:, l, :, :], ALU.mult)
                link(V.tensor_tensor(prod, ui, spec_im[:, l, :, :], ALU.mult))
                link(V.tensor_tensor(yr, yr, prod, ALU.subtract))
                splits(c0 + part["gv"] + 2)
                dve.wait_ge(head_t, p + 1)
                for b in range(2):
                    ins = V.tensor_scalar(y[:, 2 * b:2 * b + 2, :], PS[:, [TURN, MISC][b], :].rearrange("p (k t) -> p k t", t=T),
                                          subln_g[:, l, :], None, ALU.mult)
                ins.then_inc(y_ready, 1)
                split(c0 + part["ga"] + RING)
                V.tensor_tensor(yi, ur, spec_im[:, l, :, :], ALU.mult)
                V.tensor_tensor(prod[:, 0, :], ui[:, 0, :], spec_ny[:, l, :], ALU.mult)
                link(V.tensor_tensor(prod[:, 1, :], ui[:, 1, :], spec_re[:, l, 1, :], ALU.mult))
                V.tensor_tensor(yi, yi, prod, ALU.add).then_inc(yspec_ready, 1)
                split(c0 + part["ga"] + 1 + RING)
                dve.wait_ge(act_evac, act_pairs(p, 3))
                link(V.reduce_sum(ln_sum, gv[:, :, :], AX_X))
                for t in range(TT):
                    ins = V.scalar_tensor_tensor(gvc[:, t, :], ln_sum[:, t:t + 1].to_broadcast([P, BR]), -1.0 / BR, gv[:, t, :],
                                                 ALU.mult, ALU.add)
                ins.then_inc(ln_centered, 1)
                dve.wait_ge(y_ready, p + 1)
                gating(p, 0, c0, 1)
                dve.wait_ge(ln_rt_ready, p + 1)
                dve.wait_ge(layer_loaded, 16 * (l + 1))
                link(V.reciprocal(ln_rs, ln_rt))
                for t in range(TT):
                    ins = V.scalar_tensor_tensor(gvc[:, t, :], gvc[:, t, :], ln_rs[:, t:t + 1], row("ln_g"), ALU.mult,
                                                 ALU.mult)
                link(ins)
                for t in range(TT):
                    ins = V.tensor_tensor(lnv[:, t, :], gvc[:, t, :], row("ln_b"), ALU.add)
                ins.then_inc(lnv_ready, 1)
                dve.wait_ge(conv_done, p + 1)
                for c in range(KB):
                    ins = V.scalar_tensor_tensor(y[:, c, :], u[:, c, :], col(f"conv_bias{l}", c),
                                                 PS[:, [TURN, MISC][c // 2], (c % 2) * T:(c % 2 + 1) * T], ALU.mult, ALU.add)
                link(ins)
                link(V.tensor_tensor(y[:, :, :], y[:, :, :], hy[:, 0:4, :], ALU.mult))
                gating(p, 1, c0)
                dve.wait_ge(mixed, p + 1)
                bias = row("mix_bias").rearrange("p (k o t) -> p k o t", k=KB, o=1).to_broadcast([P, KB, TT, P])
                link(V.tensor_tensor(y[:, :, :].rearrange("p k (c t) -> p k c t", c=TT),
                                     PS[:, SCORES:SCORES + 2, :].rearrange("p b (k c t) -> p (b k) c t", c=TT, t=P),
                                     bias, ALU.add))
                link(V.tensor_tensor(y[:, :, :], y[:, :, :], gu[:, :, :], ALU.mult))
                V.memset(signal, 0.0).then_inc(merge_free, 2)
                gating(p, 2, c0)
                V.memset(signal, 0.0).then_inc(merge_free, 1)
                each, per, ahead = (5, MERGE_TURN, 2) if p == 1 else (3, 9, 0)
                with dve.Fori(0, 4) as i:
                    for b in range(3):
                        c = start[f"pass{p}_merge"] + each * b + ahead
                        if p == 1:
                            for j in range(2):
                                split(c - ahead + j + RING, i, per)
                            ada_piece(c - ahead, ADA_TURNS, b, (6, 7), i)
                        split(c + RING, i, per)
                        split(c + 1 + RING, i, per)
                        dve.wait_ge(sel_ready, i * 3 + (12 * p + b + 1))
                        m = merged.rearrange("p k t -> p (k t)")[:, bass.ds(i * 512, 512)]
                        V.tensor_tensor(m if b == 0 else term, sel[:, b, :], PS[:, 2 * b, :], ALU.mult).then_inc(merge_free, 1)
                        if b >= 1:
                            dve.wait_ge(merge_free, i * 3 + (15 * p + 3 + b + 1))
                            if b == 2:
                                dve.wait_ge(merge_added, i * 2 + (8 * p + 1))
                            V.tensor_tensor(m, m, term, ALU.add).then_inc(merge_added, 1)
                        split(c + 2 + RING, i, per)
                    if p == 1:
                        ada_take(ADA_TURNS, 7, i)
                for kk in range(KD):
                    dve.wait_ge(m_hi, KD * p + kk + 1)
                    V.tensor_tensor(h_lo[:, kk, :], merged[:, kk, :], f32(h_hi[:, kk, :]), ALU.subtract).then_inc(m_lo, 1)

            def take_branch_sum(p, j):
                c = start[f"pass{p}_wo"] + 2 * j
                split(c + RING)
                dve.wait_ge(w_used, c + 2)
                V.tensor_copy(branch_out[:, 2 * j:2 * j + 2, :],
                              PS[:, 4 + j % 2, :].rearrange("p (k t) -> p k t", k=2)).then_inc(src_ready, 1)
                split(c + 1 + RING)

            def rope_copy(n, bank, c):
                dve.wait_ge(w_used, c + 2)
                if n >= 2:
                    dve.wait_ge(rope_rot, n - 1)
                V.tensor_copy(rope_raw[:, n % 2, :], PS[:, bank, :]).then_inc(rope_in, 1)
                dve.wait_ge(rope_in, n + 1)

            def ffn(n):
                c0 = start[f"ffn{n}"]
                V.memset(signal, 0.0).then_inc(gu_free, 2)

                def post(c, s, i, pr):
                    split(c + RING, i, 12)
                    split(c + 1 + RING, i, 12)
                    split(c + 2 + RING, i, 12)
                    b = FPAIRS * n + pr + 1
                    dve.wait_ge(silu_ready, at(b, i, 2))
                    V.tensor_tensor(act_f, silu[:, s, :], PS[:, 2 * s + 1, :], ALU.mult).then_inc(gu_free, 1)
                    dve.wait_ge(gu_free, at(13 * n + 2 + pr + 1, i, 2))
                    hi = act_hi[:, s, :, :].rearrange("p f t -> p (f t)")
                    lo = act_lo[:, s, :, :].rearrange("p f t -> p (f t)")
                    V.tensor_copy(hi, act_f).then_inc(act_hi_ready, 1)
                    dve.wait_ge(act_hi_ready, at(b, i, 2))
                    V.tensor_tensor(lo, act_f, f32(hi), ALU.subtract).then_inc(act_ready, 1)
                    split(c + 3 + RING, i, 12)

                def downs(c, i):
                    for f in range(2):
                        split(c + f + RING, i, 12)

                post(c0, 0, None, 0)
                with dve.Fori(0, 4) as i:
                    for e in range(2):
                        c = c0 + 4 + 6 * e
                        post(c, (1 + e) % 2, i, 1 + e)
                        downs(c + 4, i)
                for pr in (9, 10):
                    c = c0 + 4 + 6 * (pr - 1)
                    post(c, pr % 2, None, pr)
                    downs(c + 4, None)
                downs(c0 + FFN_SLOTS - 2, None)
                dve.wait_ge(w_used, c0 + FFN_SLOTS)
                for j in range(4):
                    s = slice(2 * j, 2 * j + 2)
                    V.scalar_tensor_tensor(x[:, s, :], PS[:, 4 + j, :].rearrange("p (k t) -> p k t", k=2), 0.5, x[:, s, :],
                                           ALU.mult, ALU.add).then_inc(src_ready, 1)

            def softmax2(n, unit, table):
                b = unit % 2
                bank = SCORES - 2 * b
                dve.wait_ge(sc2_done, 8 * n + unit + 1)
                bias = const(table).rearrange("p (o s) -> p o s", o=1).to_broadcast([P, 2, SEG])
                V.scalar_tensor_tensor(biased[:, b, :, :], PS[:, bank:bank + 2, 0:SEG], HD ** -0.5, bias, ALU.mult,
                                       ALU.add).then_inc(biased_ready, 1)
                dve.wait_ge(biased_ready, 8 * n + unit + 1)
                V.reduce_max(mx[:, 4 * b:4 * b + 2], biased[:, b, :, 0:P], AX_X)
                link(V.reduce_max(mx[:, 4 * b + 2:4 * b + 4], biased[:, b, :, P:SEG], AX_X))
                V.tensor_scalar(neg_max[:, 4 * b:4 * b + 4], mx[:, 4 * b:4 * b + 4], -1.0, None, ALU.mult).then_inc(nm2_ready, 1)

            def normalize2(n, unit):
                b = unit % 2
                dve.wait_ge(p2_ready, 8 * n + unit + 1)
                link(V.reciprocal(rden[:, 4 * b:4 * b + 4], den[:, 4 * b:4 * b + 4]))
                for h in range(2):
                    m = 4 * b + h
                    V.tensor_scalar(probs2[:, b, h, 0:P], probs2[:, b, h, 0:P], rden[:, m:m + 1], None, ALU.mult)
                    ins = V.tensor_scalar(probs2[:, b, h, P:SEG], probs2[:, b, h, P:SEG], rden[:, m + 2:m + 3], None, ALU.mult)
                ins.then_inc(p2n_ready, 1)

            def heads_low(n, unit):
                dve.wait_ge(o2_hi, 8 * n + unit + 1)
                V.tensor_tensor(g_lo[:, unit, :], PS[:, 6, 0:T], f32(g_hi[:, unit, :]), ALU.subtract).then_inc(o2_ready, 1)

            def attention2(n, table):
                softmax2(n, 0, table)
                for unit in range(8):
                    if unit + 1 < 8:
                        softmax2(n, unit + 1, table)
                    normalize2(n, unit)
                    if unit >= 1:
                        heads_low(n, unit - 1)
                heads_low(n, 7)

            def rope_phase(c0, n0, dsts):
                for j, dst in enumerate(dsts):
                    split(c0 + 2 * j + RING)
                    rope_copy(n0 + j, j % 2, c0 + 2 * j)
                    split(c0 + 2 * j + 1 + RING)
                    if j >= 1:
                        rope_turn(n0 + j - 1, dsts[j - 1], "cos_b", "sin_b")

            def values_phase(c0, n0, dst):
                for j in range(4):
                    split(c0 + 2 * j + RING)
                    take_values(c0 + 2 * j, j % 2, v2[:, :, j * T:(j + 1) * T], qkv_evac)
                    split(c0 + 2 * j + 1 + RING)
                    if j == 0:
                        rope_turn(n0, dst, "cos_b", "sin_b")

            def out_proj(name):
                c0 = start[name]
                for j in range(4):
                    s = slice(2 * j, 2 * j + 2)
                    split(c0 + 2 * j + RING)
                    dve.wait_ge(w_used, c0 + 2 * j + 2)
                    V.tensor_tensor(x[:, s, :], x[:, s, :], PS[:, 4 + j % 2, :].rearrange("p (k t) -> p k t", k=2),
                                    ALU.add).then_inc(src_ready, 1)
                    split(c0 + 2 * j + 1 + RING)

            def pairs_of(t):
                return [t[:, 2 * j:2 * j + 2, :] for j in range(4)]

            V.memset(ones[:, :], 1.0 / D)
            V.memset(zeros[:, :], 0.0)
            V.memset(eps[:, :], EPS).then_inc(ones_ready, 1)
            dve.wait_ge(cond_act, 1)
            cond = c_act[:, :].rearrange("p (k w) -> p k w", w=2)
            V.tensor_copy(c_parts[:, :, 0:2], cond).then_inc(cond_hi, 1)
            dve.wait_ge(cond_hi, 1)
            V.tensor_tensor(c_parts[:, :, 2:4], cond, f32(c_parts[:, :, 0:2]), ALU.subtract).then_inc(cond_ready, 1)
            modulation(0)
            sine_args(0)
            ada_take(0, 1)
            modulation(1)
            sine_args(1)
            ada_take(1, 1)
            modulation(2)
            filter_taps(0)
            ada_take(2, 1)
            lambdas()
            modulation(3)
            filter_spectrum(0)
            ada_take(3, 1)
            mod_vectors(0)
            filter_taps(1)
            for c in range(RING):
                split(c)
            norm_split(0, 0, cx, lambda kk: gain[:, 0, kk, 1:2], lambda kk: mod[:, 0, kk, 1:2])
            filter_spectrum(1)
            keys_queries(0)
            run_pass(0)
            for j in range(4):
                take_branch_sum(0, j)
            norm_split(2, 1, x, lambda kk: gain[:, 0, kk, 0:1], lambda kk: mod[:, 0, kk, 0:1])
            keys_queries(1, behind_second=(0, 1))
            run_pass(1)
            mod_vectors(1)
            take_branch_sum(1, 0)
            norm_split(4, 2, cx, lambda kk: gain[:, 1, kk, 1:2], lambda kk: mod[:, 1, kk, 1:2], g_hi, g_lo)
            for j in range(1, 4):
                take_branch_sum(1, j)
            for j in range(2):
                c = start["ctx_k"] + 2 * j
                split(c + RING)
                dve.wait_ge(w_used, c + 2)
                V.tensor_copy(k[:, 4 + 2 * j:6 + 2 * j, :], PS[:, j, :].rearrange("p (k t) -> p k t", k=2)).then_inc(dve_evac, 1)
                split(c + 1 + RING)
            post_norm(1, 3)
            for j in range(2):
                c = start["ctx_v"] + 2 * j
                split(c + RING)
                take_values(c, j, v[:, 2:4, j * T:(j + 1) * T], dve_evac)
                split(c + 1 + RING)
            norm_split(5, 3, x, lambda kk: gain[:, 1, kk, 0:1], lambda kk: mod[:, 1, kk, 0:1])
            keys_queries(2)
            run_pass(2)
            for j in range(4):
                take_branch_sum(2, j)
            post_norm(2, 6)
            norm_split(7, 4, x, lambda kk: col("ffn10", kk))
            ffn(0)
            norm_split(8, 5, x, lambda kk: col("mix0", kk))
            rope_phase(start["qkv0"], 8, pairs_of(q) + pairs_of(k))
            values_phase(start["qkv0"] + 16, 15, pairs_of(k)[3])
            attention2(0, "bias_dilated")
            out_proj("wo0")
            norm_split(9, 6, x, lambda kk: col("ffn20", kk))
            ffn(1)
            norm_split(10, 7, x, lambda kk: col("kv_norm", kk))
            rope_phase(start["kv"], 16, pairs_of(k))
            values_phase(start["kv"] + 8, 19, pairs_of(k)[3])
            norm_split(11, 8, x, lambda kk: col("ffn11", kk))
            ffn(2)
            norm_split(12, 9, x, lambda kk: col("mix1", kk))
            rope_phase(start["q1"], 20, pairs_of(q))
            rope_turn(23, pairs_of(q)[3], "cos_b", "sin_b")
            attention2(1, "bias_causal")
            out_proj("wo1")
            norm_split(13, 10, x, lambda kk: col("ffn21", kk))
            ffn(3)
            norm_rstd(14)
            for kk in range(KD):
                V.scalar_tensor_tensor(normed[:, kk, :], x[:, kk, :], col("final_norm", kk), rstd, ALU.mult,
                                       ALU.mult).then_inc(out_ready, 1)


OUT_EVENT = [0, 2, 4]
MS_ORDER = [0, 2, 1, 4, 3] + list(range(5, 15))


def constants():
    f = np.float32
    t = np.arange(T)
    out = {"ident": np.eye(P)}

    def rotary(width, ang_of, perm_name, cos_name, sin_name):
        cos, sin, perm = np.ones((P, T)), np.zeros((P, T)), np.zeros((P, P))
        for i in range(P):
            found = ang_of(i % width)
            if found is None:
                continue
            ang, first, half = found
            cos[i], sin[i] = np.cos(ang), np.sin(ang)
            if first:
                perm[i + half, i] = -1.0
            else:
                perm[i - half, i] = 1.0
        out[perm_name], out[cos_name], out[sin_name] = perm, cos, sin

    nf = SUB // 4

    def axial(i):
        axis, rest = divmod(i, 2 * nf)
        half, fr = divmod(rest, nf)
        inv = f(10000.0) ** (-np.arange(nf, dtype=f) / f(nf))
        pos = (t // 64 if axis == 0 else t % 64).astype(f)
        return (pos * inv[fr]).astype(f), half == 0, nf

    def partial(i):
        half_dim = HD // 8
        if i >= 2 * half_dim:
            return None
        half, fr = divmod(i, half_dim)
        inv = f(500000.0) ** (-np.arange(half_dim, dtype=f) / f(half_dim))
        return (t.astype(f) * inv[fr]).astype(f), half == 0, half_dim

    rotary(SUB, axial, "perm_a", "cos_a", "sin_a")
    rotary(HD, partial, "perm_b", "cos_b", "sin_b")

    diff = t[:, None] - t[None, :]
    causal = diff >= 0
    count = sum((causal & (diff <= w) & (diff % d == 0)).astype(int) for w, d in ((128, 1), (512, 4), (2048, 16)))
    for name, n in (("bias_dilated", count), ("bias_causal", causal.astype(int))):
        b = np.where(n > 0, np.log(np.maximum(n, 1)), -1e30)
        out[name] = np.concatenate([b[0:P, 0:P], b[P:T, :]], axis=1)

    def tiled(m):
        return m.reshape(-1, P, m.shape[1]).transpose(1, 0, 2).reshape(P, -1)

    w = np.pi * np.outer(t, t) / T
    sign = np.where(t % 2 == 0, 1.0, -1.0)
    out["dft_cos"] = tiled(np.cos(w))
    s = -np.sin(w)
    out["dft_sin_k"] = tiled(s)
    s = s.copy()
    s[:, 0] = sign
    out["dft_sin_u"] = tiled(s)
    ny = np.cos(w)[:, 0:P].copy()
    ny[:, 0] = sign
    out["dft_nyq"] = tiled(ny)
    weight = np.where(t == 0, 1.0, 2.0)[:, None] / (2 * T)
    re, im = weight * np.cos(w), -weight * np.sin(w)
    im[0, :] = sign / (2 * T)
    out["idft"] = tiled(np.concatenate([re, im], axis=0))
    lin = np.linspace(0.0, 1.0, T)
    lo, hi = math.log(1e-2) / 1.5, math.log(1e-2) / 0.3
    out["decay"] = tiled(np.exp(-lin[:, None] * np.abs(np.linspace(lo, hi, BR))[None, :]))
    wpos = (2.0 * math.pi / T) * t[None, :]
    bands = np.linspace(1e-4, 15, 16)[:, None]
    z = np.concatenate([lin[None, :], np.cos(bands * wpos), -np.sin(bands * wpos)], axis=0)
    out["filter_z"] = np.tile(np.concatenate([z, np.zeros((64 - 33, T))], axis=0), (DEPTH, 1))
    return [np.ascontiguousarray(np.concatenate([out[n].astype(f) for n, _ in part], axis=1))
            for part in (CONSTS, FILTER_CONSTS)]


def pack(inputs):
    g = {n: np.asarray(a) for n, a in inputs.items()}
    slots = []

    def tiles(w, lo=0, hi=None):
        w = w[:, lo:hi]
        for c in range(0, w.shape[1], P):
            slots.append(w[:, c:c + P].reshape(KD, P, P).transpose(1, 0, 2).reshape(P, SLOT))

    def token(w, lo=0, hi=None):
        w = w[:, lo:hi]
        for c in range(0, w.shape[1], T):
            for r in range(0, D, D // 2):
                slots.append(w[r:r + D // 2, c:c + T].reshape(4, P, T).transpose(1, 0, 2).reshape(P, SLOT))

    for l in range(DEPTH):
        token(g["ada_w"][l])
        w = g["w_in"][l]
        tiles(w, 0, 512)
        tiles(w, 1024, 1536)
        token(w, 512, 1024)
        tiles(w, 2048, 3584)
        tiles(w, 4096, 4608)
        token(w, 4608, 5120)
        tiles(w, 1536, 2048)
        tiles(w, 3584, 4096)
        tiles(w, 5120, 5632)
        for c in range(0, D, T):
            for b in range(3):
                slots.append(g["w_branch"][l, b][:, c:c + T].reshape(KB, P, T).transpose(1, 0, 2).reshape(P, SLOT))
                tiles(w, 5632 + b * D + c, 5632 + b * D + c + T)
        tiles(g["w_out"][l])

    def ffn(n, l):
        gate, up, down = (g[f"ffn{n}_w_{x}_2"][l] for x in ("gate", "up", "down"))
        for p in range(FPAIRS + 1):
            if p < FPAIRS:
                tiles(gate, 2 * P * p, 2 * P * (p + 1))
                tiles(up, 2 * P * p, 2 * P * (p + 1))
            if p >= 1:
                for f in (2 * p - 2, 2 * p - 1):
                    slots.append(down[f * P:(f + 1) * P, :])

    ffn(1, 0)
    tiles(g["a_w_qkv_2"][0], 0, 2 * D)
    token(g["a_w_qkv_2"][0], 2 * D, 3 * D)
    tiles(g["a_w_o_2"][0])
    ffn(2, 0)
    tiles(g["kv_w_2"], 0, D)
    token(g["kv_w_2"], D, 2 * D)
    ffn(1, 1)
    tiles(g["b_w_q_2"][0])
    tiles(g["b_w_o_2"][0])
    ffn(2, 1)
    weights = np.stack(slots)

    def column(v):
        return v.reshape(-1, P).T

    def padded(v, rows):
        return np.concatenate([v, np.zeros((rows - v.shape[0], v.shape[1]), v.dtype)], axis=0)

    cols = {"cond": np.stack([column(g["c"][0]), column(g["c_ctx"])], axis=2).reshape(P, 16),
            "ada_sum": padded(np.tile(np.eye(2, dtype=np.float32), (2, 1)), P),
            "kv_norm": column(g["kv_norm_2"]), "final_norm": column(g["final_norm_2"])}
    for name, v in (("filter_b1", g["hy_f_b1"]), ("filter_b2", g["hy_f_b2"]), ("freq0", g["hy_f_freq"][:, 0]),
                    ("freq1", g["hy_f_freq"][:, 1])):
        cols[name] = v.reshape(P, 1)
    layers, filters, lams = [], [], []
    for l in range(DEPTH):
        cols[f"norm_pre{l}"] = column(g["norm_pre"][l])
        cols[f"norm_post{l}"] = column(g["norm_post"][l])
        cols[f"ada_b{l}"] = column(g["ada_b"][l])
        cols[f"subln{l}"] = column(g["da_subln"][l])
        cols[f"short_w{l}"] = column(g["hy_short_w"][l].reshape(-1))
        cols[f"short_b{l}"] = column(g["hy_short_b"][l])
        cols[f"conv_bias{l}"] = column(g["hy_bias"][l])
        cols[f"ffn1{l}"] = column(g["ffn1_norm_2"][l])
        cols[f"mix{l}"] = column(g["mix_norm_2"][l])
        cols[f"ffn2{l}"] = column(g["ffn2_norm_2"][l])
        mix_bias = np.repeat(g["gm_bs"][l].reshape(KB, 2, 1, P), SUB, axis=2).reshape(KB, P, P)
        layers.append(np.concatenate([np.broadcast_to(g["gm_ln_g"][l], (P, BR)), np.broadcast_to(g["gm_ln_b"][l], (P, BR)),
                                      mix_bias.transpose(1, 0, 2).reshape(P, -1),
                                      g["gm_ws"][l].transpose(2, 0, 1).reshape(P, -1)], axis=1))
        filters.append(np.concatenate([padded(g["hy_f_w1"][l], 64), g["hy_f_w2"][l], g["hy_f_w3"][l]], axis=1))
        lams.append(np.broadcast_to(g["da_lambda"][l].reshape(-1), (P, 4 * SUB)))

    consts, filter_consts = constants()

    def stream(a):
        return np.ascontiguousarray(a[0].T.reshape(KD, P, T).transpose(1, 0, 2))

    return {"weights": weights, "x_in": stream(g["x"]), "ctx_in": stream(g["ctx"]),
            "cols_in": np.ascontiguousarray(np.concatenate([cols[n] for n, _ in COLUMNS], axis=1)),
            "consts_in": consts, "filter_consts_in": filter_consts, "layer_in": np.stack(layers), "filter_in": np.concatenate(filters, axis=0),
            "lam_in": np.stack(lams)}


def kernel(**inputs):
    import concourse.bacc as bacc
    from concourse.bass_utils import run_bass_kernel_spmd

    nc = bacc.Bacc("TRN2", target_bir_lowering=False, num_devices=1)
    arrays = pack(inputs)
    aps = {n: nc.dram_tensor(n, a.shape, mybir.dt.from_np(a.dtype), kind="ExternalInput").ap()
           for n, a in arrays.items()}
    out = nc.dram_tensor("out", (P, KD, T), F32, kind="ExternalOutput").ap()
    build(nc, out=out, **aps)
    r = run_bass_kernel_spmd(nc, [arrays], core_ids=[0])
    res = np.asarray(r.results[0]["out"])
    return np.ascontiguousarray(res.transpose(2, 1, 0).reshape(1, T, D))
```

```python
import math
from contextlib import ExitStack

import concourse.bass as bass
import numpy as np
from concourse import mybir

F32 = mybir.dt.float32
F32R = mybir.dt.float32r
ALU = mybir.AluOpType
ACT = mybir.ActivationFunctionType
AX_X = mybir.AxisListType.X

P = 128
T = 256
TT = T // P
D = 1024
KD = D // P
BR = 512
KB = BR // P
DEPTH = 2
FF = 2816
FPAIRS = FF // (2 * P)
HEADS_A, SUB = 4, 64
HEADS_B, HD = 16, 64
SLOT = 1024
RING = 3
SEG = 3 * P
EPS = 1e-6
TWO_PI_HI = 6.28125
TWO_PI_LO = 2 * math.pi - 6.28125
ROUND = 1.5 * 2 ** 23
PI_SAFE = 3.1415925

PASS = [("kq", 8), ("v", 4), ("hy", 12), ("gu", 4), ("gv", 4), ("ga", 4), ("gb", 4),
        ("gc", 4), ("merge", 36), ("wo", 8)]
PASS_SLOTS = sum(n for _, n in PASS)
MERGE_SLOTS = dict(PASS)["merge"]
MERGE_TURN = 3 * (3 + 2)
MERGE_AT = PASS_SLOTS - MERGE_SLOTS - dict(PASS)["wo"]
ADA_SLOTS = 3 * D // P
ADA_TURN = 6
ADA_TURNS = ADA_SLOTS // ADA_TURN
FFN_SLOTS = 3 * FF // P
SCORES, TURN, HEADS_OUT, MISC = 2, 4, 5, 7

COLUMNS = [("cond", 16), ("ada_sum", 2)]
for _l in range(DEPTH):
    COLUMNS += [(f"norm_pre{_l}", KD), (f"norm_post{_l}", KD), (f"ada_b{_l}", 24), (f"subln{_l}", 1),
                (f"short_w{_l}", 36), (f"short_b{_l}", 12), (f"conv_bias{_l}", KB),
                (f"ffn1{_l}", KD), (f"mix{_l}", KD), (f"ffn2{_l}", KD)]
COLUMNS += [("kv_norm", KD), ("final_norm", KD)]
COLUMNS += [("filter_b1", 1), ("filter_b2", 1), ("freq0", 1), ("freq1", 1)]
CONSTS = [("ident", P), ("perm_a", P), ("perm_b", P), ("cos_a", T), ("sin_a", T), ("cos_b", T),
          ("sin_b", T), ("bias_dilated", SEG), ("bias_causal", SEG), ("dft_cos", TT * T),
          ("dft_sin_u", TT * T), ("idft", 4 * T)]
FILTER_CONSTS = [("dft_sin_k", TT * T), ("dft_nyq", TT * P), ("decay", TT * BR), ("filter_z", T)]
LAYER = [("ln_g", BR), ("ln_b", BR), ("mix_bias", KB * P), ("mix_w", 8 * P)]
FILTER = [("w1", 64), ("w2", 64), ("w3", 2 * BR)]


def places(parts):
    out, at = {}, 0
    for name, n in parts:
        out[name] = (at, at + n)
        at += n
    return out, at


def build(nc, weights, x_in, ctx_in, cols_in, consts_in, filter_consts_in, layer_in, filter_in, lam_in, out):
    col_at, ncols = places(COLUMNS)
    const_at, nconsts = places(CONSTS)
    fconst_at, nfconsts = places(FILTER_CONSTS)
    layer_at, nlayer = places(LAYER)
    filter_at, nfilter = places(FILTER)

    start = {}
    stretches = []
    stream_len = 0

    def stretch(name, dram, n):
        nonlocal stream_len
        start[name] = stream_len
        stretches.append((stream_len, dram, n))
        stream_len += n

    dram_pass = [ADA_SLOTS, 2 * ADA_SLOTS + PASS_SLOTS]
    stretch("pass0", dram_pass[0], PASS_SLOTS)
    stretch("pass1", dram_pass[0], MERGE_AT)
    stretch("pass1_merge", None, MERGE_SLOTS + ADA_SLOTS)
    stretch("pass1_wo", dram_pass[0] + MERGE_AT + MERGE_SLOTS, 8)
    stretch("ctx_k", dram_pass[1], 2)
    stretch("ctx_k_rest", dram_pass[1] + 4, 2)
    stretch("ctx_v", dram_pass[1] + 8, 4)
    stretch("pass2", dram_pass[1], PASS_SLOTS)
    dram = dram_pass[1] + PASS_SLOTS
    for p in (0, 2):
        start[f"pass{p}_merge"] = start[f"pass{p}"] + MERGE_AT
        start[f"pass{p}_wo"] = start[f"pass{p}"] + MERGE_AT + MERGE_SLOTS
    tail = [("ffn0", FFN_SLOTS), ("vqk0", 24), ("wo0", 8), ("ffn1", FFN_SLOTS), ("kv", 16),
            ("ffn2", FFN_SLOTS), ("q1", 8), ("wo1", 8), ("ffn3", FFN_SLOTS)]
    for name, n in tail:
        stretch(name, dram, n)
        dram += n
    TOTAL = stream_len
    part = {}
    a = 0
    for name, n in PASS:
        part[name] = a
        a += n

    ctx = ExitStack()
    with ctx:
        def sb(name, shape, dt=F32):
            return ctx.enter_context(nc.sbuf_tensor(name, shape, dt))

        def sem(name):
            return ctx.enter_context(nc.semaphore(name))

        PS = ctx.enter_context(nc.psum_tensor("PS", [P, 8, 512], F32))
        raw = sb("raw", [P, RING, SLOT])
        w_hi = sb("w_hi", [P, RING, SLOT], F32R)
        w_lo = sb("w_lo", [P, RING, SLOT], F32R)
        x = sb("x", [P, KD, T])
        cx = sb("cx", [P, KD, T])
        h_hi = sb("h_hi", [P, KD, T], F32R)
        h_lo = sb("h_lo", [P, KD, T], F32R)
        g_hi = sb("g_hi", [P, 12, T], F32R)
        g_lo = sb("g_lo", [P, 12, T], F32R)
        qk = sb("qk", [P, 2 * KD, T])
        q = qk[:, 0:KD, :]
        k = qk[:, KD:2 * KD, :]
        v = sb("v", [P, 4, BR])
        v2 = v[:, :, :].rearrange("p (t a) c -> p t (a c)", a=2)
        cols = sb("cols", [P, ncols])
        consts = sb("consts", [P, nconsts])
        layer = sb("layer", [P, nlayer])
        spec_re = sb("spec_re", [P, DEPTH, 2, BR])
        spec_im = sb("spec_im", [P, DEPTH, 2, BR])
        spec_ny = sb("spec_ny", [P, DEPTH, BR])
        ones = sb("ones", [P, P])
        zeros = sb("zeros", [P, P], mybir.dt.bfloat16)
        eps = sb("eps", [P, 1])
        c_parts = sb("c_parts", [P, KD, 4], F32R)
        c_act = sb("c_act", [P, 16])
        mod_raw = sb("mod_raw", [P, 48])
        mod = sb("mod", [P, DEPTH, 24, 2])
        gain = sb("gain", [P, DEPTH, KD, 2])
        gate = sb("gate", [P, DEPTH, KD, 2])
        stat = sb("stat", [P, 88])
        arena = sb("arena", [P, 10752])

        def col(name, j=0, n=1):
            a = col_at[name][0] + j
            return cols[:, a:a + n]

        def const(name):
            a, b = const_at[name]
            return consts[:, a:b]

        def row(name):
            a, b = layer_at[name]
            return layer[:, a:b]

        def scratch(a, n):
            return arena[:, a:a + n]

        sq = scratch(0, 2048).rearrange("p (k t) -> p k t", k=KD)
        sq_behind = scratch(7680, 2048).rearrange("p (k t) -> p k t", k=KD)
        normed = scratch(2048, 2048).rearrange("p (k t) -> p k t", k=KD)
        rt = scratch(10240, 256)
        rstd = scratch(10496, 256)
        branch_out = scratch(4608, 2048).rearrange("p (k t) -> p k t", k=KD)
        merged = scratch(0, 2048).rearrange("p (k t) -> p k t", k=KD)
        sel = scratch(2048, 1536).rearrange("p (i n) -> p i n", i=3)
        term = scratch(3584, 512)
        rope_raw = scratch(0, 1024).rearrange("p (b n) -> p b n", b=2)
        rope_a = scratch(1024, 512)
        rope_b = scratch(1536, 512)
        probs = scratch(2048, 1024).rearrange("p (m n) -> p m n", m=2)
        mixw = scratch(3072, 512)
        mixw_t = scratch(3584, 2048).rearrange("p (b k t) -> p b k t", b=2, k=4)
        head_y = scratch(5632, 1024).rearrange("p (h q d) -> p h q d", h=4, q=2)
        y = scratch(6656, 1024).rearrange("p (k t) -> p k t", k=KB)
        squared = scratch(6656, 1024).rearrange("p (n d) -> p n d", n=8)
        hy = scratch(7680, 3072).rearrange("p (k t) -> p k t", k=12)
        u = hy[:, 4:8, :]
        gu = scratch(0, 1024).rearrange("p (k t) -> p k t", k=KB)
        gv = scratch(1024, 1024).rearrange("p (t c) -> p t c", t=TT)
        gvc = scratch(2048, 1024).rearrange("p (t c) -> p t c", t=TT)
        lnv = scratch(3584, 1024).rearrange("p (t c) -> p t c", t=TT)
        gate_act = scratch(4608, 1024).rearrange("p (b n) -> p b n", b=2)
        gated = scratch(5632, 1024).rearrange("p (b k t) -> p b k t", b=2, k=2)
        u_tok = v[:, 0:2, :]
        prod = k[:, 0:4, :].rearrange("p (a k) t -> p a (k t)", a=2)
        yspec = q[:, :, :].rearrange("p (a k) t -> p a (k t)", a=4)
        hw = q[:, :, :].rearrange("p (d t a) c -> p d t (a c)", d=2, t=TT)
        h_sum = k[:, 0:4, :].rearrange("p (t a) c -> p t (a c)", t=TT)
        h_dif = k[:, 4:8, :].rearrange("p (t a) c -> p t (a c)", t=TT)
        h_sq = v[:, :, :].rearrange("p (d t) c -> p d t c", d=2)
        fil = scratch(0, nfilter)
        arg = scratch(2304, T)
        turns = scratch(2816, T)
        hid1 = scratch(3328, T)
        hid2 = scratch(3840, T)
        lam_rows = scratch(4608, 512).rearrange("p (l n) -> p l n", l=DEPTH)
        fconsts = scratch(5120, nfconsts)
        conv_rt = scratch(7168, BR)
        conv_rs = conv_rt
        ada_rows = scratch(9728, 3 * T)
        ada_raw = [raw[:, 0, :], raw[:, 1, :], raw[:, 2, :], scratch(8192, SLOT)]
        ada_raw += [x[:, 4 * j:4 * j + 4, :].rearrange("p k t -> p (k t)") for j in range(2)]
        silu = scratch(4608, 1024).rearrange("p (b n) -> p b n", b=2)
        act_f = scratch(5632, 512)
        gate_in = scratch(6144, 1024).rearrange("p (b n) -> p b n", b=2)
        rstd_pair = rstd.rearrange("p (o t) -> p o t", o=1).to_broadcast([P, 2, T])
        act_hi = g_hi[:, 0:4, :].rearrange("p (b f) t -> p b f t", b=2)
        act_lo = g_lo[:, 0:4, :].rearrange("p (b f) t -> p b f t", b=2)
        kv_hi, kv_lo = g_hi[:, 4:12, :], g_lo[:, 4:12, :]
        biased = scratch(2048, 4 * SEG).rearrange("p (b h n) -> p b h n", b=2, h=2)
        probs2 = scratch(3584, 4 * SEG).rearrange("p (b h n) -> p b h n", b=2, h=2)
        probs2_t = scratch(5120, 4 * SEG).rearrange("p (b h n) -> p b h n", b=2, h=2)

        def filt(l, name):
            a, b = filter_at[name]
            return fil[64 * l:64 * l + 64, a:b]

        def fconst(name):
            a, b = fconst_at[name]
            return fconsts[:, a:b]

        neg_max = stat[:, 0:8]
        mx = stat[:, 8:16]
        den = stat[:, 16:24]
        rden = stat[:, 24:32]
        head_ss = stat[:, 32:40]
        head_rt = stat[:, 40:48]
        head_rs = stat[:, 48:56]
        ln_sum = stat[:, 64:66]
        ln_ss = stat[:, 66:68]
        ln_rt = stat[:, 68:70]
        ln_rs = stat[:, 70:72]
        dots = stat[:, 72:74]
        dot_exp = stat[:, 74:76]
        lam = stat[:, 76:77]
        wden = stat[:, 80:82]
        rstd_tok = stat[:, 56:58]
        signal = stat[:, 82:84]
        by_layer = stat[:, 84:88].rearrange("p (l n) -> p l n", l=DEPTH)
        neg_lam = by_layer[:, :, 0:1]
        subln_g = by_layer[:, :, 1:2]

        ada_loaded = [sem(f"ada_loaded{j}") for j in range(ADA_TURN)]
        ada_used = sem("ada_used")
        raw_loaded = [sem(f"raw_loaded{r}") for r in range(RING)]
        w_hi_ready = sem("w_hi_ready")
        w_lo_ready = sem("w_lo_ready")
        w_used = sem("w_used")
        consts_loaded = sem("consts_loaded")
        x_loaded = sem("x_loaded")
        ctx_loaded = sem("ctx_loaded")
        layer_loaded = sem("layer_loaded")
        filter_loaded = sem("filter_loaded")
        lam_loaded = sem("lam_loaded")
        ones_ready = sem("ones_ready")
        dve_chain = sem("dve_chain")
        act_chain = sem("act_chain")
        cond_act = sem("cond_act")
        cond_hi = sem("cond_hi")
        cond_ready = sem("cond_ready")
        ada_rows_ready = sem("ada_rows_ready")
        ada_turned = sem("ada_turned")
        ada_taken = sem("ada_taken")
        fil_mm = sem("fil_mm")
        fil_arg = sem("fil_arg")
        fil_sin = sem("fil_sin")
        fil_hw = sem("fil_hw")
        fil_h = sem("fil_h")
        fil_sq = sem("fil_sq")
        fil_rt = sem("fil_rt")
        fil_taken = sem("fil_taken")
        cols_loaded = sem("cols_loaded")
        lam_dots = sem("lam_dots")
        lam_exp = sem("lam_exp")
        src_ready = sem("src_ready")
        sq_ready = sem("sq_ready")
        ms_ready = sem("ms_ready")
        rt_ready = sem("rt_ready")
        norm_v = sem("norm_v")
        norm_hi = sem("norm_hi")
        norm_lo = sem("norm_lo")
        dve_evac = sem("dve_evac")
        ctx_taken = sem("ctx_taken")
        act_evac = sem("act_evac")
        tap_ready = sem("tap_ready")
        rope_in = sem("rope_in")
        rope_rot = sem("rope_rot")
        rope_out = sem("rope_out")
        sc_done = sem("sc_done")
        nm_ready = sem("nm_ready")
        p_ready = sem("p_ready")
        mixw_ready = sem("mixw_ready")
        turned = sem("turned")
        mixw_t_ready = sem("mixw_t_ready")
        pv_done = sem("pv_done")
        head_sq = sem("head_sq")
        head_rt_ready = sem("head_rt_ready")
        head_y_ready = sem("head_y_ready")
        head_t = sem("head_t")
        u_ready = sem("u_ready")
        u_t = sem("u_t")
        u_tok_ready = sem("u_tok_ready")
        dft_done = sem("dft_done")
        yspec_ready = sem("yspec_ready")
        conv_done = sem("conv_done")
        ln_centered = sem("ln_centered")
        ln_rt_ready = sem("ln_rt_ready")
        lnv_ready = sem("lnv_ready")
        mixed = sem("mixed")
        gated_ready = sem("gated_ready")
        merge_free = sem("merge_free")
        merge_added = sem("merge_added")
        sel_ready = sem("sel_ready")
        m_hi = sem("m_hi")
        m_lo = sem("m_lo")
        gu_free = sem("gu_free")
        gate_normed = sem("gate_normed")
        down_done = sem("down_done")
        silu_scaled = sem("silu_scaled")
        rstd_ready = sem("rstd_ready")
        rstd_turned = sem("rstd_turned")
        silu_ready = sem("silu_ready")
        act_raw = sem("act_raw")
        act_hi_ready = sem("act_hi_ready")
        act_ready = sem("act_ready")
        sc2_done = sem("sc2_done")
        nm2_ready = sem("nm2_ready")
        biased_ready = sem("biased_ready")
        p2_ready = sem("p2_ready")
        p2n_ready = sem("p2n_ready")
        turned2 = sem("turned2")
        p2t_ready = sem("p2t_ready")
        pv2_done = sem("pv2_done")
        o2_hi = sem("o2_hi")
        o2_ready = sem("o2_ready")
        qkv_evac = sem("qkv_evac")
        y_ready = sem("y_ready")
        out_ready = sem("out_ready")
        out_stored = sem("out_stored")

        block = ctx.enter_context(nc.Block())

        def at(value, i, per):
            return value if i is None else i * per + value

        def f32(ap):
            return ap.bitcast(F32)

        LAYER_OF = [0, 0, 1]
        ON_CTX = [True, False, False]

        def key_tiles(p):
            return [2, 3] if ON_CTX[p] else [0, 1, 2, 3]

        def sources(p):
            return cx if ON_CTX[p] else x

        ROPE_BASE = [0, 0, 4]
        TAKEN_BASE = [0, 12, 20]

        def taken(p, j):
            if ON_CTX[p]:
                return dve_evac, TAKEN_BASE[p] + j + 1
            if j < 4:
                return rope_in, ROPE_BASE[p] + j + 1
            return dve_evac, TAKEN_BASE[p] + j - 4 + 1

        def act_pairs(p, j):
            return 10 * p + j + 1

        def merged_parts(p):
            return (g_hi, g_lo) if p == 0 else (h_hi, h_lo)

        def NORM_BANK(nid):
            return 0 if nid == 0 else MISC if nid in (8, 10, 12) else 2

        def normed_of(nid_lo):
            return sq_behind if nid_lo == 0 else normed

        def squares_of(nid):
            return sq_behind if nid in (0, 1, 3) else sq

        @block.sync
        def _(sp):
            for turn in range(ADA_TURNS):
                for j in range(ADA_TURN):
                    n = turn * ADA_TURN + j
                    if turn >= 1:
                        sp.wait_ge(ada_used, n - ADA_TURN + 1)
                    sp.dma_start(ada_raw[j], weights[n]).then_inc(ada_loaded[j], 16)

            def load(n, d, i=None, per=RING, dper=RING):
                r = n % RING
                if i is not None:
                    src = weights[bass.ds(i * dper + d, 1)].rearrange("o p n -> (o p) n")
                    sp.wait_ge(w_lo_ready, i * per + (n - RING + 1))
                else:
                    src = weights[d]
                    if n >= RING:
                        sp.wait_ge(w_lo_ready, n - RING + 1)
                    else:
                        sp.wait_ge(ada_used, ADA_SLOTS - ADA_TURN + n + 1)
                sp.dma_start(raw[:, r, :], src).then_inc(raw_loaded[r], 16)

            for n0, d0, count in stretches:
                if d0 is None:
                    dm, da = dram_pass[0] + MERGE_AT, dram_pass[1] - ADA_SLOTS
                    with sp.Fori(0, 4) as i:
                        for b in range(3):
                            load(n0 + 5 * b, da + 2 * b, i, MERGE_TURN, ADA_TURN)
                            load(n0 + 5 * b + 1, dm + 3 * b, i, MERGE_TURN, 9)
                            load(n0 + 5 * b + 2, da + 2 * b + 1, i, MERGE_TURN, ADA_TURN)
                            load(n0 + 5 * b + 3, dm + 3 * b + 1, i, MERGE_TURN, 9)
                            load(n0 + 5 * b + 4, dm + 3 * b + 2, i, MERGE_TURN, 9)
                    continue
                first = RING if n0 == 0 else 0
                for j in range(first):
                    load(n0 + j, d0 + j)
                turns_ = (count - first) // RING
                if turns_ > 1:
                    with sp.Fori(0, turns_) as i:
                        for j in range(RING):
                            load(n0 + first + j, d0 + first + j, i)
                    first += turns_ * RING
                for j in range(first, count):
                    load(n0 + j, d0 + j)

        @block.gpsimd
        def _(pool):
            pool.dma_start(cols[:, :], cols_in).then_inc(cols_loaded, 16)
            pool.dma_start(fil, filter_in).then_inc(filter_loaded, 16)
            pool.dma_start(fconsts, filter_consts_in).then_inc(filter_loaded, 16)
            pool.wait_ge(ada_used, ADA_TURN)
            pool.dma_start(consts[:, :], consts_in).then_inc(consts_loaded, 16)
            for l in range(DEPTH):
                pool.dma_start(lam_rows[:, l, :], lam_in[l]).then_inc(lam_loaded, 16)
            pool.wait_ge(ada_used, 2 * ADA_TURN)
            pool.dma_start(cx[:, :, :], ctx_in).then_inc(ctx_loaded, 16)
            pool.wait_ge(ada_used, ADA_SLOTS)
            pool.dma_start(x[:, :, :], x_in).then_inc(x_loaded, 16)
            pool.dma_start(layer[:, :], layer_in[0]).then_inc(layer_loaded, 16)
            pool.wait_ge(src_ready, 16)
            pool.dma_start(layer[:, :], layer_in[1]).then_inc(layer_loaded, 16)
            for half in range(2):
                s = slice(4 * half, 4 * half + 4)
                pool.wait_ge(out_ready, 4 * half + 4)
                pool.dma_start(out[:, s, :], normed[:, s, :]).then_inc(out_stored, 16)
            pool.wait_ge(out_stored, 32)

        @block.tensor
        def _(pe):
            def mm3(dst, hi, lo, m_hi_, m_lo_, first, last, **kw):
                pe.matmul(dst, hi, m_hi_, start=first, stop=False, **kw)
                pe.matmul(dst, hi, m_lo_, start=False, stop=False, **kw)
                return pe.matmul(dst, lo, m_hi_, start=False, stop=last, **kw)

            def slot_ready(c, i, per):
                pe.wait_ge(w_lo_ready, at(c + 1, i, per))

            def project(c, dst, i=None, per=0, tiles=None, hi=h_hi, lo=h_lo, nk=KD):
                slot_ready(c, i, per)
                r = c % RING
                for kk in range(nk):
                    if tiles is not None:
                        pe.wait_ge(*tiles(kk))
                    w = slice(kk * P, kk * P + P)
                    mm = mm3(dst, w_hi[:, r, w], w_lo[:, r, w], hi[:, kk, :], lo[:, kk, :],
                             kk == 0, kk == nk - 1)
                mm.then_inc(w_used, 1)

            def pair(c, bank, i=None, per=0, tiles=None, hi=h_hi, lo=h_lo):
                project(c, PS[:, bank, 0:T], i, per, tiles, hi, lo)
                project(c + 1, PS[:, bank, T:2 * T], i, per, None, hi, lo)

            def token_pair(c, bank, hi=h_hi, lo=h_lo, tiles=None):
                for half in range(2):
                    slot_ready(c + half, None, 0)
                    r = (c + half) % RING
                    for t in range(TT):
                        tok = slice(t * P, t * P + P)
                        for j in range(4):
                            kk, w = 4 * half + j, slice(j * T, (j + 1) * T)
                            if tiles is not None and t == 0:
                                pe.wait_ge(*tiles(kk))
                            mm = mm3(PS[:, bank, t * T:(t + 1) * T], hi[:, kk, tok], lo[:, kk, tok], w_hi[:, r, w], w_lo[:, r, w],
                                     kk == 0 and t == 0, kk == KD - 1, skip_group_check=True)
                    mm.then_inc(w_used, 1)

            def norm_part(nid, c):
                pe.wait_ge(sq_ready, 4 * MS_ORDER.index(nid) + c + 1)
                for kk in (2 * c, 2 * c + 1):
                    mm = pe.matmul(PS[:, NORM_BANK(nid), 0:T], ones[:, :], squares_of(nid)[:, kk, :], start=(kk == 0),
                                   stop=(kk == KD - 1))
                if c == 3:
                    mm.then_inc(ms_ready, 1)

            def norm(nid):
                for c in range(4):
                    norm_part(nid, c)

            def normed_tiles(nid_lo):
                return lambda kk: (norm_lo, KD * nid_lo + kk + 1)

            def ada(c, m, half, i):
                if half == 0 and m == 1:
                    pe.wait_ge(ada_taken, at(ADA_TURNS, i, 1))
                if half == 0 and m == 2:
                    pe.wait_ge(ada_rows_ready, at(3 * ADA_TURNS + 1, i, 3))
                dst = PS[0:4, 6 + m % 2, 0:T]
                slot_ready(c, i, MERGE_TURN)
                r = c % RING
                for j in range(4):
                    kk, w = 4 * half + j, slice(j * T, (j + 1) * T)
                    pe.matmul(dst, c_parts[:, kk, :], w_hi[:, r, w], start=(kk == 0), stop=False)
                    mm = pe.matmul(dst, c_parts[:, kk, :], w_lo[:, r, w], start=False, stop=(kk == KD - 1))
                mm.then_inc(w_used, 1)

            def ada_turn(turn, bank, i=None):
                rows = 2 if i is None else 4
                pe.wait_ge(ada_rows_ready, at(3 * turn + 3, i, 3))
                for j in range(6):
                    mm = pe.matmul(PS[:, bank, 2 * j:2 * j + 2], ada_rows[0:rows, j * P:(j + 1) * P],
                                   col("ada_sum", 0, 2)[0:rows, :],
                                   start=True, stop=True)
                mm.then_inc(ada_turned, 1)

            def modulation(turn):
                for m in range(3):
                    if m == 1 and turn > 0:
                        pe.wait_ge(ada_taken, turn)
                    if m == 2:
                        pe.wait_ge(ada_rows_ready, 3 * turn + 1)
                    for half in range(2):
                        pe.wait_ge(ada_loaded[2 * m + half], 16 * (turn + 1))
                        for j in range(4):
                            kk = 4 * half + j
                            mm = pe.matmul(PS[0:2, m % 2, 0:T], c_act[:, 2 * kk:2 * kk + 2],
                                           ada_raw[2 * m + half][:, j * T:(j + 1) * T], start=(kk == 0), stop=(kk == KD - 1))
                        mm.then_inc(ada_used, 1)

            def filter_hidden(n):
                for l in range(DEPTH):
                    rows = slice(64 * l, 64 * l + 64)
                    if n == 0:
                        lhs, rhs = filt(l, "w1"), fconst("filter_z")[rows, :]
                    else:
                        pe.wait_ge(fil_sin, 1)
                        lhs, rhs = filt(l, "w2"), hid1[rows, :]
                    mm = pe.matmul(PS[rows, 2 + n, 0:T], lhs, rhs, start=True, stop=True)
                mm.then_inc(fil_mm, 1)

            def filter_taps(l):
                pe.wait_ge(fil_sin, 2)
                if l == 1:
                    pe.wait_ge(fil_taken, 1)
                for d in range(2):
                    for t in range(TT):
                        mm = pe.matmul(PS[:, 4 + 2 * d + t, :], hid2[64 * l:64 * l + 64, t * P:(t + 1) * P],
                                       filt(l, "w3")[:, d * BR:(d + 1) * BR], start=True, stop=True)
                mm.then_inc(fil_mm, 1)

            def filter_energy(l):
                pe.wait_ge(fil_sq, l + 1)
                for n, (d, t) in enumerate([(0, 0), (0, 1), (1, 0), (1, 1)]):
                    mm = pe.matmul(PS[:, 2, :], ones[:, :], h_sq[:, d, t, :], start=(n == 0), stop=(n == 3))
                mm.then_inc(fil_mm, 1)

            def filter_spectrum(l):
                pe.wait_ge(fil_h, l + 1)
                dft_c = const("dft_cos").rearrange("p (t f) -> p t f", t=TT)
                dft_s = fconst("dft_sin_k").rearrange("p (t f) -> p t f", t=TT)
                dft_n = fconst("dft_nyq").rearrange("p (t f) -> p t f", t=TT)
                for f in range(2):
                    for t in range(TT):
                        pe.matmul(PS[:, 4 + f, :], dft_c[:, t, f * P:(f + 1) * P], h_sum[:, t, :],
                                  start=(t == 0), stop=(t == 1))
                for f in range(2):
                    for t in range(TT):
                        pe.matmul(PS[:, 6 + f, :], dft_s[:, t, f * P:(f + 1) * P], h_dif[:, t, :],
                                  start=(t == 0), stop=(t == 1))
                for t in range(TT):
                    mm = pe.matmul(PS[:, 3, :], dft_n[:, t, :], h_sum[:, t, :], start=(t == 0), stop=(t == 1))
                mm.then_inc(fil_mm, 1)

            def rotate(n, perm):
                pe.wait_ge(rope_in, n + 1)
                if n >= 1:
                    pe.wait_ge(rope_out, n)
                pe.matmul(PS[:, MISC, :], const(perm), rope_raw[:, n % 2, :], start=True,
                          stop=True).then_inc(rope_rot, 1)

            def scores(p, n):
                h, qt = n // 2, n % 2
                if n >= 1:
                    pe.wait_ge(p_ready, 8 * p + n)
                kt = key_tiles(p)
                for m in range(2):
                    s = slice(SUB * m, SUB * m + SUB)
                    for g in range(len(kt) // 2):
                        base = 0 if kt[2 * g] == 0 else 4
                        mm = pe.matmul(PS[:, SCORES + m, g * T:(g + 1) * T], q[s, h, qt * P:(qt + 1) * P],
                                       k[s, base + h, :], start=True, stop=True)
                mm.then_inc(sc_done, 1)

            def turn(p, n):
                pe.wait_ge(mixw_ready, 8 * p + n + 1)
                if n >= 1:
                    pe.wait_ge(mixw_t_ready, 8 * p + n)
                for j in range(len(key_tiles(p))):
                    mm = pe.transpose(PS[:, TURN, j * P:(j + 1) * P], mixw[:, j * P:(j + 1) * P], const("ident"))
                mm.then_inc(turned, 1)

            def values(p, n):
                h, qt = n // 2, n % 2
                pe.wait_ge(mixw_t_ready, 8 * p + n + 1)
                if n == 0:
                    pe.wait_ge(*taken(p, 5))
                kt = key_tiles(p)
                for j, t in enumerate(kt):
                    mm = pe.matmul(PS[:, HEADS_OUT + qt, h * P:(h + 1) * P], mixw_t[:, h % 2, j, qt * P:(qt + 1) * P],
                                   v[:, t, h * P:(h + 1) * P], start=(j == 0), stop=(j == len(kt) - 1))
                mm.then_inc(pv_done, 1)

            def keys_queries(p, nid_lo, behind_second=None):
                c0 = start[f"pass{p}"]
                on_x = not ON_CTX[p]
                rb = ROPE_BASE[p]
                for j in range(4):
                    if j >= 2:
                        pe.wait_ge(*taken(p, j - 2))
                    pair(c0 + 2 * j, j % 2, tiles=normed_tiles(nid_lo) if j == 0 else None)
                    if on_x and j >= 1:
                        rotate(rb + j - 1, "perm_a")
                    if j == 1 and behind_second is not None:
                        norm(behind_second)
                pe.wait_ge(*taken(p, 2))
                token_pair(c0 + part["v"], 0)
                if on_x:
                    rotate(rb + 3, "perm_a")

            def run_pass(p):
                c0 = start[f"pass{p}"]
                on_x = not ON_CTX[p]
                rb = ROPE_BASE[p]
                for n in range(8):
                    if p == 2 and n == 0:
                        pe.wait_ge(ctx_taken, 4)
                    if n % 4 == 0:
                        if on_x:
                            pe.wait_ge(rope_out, rb + 2 + n // 2)
                        else:
                            pe.wait_ge(*taken(p, 1 + n // 2))
                    scores(p, n)
                    j = 5 + n
                    pe.wait_ge(*taken(p, j - 2))
                    if j == 5:
                        token_pair(c0 + part["v"] + 2, 1)
                    else:
                        project(c0 + 2 * j, PS[:, j % 2, 0:T])
                        values(p, n - 1)
                        project(c0 + 2 * j + 1, PS[:, j % 2, T:2 * T])
                    turn(p, n)
                pe.wait_ge(*taken(p, 11))
                pair(c0 + part["gu"] + 2, 1)
                values(p, 7)
                pe.wait_ge(u_ready, p + 1)
                for t in range(TT):
                    for c in range(KB):
                        mm = pe.transpose(PS[:, [TURN, MISC][t], c * P:(c + 1) * P], u[:, c, t * P:(t + 1) * P],
                                          const("ident"))
                mm.then_inc(u_t, 1)
                pe.wait_ge(p_ready, 8 * (p + 1))
                token_pair(c0 + part["gv"], 2)
                pe.wait_ge(u_tok_ready, p + 1)
                pe.wait_ge(act_evac, act_pairs(p, 1))
                pe.wait_ge(head_y_ready, p + 1)
                for n, name in enumerate(("dft_cos", "dft_sin_u")):
                    dft = const(name).rearrange("p (t f) -> p t f", t=TT)
                    for f in range(2):
                        for t in range(TT):
                            mm = pe.matmul(PS[:, [0, HEADS_OUT][n] + f, :], dft[:, t, f * P:(f + 1) * P],
                                           u_tok[:, t, :], start=(t == 0), stop=(t == 1))
                mm.then_inc(dft_done, 1)
                token_pair(c0 + part["gv"] + 2, 3)
                for h in range(HEADS_A):
                    for qt in range(TT):
                        mm = pe.transpose(PS[:, [TURN, MISC][h // 2], (h % 2) * T + qt * P:(h % 2) * T + (qt + 1) * P],
                                          head_y[:, h, qt, :], const("ident"))
                mm.then_inc(head_t, 1)
                for j in range(2):
                    pe.wait_ge(act_evac, act_pairs(p, 2 + j))
                    pair(c0 + part["ga"] + 2 * j, 2 + j)
                pe.wait_ge(yspec_ready, p + 1)
                pe.wait_ge(y_ready, p + 1)
                idft = const("idft").rearrange("p (a t) -> p a t", a=4)
                for c in range(KB):
                    for a_ in range(4):
                        mm = pe.matmul(PS[:, [TURN, MISC][c // 2], (c % 2) * T:(c % 2 + 1) * T],
                                       yspec[:, a_, c * P:(c + 1) * P], idft[:, a_, :], start=(a_ == 0), stop=(a_ == 3))
                mm.then_inc(conv_done, 1)
                for j in range(2):
                    pair(c0 + part["gb"] + 2 * j, j)
                pe.wait_ge(lnv_ready, p + 1)
                pe.wait_ge(layer_loaded, 16 * (LAYER_OF[p] + 1))
                pe.wait_ge(act_evac, act_pairs(p, 5))
                mixw_g = row("mix_w").rearrange("p (g t) -> p g t", g=8)
                for g in range(8):
                    for c in range(TT):
                        o = SUB * (g % 2)
                        f = (g // 2) * T + c * P
                        mm = pe.matmul(PS[o:o + SUB, SCORES + f // 512, f % 512:f % 512 + P],
                                       lnv[:, c, g * SUB:(g + 1) * SUB], mixw_g[:, g, :], start=True, stop=True)
                mm.then_inc(mixed, 1)
                for j in range(2):
                    pe.wait_ge(act_evac, act_pairs(p, 6 + j))
                    pair(c0 + part["gc"] + 2 * j, j)
                pe.wait_ge(act_evac, act_pairs(p, 9))
                each, per = (5, MERGE_TURN) if p == 1 else (3, 9)
                with pe.Fori(0, 4) as i:
                    for b in range(3):
                        c = start[f"pass{p}_merge"] + each * b
                        if p == 1:
                            ada(c, b, 0, i)
                            c += 1
                        pe.wait_ge(merge_free, i * 3 + (15 * p + b + 1))
                        slot_ready(c, i, per)
                        r = c % RING
                        for o in range(2):
                            for kk in range(KB):
                                w = slice(kk * T + o * P, kk * T + (o + 1) * P)
                                mm = mm3(PS[:, 2 * b, o * T:(o + 1) * T], w_hi[:, r, w], w_lo[:, r, w],
                                         g_hi[:, KB * b + kk, :], g_lo[:, KB * b + kk, :], kk == 0, kk == KB - 1)
                        mm.then_inc(w_used, 1)
                        if p == 1:
                            ada(c + 1, b, 1, i)
                            c += 1
                        pair(c + 1, 2 * b + 1, i, per)
                    if p == 1:
                        ada_turn(ADA_TURNS, 7, i)

            def branch_sum(p, j):
                if j >= 2:
                    pe.wait_ge(src_ready, 4 * OUT_EVENT[p] + j - 1)
                hi, lo = merged_parts(p)
                pair(start[f"pass{p}_wo"] + 2 * j, 4 + j % 2,
                     tiles=(lambda kk: (m_lo, KD * p + kk + 1)) if j == 0 else None, hi=hi, lo=lo)

            def ctx_keys(j, nid_lo):
                pair(start["ctx_k"] + 2 * j, j, tiles=normed_tiles(nid_lo) if j == 0 else None, hi=g_hi, lo=g_lo)

            def ctx_values(j):
                pe.wait_ge(src_ready, 4 * OUT_EVENT[1] + 3 + j)
                token_pair(start["ctx_v"] + 2 * j, 4 + j, g_hi, g_lo)

            def down(c, s, f, i, per, last):
                slot_ready(c, i, per)
                r = c % RING
                for o in range(KD):
                    w = slice(o * P, o * P + P)
                    mm = mm3(PS[:, 4 + o // 2, (o % 2) * T:(o % 2 + 1) * T], w_hi[:, r, w], w_lo[:, r, w],
                             act_hi[:, s, f, :], act_lo[:, s, f, :], False, last, skip_group_check=True)
                    if last and f == 1 and o in (1, 3, 5):
                        mm.then_inc(down_done, 1)
                mm.then_inc(w_used, 1)

            def ffn(n, nid_lo, nid=None):
                c0 = start[f"ffn{n}"]

                def gate_up(c, s, i, base, tiles=None):
                    pe.wait_ge(gu_free, base if i is None else i * 2 + base)
                    pair(c, 2 * s, i, 12, tiles)
                    pair(c + 2, 2 * s + 1, i, 12)

                def downs(c, s, i, base, last=False):
                    pe.wait_ge(act_ready, base if i is None else i * 2 + base)
                    for f in range(2):
                        down(c + f, s, f, i, 12, last)

                g, a_ = 13 * n, FPAIRS * n
                pe.wait_ge(gu_free, g + 1)
                pair(c0, 0, None, 12, normed_tiles(nid_lo))
                if nid is not None:
                    norm(nid)
                for b in range(4):
                    pe.matmul(PS[:, 4 + b, :], zeros[:, :], zeros[:, 0:1].to_broadcast([P, 512]), start=True, stop=False,
                              skip_group_check=True)
                pair(c0 + 2, 1, None, 12)
                if nid is not None:
                    pe.wait_ge(rt_ready, MS_ORDER.index(nid) + 1)
                with pe.Fori(0, 4) as i:
                    for e in range(2):
                        c = c0 + 4 + 6 * e
                        gate_up(c, (1 + e) % 2, i, g + 2 + e)
                        downs(c + 4, e % 2, i, a_ + 1 + e)
                for pr in (9, 10):
                    c = c0 + 4 + 6 * (pr - 1)
                    gate_up(c, pr % 2, None, g + pr + 1)
                    downs(c + 4, (pr - 1) % 2, None, a_ + pr)
                downs(c0 + FFN_SLOTS - 2, 10 % 2, None, a_ + 11, True)

            def scores2(n, unit):
                if unit >= 1:
                    pe.wait_ge(biased_ready, 8 * n + unit)
                for h in range(2):
                    s = slice(HD * h, HD * h + HD)
                    pe.matmul(PS[:, SCORES + h, 0:P], q[s, unit, 0:P], k[s, unit, 0:P], start=True, stop=True)
                    mm = pe.matmul(PS[:, SCORES + h, P:SEG], q[s, unit, P:T], k[s, unit, :], start=True, stop=True)
                mm.then_inc(sc2_done, 1)

            def turn2(n, unit):
                pe.wait_ge(p2n_ready, 8 * n + unit + 1)
                if unit >= 1 or n >= 1:
                    pe.wait_ge(p2t_ready, 8 * n + unit)
                for h in range(2):
                    for j in range(3):
                        mm = pe.transpose(PS[:, TURN + h, j * P:(j + 1) * P], probs2[:, unit % 2, h, j * P:(j + 1) * P],
                                          const("ident"))
                mm.then_inc(turned2, 1)

            def values2(n, unit):
                pe.wait_ge(p2t_ready, 8 * n + unit + 1)
                if unit >= 1 or n >= 1:
                    pe.wait_ge(o2_ready, 8 * n + unit)
                for h in range(2):
                    o, c = HD * h, unit * P + HD * h
                    pe.matmul(PS[o:o + HD, 6, 0:T], v2[:, 0, c:c + HD], probs2_t[:, unit % 2, h, 0:T],
                              start=True, stop=False)
                    mm = pe.matmul(PS[o:o + HD, 6, P:T], v2[:, 1, c:c + HD], probs2_t[:, unit % 2, h, T:SEG],
                                   start=False, stop=True)
                mm.then_inc(pv2_done, 1)

            def projected_tile(c0, n0, tile, nid_lo, nid):
                pr = tile // 2
                if pr >= 2 and tile % 2 == 0:
                    pe.wait_ge(rope_in, n0 + pr - 1)
                project(c0 + tile, PS[:, pr % 2, (tile % 2) * T:(tile % 2 + 1) * T],
                        tiles=normed_tiles(nid_lo) if nid is not None and tile == 0 else None)
                if nid is not None and tile == 0:
                    norm(nid)

            def attention_a(c0, n0):
                for unit in range(-3, 9):
                    ahead, nxt = unit + 3, unit + 2
                    if ahead < 8:
                        projected_tile(c0, n0, 2 * ahead, None, None)
                    if 0 <= nxt < 8:
                        rotate(n0 + nxt, "perm_b")
                    if unit >= 1:
                        values2(0, unit - 1)
                    if ahead < 8:
                        projected_tile(c0, n0, 2 * ahead + 1, None, None)
                    if 0 <= nxt < 8:
                        pe.wait_ge(rope_out, n0 + nxt + 1)
                        scores2(0, nxt)
                    if 0 <= unit < 8:
                        turn2(0, unit)

            def attention_b(c0, n0, nid_lo, nid):
                for unit in range(-5, 9):
                    ahead, nxt = unit + 5, unit + 2
                    if ahead < 8:
                        projected_tile(c0, n0, ahead, nid_lo, nid)
                    if 2 <= ahead <= 8 and ahead % 2 == 0:
                        rotate(n0 + ahead // 2 - 1, "perm_b")
                    if unit >= 1:
                        values2(1, unit - 1)
                    if 0 <= nxt < 8:
                        pe.wait_ge(rope_out, n0 + nxt // 2 + 1)
                        scores2(1, nxt)
                    if 0 <= unit < 8:
                        turn2(1, unit)

            def rstd_columns(turn):
                pe.wait_ge(rstd_ready, turn + 1)
                for t in range(TT):
                    mm = pe.matmul(PS[:, 6, t:t + 1], rstd[:, t * P:(t + 1) * P], const("ident")[:, 0:1], start=True, stop=True)
                mm.then_inc(rstd_turned, 1)

            def out_proj(n, event, name):
                c0 = start[name]
                for j in range(4):
                    if j >= 2:
                        pe.wait_ge(src_ready, 4 * event + j - 1)
                    pair(c0 + 2 * j, 4 + j % 2, hi=g_hi, lo=g_lo,
                         tiles=(lambda kk: (o2_ready, 8 * n + kk + 1)) if j == 0 else None)

            pe.wait_ge(ones_ready, 1)
            pe.wait_ge(cond_ready, 1)
            modulation(0)
            pe.wait_ge(filter_loaded, 32)
            filter_hidden(0)
            ada_turn(0, 1)
            modulation(1)
            filter_hidden(1)
            ada_turn(1, 1)
            modulation(2)
            filter_taps(0)
            ada_turn(2, 1)
            modulation(3)
            pe.wait_ge(consts_loaded, 16)
            filter_energy(0)
            filter_spectrum(0)
            ada_turn(3, 1)
            norm(0)
            filter_taps(1)
            filter_energy(1)
            filter_spectrum(1)
            keys_queries(0, 0)
            run_pass(0)
            branch_sum(0, 0)
            norm(2)
            for j in range(1, 4):
                branch_sum(0, j)
            keys_queries(1, 1, behind_second=1)
            run_pass(1)
            branch_sum(1, 0)
            norm(4)
            for j in range(1, 4):
                branch_sum(1, j)
            ctx_keys(0, 2)
            norm(3)
            ctx_keys(1, 2)
            ctx_values(0)
            norm(5)
            ctx_values(1)
            keys_queries(2, 3)
            run_pass(2)
            for j in range(4):
                branch_sum(2, j)
                if j >= 1:
                    norm_part(6, j - 1)
            norm_part(6, 3)
            ffn(0, 4, 7)
            for j in range(4):
                token_pair(start["vqk0"] + 2 * j, j, tiles=normed_tiles(5) if j == 0 else None)
                if j == 0:
                    norm(8)
                if j == 1:
                    rstd_columns(0)
            pe.wait_ge(qkv_evac, 4)
            attention_a(start["vqk0"] + 8, 8)
            out_proj(0, 7, "wo0")
            ffn(1, 6, 9)
            for j in range(4):
                pair(start["kv"] + 2 * j, j, tiles=normed_tiles(7) if j == 0 else None, hi=kv_hi, lo=kv_lo)
                if j == 0:
                    norm(10)
                if j == 1:
                    rstd_columns(1)
                if j >= 1:
                    rotate(16 + j - 1, "perm_b")
            for j in range(4):
                pe.wait_ge(rope_in, 16 + j + 1)
                token_pair(start["kv"] + 8 + 2 * j, j, kv_hi, kv_lo)
                if j == 0:
                    rotate(19, "perm_b")
            ffn(2, 8)
            attention_b(start["q1"], 20, 9, 12)
            out_proj(1, 10, "wo1")
            ffn(3, 10, 13)
            norm(14)

        @block.scalar
        def _(act):
            chain = [0]

            def link(ins):
                chain[0] += 1
                ins.then_inc(act_chain, 1)
                act.wait_ge(act_chain, chain[0])

            def split(c, i=None, per=0):
                if i is None and c >= TOTAL:
                    return
                r = c % RING
                if i is None:
                    act.wait_ge(raw_loaded[r], 16 * (c // RING + 1))
                    if c >= RING:
                        act.wait_ge(w_used, c - RING + 1)
                else:
                    act.wait_ge(raw_loaded[r], i * (16 * per // RING) + 16 * (c // RING + 1))
                    act.wait_ge(w_used, i * per + (c - RING + 1))
                nc.scalar.activation(w_hi[:, r, :], raw[:, r, :], ACT.Copy).then_inc(w_hi_ready, 1)

            def splits(c, n=2):
                for j in range(n):
                    split(c + j + RING)

            def square(nid, src, event, c):
                if event is None:
                    act.wait_ge(ctx_loaded if src is cx else x_loaded, 16)
                else:
                    act.wait_ge(src_ready, 4 * event + c + 1)
                nc.scalar.activation(squares_of(nid)[:, 2 * c:2 * c + 2, :], src[:, 2 * c:2 * c + 2, :],
                                     ACT.Square).then_inc(sq_ready, 1)

            def squares(nid, src, event=None):
                for c in range(4):
                    square(nid, src, event, c)

            def root(nid):
                act.wait_ge(ms_ready, MS_ORDER.index(nid) + 1)
                nc.scalar.activation(rt, PS[:, NORM_BANK(nid), 0:T], ACT.Sqrt, bias=eps[:, 0:1]).then_inc(rt_ready, 1)

            def norm(nid, src, event=None):
                squares(nid, src, event)
                root(nid)

            def high(nid_lo, shift, hi=h_hi, first=0, end=KD):
                for kk in range(first, end):
                    act.wait_ge(norm_v, KD * nid_lo + kk + 1)
                    nc.scalar.activation(hi[:, kk, :], normed_of(nid_lo)[:, kk, :], ACT.Identity,
                                         bias=shift(kk)).then_inc(norm_hi, 1)

            def ctx_keys(j):
                c = start["ctx_k"] + 2 * j
                split(c + RING)
                act.wait_ge(w_used, c + 2)
                nc.scalar.activation(k[:, 4 + 2 * j:6 + 2 * j, :], PS[:, j, :].rearrange("p (k t) -> p k t", k=2),
                                     ACT.Copy).then_inc(ctx_taken, 1)
                split(c + 1 + RING)

            def ctx_values(j, split_off=0):
                c = start["ctx_v"] + 2 * j
                if not split_off:
                    split(c + RING)
                act.wait_ge(w_used, c + 2)
                nc.scalar.activation(v[:, 2:4, j * T:(j + 1) * T], PS[:, 4 + j, :].rearrange("p (t c) -> p t c", t=TT),
                                     ACT.Copy).then_inc(ctx_taken, 1)
                split(c + 1 + RING)

            def sums_and_norm(p, nid, nid_lo, shift, hi=h_hi):
                c = start[f"pass{p}_wo"]
                for j in range(4):
                    splits(c + 2 * j)
                    if j == 0:
                        root(nid)
                    if j < 3:
                        high(nid_lo, shift, hi, *BEHIND_SUMS[j])

            def sines(n):
                act.wait_ge(fil_arg, n + 1)
                nc.scalar.activation((hid1, hid2)[n], arg, ACT.Sin).then_inc(fil_sin, 1)

            def tap_squares(l):
                act.wait_ge(fil_hw, l + 1)
                nc.scalar.activation(h_sq[:, :, :, :], hw[:, :, :, :], ACT.Square).then_inc(fil_sq, 1)

            def tap_roots(l):
                act.wait_ge(fil_mm, [4, 7][l])
                nc.scalar.activation(conv_rt, PS[:, 2, :], ACT.Sqrt, scale=float(D)).then_inc(fil_rt, 1)

            def lambdas():
                for l in range(DEPTH):
                    act.wait_ge(lam_dots, l + 1)
                    nc.scalar.activation(dot_exp, dots, ACT.Exp).then_inc(lam_exp, 1)

            def exps(p, n):
                nk = P * len(key_tiles(p))
                act.wait_ge(nm_ready, 8 * p + n + 1)
                for m in range(2):
                    ins = nc.scalar.activation(probs[:, m, 0:nk], PS[:, SCORES + m, 0:nk], ACT.Exp,
                                               bias=neg_max[:, m:m + 1], scale=SUB ** -0.5,
                                               accum_out=den[:, m:m + 1])
                ins.then_inc(p_ready, 1)

            def head_squares(p, n):
                h, qt = n // 2, n % 2
                act.wait_ge(pv_done, 8 * p + n + 1)
                ins = nc.scalar.activation(squared[:, n, :], PS[:, HEADS_OUT + qt, h * P:(h + 1) * P], ACT.Square,
                                           accum_out=head_ss[:, 2 * h + qt:2 * h + qt + 1])
                if n == 7:
                    link(ins)

            def taps(p, j):
                l = LAYER_OF[p]
                act.wait_ge(w_used, start[f"pass{p}"] + part["hy"] + 2 * j + 2)
                for a_ in range(2):
                    f = 2 * j + a_
                    ins = nc.scalar.activation(hy[:, f, :], PS[:, j % 2, a_ * T:(a_ + 1) * T], ACT.Identity,
                                               scale=col(f"short_w{l}", 12 + f), bias=col(f"short_b{l}", f))
                ins.then_inc(tap_ready, 1)

            def take_turned(p, n):
                h, qt = n // 2, n % 2
                nt = len(key_tiles(p))
                act.wait_ge(turned, 8 * p + n + 1)
                nc.scalar.activation(mixw_t[:, h % 2, 0:nt, qt * P:(qt + 1) * P],
                                     PS[:, TURN, 0:nt * P].rearrange("p (k t) -> p k t", k=nt),
                                     ACT.Copy).then_inc(mixw_t_ready, 1)

            def keys_queries(p, behind_second=None, src=None, event=None):
                c0 = start[f"pass{p}"]
                splits(c0)
                if behind_second is not None:
                    squares(behind_second, src, event)
                splits(c0 + 2)
                if behind_second is not None:
                    root(behind_second)
                splits(c0 + 4, 4)
                splits(c0 + part["v"])

            def run_pass(p):
                c0 = start[f"pass{p}"]
                for n in range(8):
                    if n >= 2:
                        taps(p, n - 2)
                    exps(p, n)
                    splits(c0 + part["v"] + 2 + 2 * n)
                    take_turned(p, n)
                    if n >= 1:
                        head_squares(p, n - 1)
                splits(c0 + part["gu"] + 2)
                head_squares(p, 7)
                nc.scalar.activation(head_rt, head_ss, ACT.Sqrt, scale=1.0 / P,
                                     bias=eps[:, 0:1]).then_inc(head_rt_ready, 1)
                for j in range(2):
                    act.wait_ge(w_used, c0 + part["gu"] + 2 * j + 2)
                    nc.scalar.activation(gu[:, 2 * j:2 * j + 2, :], PS[:, j, :], ACT.Gelu).then_inc(act_evac, 1)
                for j in range(2):
                    split(c0 + part["gv"] + 2 * j + RING)
                    act.wait_ge(w_used, c0 + part["gv"] + 2 * j + 2)
                    nc.scalar.activation(gv[:, :, j * T:(j + 1) * T], PS[:, 2 + j, :].rearrange("p (t c) -> p t c", t=TT),
                                         ACT.Gelu).then_inc(act_evac, 1)
                    split(c0 + part["gv"] + 2 * j + 1 + RING)

                def gates(name, b, bank=0):
                    for j in range(2):
                        c = c0 + part[name] + 2 * j
                        split(c + RING)
                        act.wait_ge(w_used, c + 2)
                        if b >= 1:
                            act.wait_ge(gated_ready, 6 * p + 2 * (b - 1) + j + 1)
                        nc.scalar.activation(gate_act[:, j, :], PS[:, bank + j, :], ACT.Silu).then_inc(act_evac, 1)
                        if (b, j) != (2, 1):
                            split(c + 1 + RING)

                gates("ga", 0, 2)
                act.wait_ge(ln_centered, p + 1)
                for t in range(TT):
                    ins = nc.scalar.activation(lnv[:, t, :], gvc[:, t, :], ACT.Square,
                                               accum_out=ln_ss[:, t:t + 1])
                link(ins)
                nc.scalar.activation(ln_rt, ln_ss, ACT.Sqrt, scale=1.0 / BR,
                                     bias=eps[:, 0:1]).then_inc(ln_rt_ready, 1)
                gates("gb", 1)
                gates("gc", 2)
                each, per = (5, MERGE_TURN) if p == 1 else (3, 9)
                with act.Fori(0, 4) as i:
                    for b in range(3):
                        c = start[f"pass{p}_merge"] + each * b
                        for j in range(-1, each - 1):
                            split(c + j + RING, i, per)
                        act.wait_ge(merge_free, i * 3 + (15 * p + b + 1))
                        act.wait_ge(w_used, i * per + (c + each))
                        nc.scalar.activation(sel[:, b, :], PS[:, 2 * b + 1, :], ACT.Sigmoid).then_inc(sel_ready, 1)
                end = start[f"pass{p}_wo"]
                act.wait_ge(w_used, end)
                for kk in range(KD):
                    act.wait_ge(merge_added, 8 * p + 2 * (kk // 2) + 2)
                    nc.scalar.activation(merged_parts(p)[0][:, kk, :], merged[:, kk, :], ACT.Copy).then_inc(m_hi, 1)
                    if kk == 1:
                        split(end - 1 + RING)
                act.wait_ge(m_lo, KD * (p + 1))

            def ffn(n, nid=None):
                c0 = start[f"ffn{n}"]

                def post(c, s, i, base, sbase, nid=None):
                    split(c + RING, i, 12)
                    split(c + 1 + RING, i, 12)
                    if nid is not None:
                        root(nid)
                    act.wait_ge(gu_free, at(base, i, 2))
                    act.wait_ge(gate_normed, at(sbase, i, 2))
                    nc.scalar.activation(silu[:, s, :], gate_in[:, s, :], ACT.Silu).then_inc(silu_ready, 1)
                    split(c + 2 + RING, i, 12)
                    split(c + 3 + RING, i, 12)

                def downs(c, i):
                    for f in range(2):
                        split(c + f + RING, i, 12)

                g, a_ = 13 * n, FPAIRS * n
                post(c0, 0, None, g + 1, a_ + 1, nid)
                with act.Fori(0, 4) as i:
                    for e in range(2):
                        c = c0 + 4 + 6 * e
                        post(c, (1 + e) % 2, i, g + 2 + e, a_ + 2 + e)
                        downs(c + 4, i)
                for pr in (9, 10):
                    c = c0 + 4 + 6 * (pr - 1)
                    post(c, pr % 2, None, g + pr + 1, a_ + pr + 1)
                    downs(c + 4, None)
                split(c0 + FFN_SLOTS - 2 + RING)

            def exps2(n, unit):
                b = unit % 2
                act.wait_ge(nm2_ready, 8 * n + unit + 1)
                for h in range(2):
                    m = 4 * b + h
                    nc.scalar.activation(probs2[:, b, h, 0:P], biased[:, b, h, 0:P], ACT.Exp,
                                         bias=neg_max[:, m:m + 1], accum_out=den[:, m:m + 1])
                    ins = nc.scalar.activation(probs2[:, b, h, P:SEG], biased[:, b, h, P:SEG], ACT.Exp,
                                               bias=neg_max[:, m + 2:m + 3], accum_out=den[:, m + 2:m + 3])
                ins.then_inc(p2_ready, 1)

            def take_turned2(n, unit):
                act.wait_ge(turned2, 8 * n + unit + 1)
                nc.scalar.activation(probs2_t[:, unit % 2, :, :], PS[:, TURN:TURN + 2, 0:SEG], ACT.Copy).then_inc(p2t_ready, 1)

            def heads_high(n, unit):
                act.wait_ge(pv2_done, 8 * n + unit + 1)
                nc.scalar.activation(g_hi[:, unit, :], PS[:, 6, 0:T], ACT.Copy).then_inc(o2_hi, 1)

            def attention_a(c0):
                for unit in range(-3, 9):
                    ahead, nxt = unit + 3, unit + 1
                    if 1 <= ahead <= 8:
                        split(c0 + 2 * ahead - 1 + RING)
                    if 0 <= nxt < 8:
                        exps2(0, nxt)
                    if ahead < 8:
                        split(c0 + 2 * ahead + RING)
                    if unit >= 1:
                        heads_high(0, unit - 1)
                    if 0 <= unit < 8:
                        take_turned2(0, unit)

            def attention_b(c0):
                for unit in range(-5, 9):
                    ahead, nxt = unit + 5, unit + 1
                    if ahead < 8:
                        split(c0 + ahead + RING)
                    if unit >= 1:
                        heads_high(1, unit - 1)
                    if 0 <= nxt < 8:
                        exps2(1, nxt)
                    if 0 <= unit < 8:
                        take_turned2(1, unit)

            def gained(nid_lo, event, gains, nid, ahead=None, behind=None, hi=h_hi):
                for j in range(4):
                    if ahead is not None:
                        split(ahead[j] + RING)
                    act.wait_ge(src_ready, 4 * event + j + 1)
                    for kk in (2 * j, 2 * j + 1):
                        nc.scalar.activation(hi[:, kk, :], x[:, kk, :], ACT.Copy, scale=col(gains, kk)).then_inc(norm_hi, 1)
                    if behind is not None and behind[j] is not None:
                        split(behind[j] + RING)
                    if nid is not None:
                        nc.scalar.activation(squares_of(nid)[:, 2 * j:2 * j + 2, :], x[:, 2 * j:2 * j + 2, :],
                                             ACT.Square).then_inc(sq_ready, 1)

            def out_slots(name, k):
                return [start[name] + 2 * j + k for j in range(4)]

            def ffn_behind(n):
                return [None, None, None, start[f"ffn{n}"] + FFN_SLOTS - 1]

            act.wait_ge(ones_ready, 1)
            act.wait_ge(cols_loaded, 16)
            nc.scalar.activation(c_act[:, :], col("cond", 0, 16), ACT.Silu).then_inc(cond_act, 1)
            sines(0)
            sines(1)
            tap_squares(0)
            lambdas()
            tap_roots(0)
            act.wait_ge(ada_rows_ready, 3 * ADA_TURNS)
            squares(0, cx)
            for c in range(RING):
                split(c)
            root(0)
            tap_squares(1)
            tap_roots(1)
            high(0, lambda kk: mod[:, 0, kk, 1:2])
            keys_queries(0)
            run_pass(0)
            squares(2, x)
            sums_and_norm(0, 2, 1, lambda kk: mod[:, 0, kk, 0:1])
            keys_queries(1, 1, branch_out, OUT_EVENT[0])
            run_pass(1)
            squares(4, cx, 1)
            sums_and_norm(1, 4, 2, lambda kk: mod[:, 1, kk, 1:2], g_hi)
            squares(3, branch_out, OUT_EVENT[1])
            ctx_keys(0)
            root(3)
            ctx_keys(1)
            squares(5, x, 3)
            ctx_values(0)
            root(5)
            for j in range(3):
                high(3, lambda kk: mod[:, 1, kk, 0:1], h_hi, *BEHIND_SUMS[j])
                if j == 0:
                    split(start["ctx_v"] + 2 + RING)
            ctx_values(1, 1)
            keys_queries(2)
            run_pass(2)
            for j in range(4):
                splits(start["pass2_wo"] + 2 * j)
                square(6, branch_out, OUT_EVENT[2], j)
            root(6)
            gained(4, 5, "ffn10", 7)
            ffn(0, 7)
            gained(5, 6, "mix0", 8, behind=ffn_behind(0))
            splits(start["vqk0"], 2)
            root(8)
            splits(start["vqk0"] + 2, 6)
            attention_a(start["vqk0"] + 8)
            gained(6, 7, "ffn20", 9, out_slots("wo0", 0), out_slots("wo0", 1))
            ffn(1, 9)
            gained(7, 8, "kv_norm", 10, behind=ffn_behind(1), hi=kv_hi)
            splits(start["kv"], 2)
            root(10)
            gained(8, 8, "ffn11", None)
            splits(start["kv"] + 2, 14)
            ffn(2)
            gained(9, 9, "mix1", 12, behind=ffn_behind(2))
            root(12)
            attention_b(start["q1"])
            gained(10, 10, "ffn21", 13, out_slots("wo1", 0), out_slots("wo1", 1))
            ffn(3, 13)
            norm(14, x, 11)

        @block.vector
        def _(dve):
            V = nc.vector
            chain = [0]

            def link(ins):
                chain[0] += 1
                ins.then_inc(dve_chain, 1)
                dve.wait_ge(dve_chain, chain[0])

            def split(c, i=None, per=0):
                if i is None and c >= TOTAL:
                    return
                r = c % RING
                dve.wait_ge(w_hi_ready, c + 1 if i is None else i * per + (c + 1))
                V.tensor_tensor(w_lo[:, r, :], raw[:, r, :], f32(w_hi[:, r, :]), ALU.subtract).then_inc(w_lo_ready, 1)

            def splits(c, n=2):
                for j in range(n):
                    split(c + j + RING)

            def norm_rstd(nid):
                dve.wait_ge(rt_ready, MS_ORDER.index(nid) + 1)
                link(V.reciprocal(rstd, rt))

            def norm_split(nid_lo, src, g, shift, hi=h_hi, lo=h_lo, first=0, end=KD):
                def scale_(kk):
                    V.scalar_tensor_tensor(normed_of(nid_lo)[:, kk, :], src[:, kk, :], g(kk), rstd, ALU.mult,
                                           ALU.mult).then_inc(norm_v, 1)

                def low(kk):
                    dve.wait_ge(norm_hi, KD * nid_lo + kk + 1)
                    V.scalar_tensor_tensor(lo[:, kk, :], normed_of(nid_lo)[:, kk, :], shift(kk), f32(hi[:, kk, :]),
                                           ALU.add, ALU.subtract).then_inc(norm_lo, 1)

                scale_(first)
                scale_(first + 1)
                for kk in range(first, end):
                    if kk + 2 < end:
                        scale_(kk + 2)
                    low(kk)

            def rstd_signal():
                V.memset(signal[:, 0:1], 0.0).then_inc(rstd_ready, 1)

            def post_norm(p, nid):
                take = post_norm_pairs(p, nid)
                for j in range(4):
                    take(j)

            def post_norm_pairs(p, nid):
                dst = sources(p)
                l, w = LAYER_OF[p], 1 if ON_CTX[p] else 0
                norm_rstd(nid)

                def take(j):
                    s = slice(2 * j, 2 * j + 2)
                    for kk in (2 * j, 2 * j + 1):
                        ins = V.scalar_tensor_tensor(branch_out[:, kk, :], branch_out[:, kk, :], gate[:, l, kk, w:w + 1], rstd,
                                                     ALU.mult, ALU.mult)
                    link(ins)
                    V.tensor_tensor(dst[:, s, :], dst[:, s, :], branch_out[:, s, :], ALU.add).then_inc(src_ready, 1)
                return take

            def ada_piece(c, turn, m, banks, i=None):
                if i is None:
                    dve.wait_ge(ada_used, ADA_TURN * turn + 2 * m + 2)
                else:
                    dve.wait_ge(w_used, at(c + 2, i, MERGE_TURN))
                if m == 0 and turn > 0:
                    dve.wait_ge(ada_turned, at(turn, i, 1))
                n = 2 if i is None else 4
                V.tensor_copy(ada_rows[0:n, m * T:(m + 1) * T], PS[0:n, banks[m % 2], 0:T]).then_inc(ada_rows_ready, 1)

            def ada_take(turn, bank, i=None):
                dve.wait_ge(ada_turned, at(turn + 1, i, 1))
                dst = mod_raw[:, 12 * turn:12 * turn + 12] if i is None else mod_raw[:, bass.ds(i * 12, 12)]
                V.tensor_copy(dst, PS[:, bank, 0:12]).then_inc(ada_taken, 1)

            def modulation(turn):
                for m in range(3):
                    ada_piece(None, turn, m, (0, 1))

            def mod_vectors(l):
                dve.wait_ge(ada_taken, ADA_TURNS * (l + 1))
                m = mod_raw[:, :].rearrange("p (f w) -> p f w", w=2)
                for w in range(2):
                    ins = V.tensor_tensor(mod[:, l, :, w], m[:, :, w], col(f"ada_b{l}", 0, 24), ALU.add)
                link(ins)
                for w in range(2):
                    V.scalar_tensor_tensor(gain[:, l, :, w], mod[:, l, KD:2 * KD, w], 1.0, col(f"norm_pre{l}", 0, KD),
                                           ALU.add, ALU.mult)
                    ins = V.tensor_tensor(gate[:, l, :, w], mod[:, l, 2 * KD:3 * KD, w], col(f"norm_post{l}", 0, KD),
                                          ALU.mult)
                link(ins)

            def sine_args(n):
                dve.wait_ge(fil_mm, n + 1)
                link(V.tensor_scalar(arg, PS[:, 2 + n, 0:T], col(f"filter_b{n + 1}"), col(f"freq{n}"), ALU.add, ALU.mult))
                link(V.tensor_scalar(turns, arg, 1 / (2 * math.pi), ROUND, ALU.mult, ALU.add))
                link(V.tensor_scalar(turns, turns, -ROUND, None, ALU.add))
                link(V.scalar_tensor_tensor(arg, turns, -TWO_PI_HI, arg, ALU.mult, ALU.add))
                link(V.scalar_tensor_tensor(arg, turns, -TWO_PI_LO, arg, ALU.mult, ALU.add))
                V.tensor_scalar(arg, arg, PI_SAFE, -PI_SAFE, ALU.min, ALU.max).then_inc(fil_arg, 1)

            def lambdas():
                dve.wait_ge(lam_loaded, 16 * DEPTH)
                for l in range(DEPTH):
                    lam_init = 0.8 - 0.6 * math.exp(-0.3 * l)
                    lp = lam_rows[:, l, :].rearrange("p (a b d) -> p a b d", a=2, b=2)
                    t_ = turns[:, 0:2 * SUB].rearrange("p (a d) -> p a d", a=2)
                    link(V.tensor_tensor(t_, lp[:, :, 0, :], lp[:, :, 1, :], ALU.mult))
                    V.reduce_sum(dots, t_, AX_X).then_inc(lam_dots, 1)
                    dve.wait_ge(lam_exp, l + 1)
                    link(V.tensor_tensor(lam, dot_exp[:, 0:1], dot_exp[:, 1:2], ALU.subtract))
                    V.tensor_scalar(neg_lam[:, l, :], lam, -1.0, -lam_init, ALU.mult, ALU.add)
                    link(V.tensor_scalar(subln_g[:, l, :], col(f"subln{l}"), 1.0 - lam_init, None, ALU.mult))

            def filter_taps(l):
                dve.wait_ge(fil_mm, [3, 6][l])
                dec = fconst("decay").rearrange("p (t c) -> p t c", t=TT)
                for d in range(2):
                    ins = V.tensor_tensor(hw[:, d, :, :], PS[:, 4 + 2 * d:6 + 2 * d, :], dec, ALU.mult)
                link(ins)
                V.memset(hw[0:1, 1, 0, :], 0.0).then_inc(fil_hw, 1)
                dve.wait_ge(fil_hw, l + 1)
                V.tensor_tensor(h_sum, hw[:, 0, :, :], hw[:, 1, :, :], ALU.add)
                V.tensor_tensor(h_dif, hw[:, 0, :, :], hw[:, 1, :, :], ALU.subtract).then_inc(fil_h, 1)

            def filter_spectrum(l):
                dve.wait_ge(fil_rt, l + 1)
                link(V.reciprocal(conv_rs, conv_rt))
                dve.wait_ge(fil_mm, [5, 8][l])
                both = conv_rs.rearrange("p (o c) -> p o c", o=1).to_broadcast([P, 2, BR])
                V.tensor_tensor(spec_re[:, l, :, :], PS[:, 4:6, :], both, ALU.mult)
                V.tensor_tensor(spec_im[:, l, :, :], PS[:, 6:8, :], both, ALU.mult)
                V.tensor_tensor(spec_ny[:, l, :], PS[:, 3, :], conv_rs, ALU.mult).then_inc(fil_taken, 1)

            def rope_turn(n, dst, cos, sin):
                def two(t):
                    return const(t).rearrange("p (o t) -> p o t", o=1).to_broadcast([P, 2, T])
                dve.wait_ge(rope_rot, n + 1)
                V.tensor_tensor(rope_a.rearrange("p (k t) -> p k t", k=2), rope_raw[:, n % 2, :].rearrange("p (k t) -> p k t", k=2),
                                two(cos), ALU.mult)
                link(V.tensor_tensor(rope_b.rearrange("p (k t) -> p k t", k=2),
                                     PS[:, MISC, :].rearrange("p (k t) -> p k t", k=2), two(sin), ALU.mult))
                V.tensor_tensor(dst, rope_a.rearrange("p (k t) -> p k t", k=2), rope_b.rearrange("p (k t) -> p k t", k=2),
                                ALU.add).then_inc(rope_out, 1)

            def take_values(c, bank, dst, done):
                dve.wait_ge(w_used, c + 2)
                V.tensor_copy(dst, PS[:, bank, :].rearrange("p (t c) -> p t c", t=TT)).then_inc(done, 1)

            def softmax_max(p, n):
                nk = P * len(key_tiles(p))
                dve.wait_ge(sc_done, 8 * p + n + 1)
                link(V.reduce_max(mx[:, 0:2], PS[:, SCORES:SCORES + 2, 0:nk], AX_X))
                V.tensor_scalar(neg_max[:, 0:2], mx[:, 0:2], -(SUB ** -0.5), None, ALU.mult).then_inc(nm_ready, 1)

            def softmax_mix(p, n):
                nk = P * len(key_tiles(p))
                dve.wait_ge(p_ready, 8 * p + n + 1)
                link(V.reciprocal(rden[:, 0:2], den[:, 0:2]))
                V.tensor_tensor(wden[:, 0:1], rden[:, 1:2], neg_lam[:, LAYER_OF[p], :], ALU.mult)
                link(V.tensor_scalar(mixw[:, 0:nk], probs[:, 0, 0:nk], rden[:, 0:1], None, ALU.mult))
                V.scalar_tensor_tensor(mixw[:, 0:nk], probs[:, 1, 0:nk], wden[:, 0:1], mixw[:, 0:nk], ALU.mult,
                                       ALU.add).then_inc(mixw_ready, 1)

            def short_conv(p, j):
                l = LAYER_OF[p]
                dve.wait_ge(tap_ready, 6 * p + j + 1)

                def outer(tap, out_tokens, in_tokens):
                    for a_ in range(2):
                        f = 2 * j + a_
                        z = PS[:, j % 2, a_ * T:(a_ + 1) * T]
                        ins = V.scalar_tensor_tensor(hy[:, f, out_tokens], z[:, in_tokens], col(f"short_w{l}", 12 * tap + f),
                                                     hy[:, f, out_tokens], ALU.mult, ALU.add)
                    return ins

                link(outer(0, slice(1, T), slice(0, T - 1)))
                outer(2, slice(0, T - 1), slice(1, T)).then_inc(dve_evac, 1)

            def gating(p, b, c0, split_off=0):
                name = ("ga", "gb", "gc")[b]
                for j in range(2):
                    c = c0 + part[name] + 2 * j
                    if j >= split_off:
                        split(c + RING)
                    s = slice(KB * b + 2 * j, KB * b + 2 * j + 2)
                    dve.wait_ge(act_evac, act_pairs(p, 4 + 2 * b + j))
                    gd = gated[:, j, :, :]
                    link(V.tensor_tensor(gd, y[:, 2 * j:2 * j + 2, :],
                                         gate_act[:, j, :].rearrange("p (k t) -> p k t", k=2), ALU.mult))
                    link(V.tensor_copy(g_hi[:, s, :], gd))
                    V.tensor_tensor(g_lo[:, s, :], gd, f32(g_hi[:, s, :]), ALU.subtract).then_inc(gated_ready, 1)
                    if j >= split_off and (b, j) != (2, 1):
                        split(c + 1 + RING)

            def keys_queries(p, behind_second=None):
                c0 = start[f"pass{p}"]
                on_x = not ON_CTX[p]
                rb = ROPE_BASE[p]
                base = 0 if on_x else 4
                dsts = [k[:, base:base + 2, :], q[:, 0:2, :], k[:, base + 2:base + 4, :], q[:, 2:4, :]]
                for j in range(4):
                    c = c0 + 2 * j
                    split(c + RING)
                    if on_x:
                        rope_copy(rb + j, j % 2, c)
                        split(c + 1 + RING)
                        if j >= 1:
                            rope_turn(rb + j - 1, dsts[j - 1], "cos_a", "sin_a")
                        if j == 1 and behind_second is not None:
                            post_norm(*behind_second)
                    else:
                        dve.wait_ge(w_used, c + 2)
                        V.tensor_copy(dsts[j], PS[:, j % 2, :].rearrange("p (k t) -> p k t", k=2)).then_inc(dve_evac, 1)
                        split(c + 1 + RING)
                kt = 0 if on_x else 2
                split(c0 + part["v"] + RING)
                take_values(c0 + part["v"], 0, v[:, kt:kt + 2, 0:T], dve_evac)
                if on_x:
                    rope_turn(rb + 3, dsts[3], "cos_a", "sin_a")
                split(c0 + part["v"] + 1 + RING)

            def run_pass(p):
                l = LAYER_OF[p]
                c0 = start[f"pass{p}"]
                kt = 0 if not ON_CTX[p] else 2
                for n in range(8):
                    softmax_max(p, n)
                    if n == 1:
                        take_values(c0 + part["v"] + 2, 1, v[:, kt:kt + 2, T:2 * T], dve_evac)
                    elif n >= 2:
                        short_conv(p, n - 2)
                    softmax_mix(p, n)
                    splits(c0 + part["v"] + 2 + 2 * n)
                V.tensor_tensor(u, u, hy[:, 8:12, :], ALU.mult).then_inc(u_ready, 1)
                splits(c0 + part["gu"] + 2)
                dve.wait_ge(head_rt_ready, p + 1)
                link(V.reciprocal(head_rs, head_rt))
                for h in range(HEADS_A):
                    for qt in range(TT):
                        ins = V.tensor_scalar(head_y[:, h, qt, :], PS[:, HEADS_OUT + qt, h * P:(h + 1) * P],
                                              head_rs[:, 2 * h + qt:2 * h + qt + 1], None, ALU.mult)
                ins.then_inc(head_y_ready, 1)
                dve.wait_ge(u_t, p + 1)
                V.tensor_copy(u_tok[:, 0, :], PS[:, TURN, :])
                V.tensor_copy(u_tok[:, 1, :], PS[:, MISC, :]).then_inc(u_tok_ready, 1)
                splits(c0 + part["gv"])
                dve.wait_ge(dft_done, p + 1)
                ur, ui = PS[:, 0:2, :], PS[:, HEADS_OUT:HEADS_OUT + 2, :]
                yr, yi = yspec[:, 0:2, :], yspec[:, 2:4, :]
                V.tensor_tensor(yr, ur, spec_re[:, l, :, :], ALU.mult)
                link(V.tensor_tensor(prod, ui, spec_im[:, l, :, :], ALU.mult))
                link(V.tensor_tensor(yr, yr, prod, ALU.subtract))
                splits(c0 + part["gv"] + 2)
                dve.wait_ge(head_t, p + 1)
                for b in range(2):
                    ins = V.tensor_scalar(y[:, 2 * b:2 * b + 2, :], PS[:, [TURN, MISC][b], :].rearrange("p (k t) -> p k t", t=T),
                                          subln_g[:, l, :], None, ALU.mult)
                ins.then_inc(y_ready, 1)
                split(c0 + part["ga"] + RING)
                V.tensor_tensor(yi, ur, spec_im[:, l, :, :], ALU.mult)
                V.tensor_tensor(prod[:, 0, :], ui[:, 0, :], spec_ny[:, l, :], ALU.mult)
                link(V.tensor_tensor(prod[:, 1, :], ui[:, 1, :], spec_re[:, l, 1, :], ALU.mult))
                V.tensor_tensor(yi, yi, prod, ALU.add).then_inc(yspec_ready, 1)
                split(c0 + part["ga"] + 1 + RING)
                dve.wait_ge(act_evac, act_pairs(p, 3))
                link(V.reduce_sum(ln_sum, gv[:, :, :], AX_X))
                for t in range(TT):
                    ins = V.scalar_tensor_tensor(gvc[:, t, :], ln_sum[:, t:t + 1].to_broadcast([P, BR]), -1.0 / BR, gv[:, t, :],
                                                 ALU.mult, ALU.add)
                ins.then_inc(ln_centered, 1)
                dve.wait_ge(y_ready, p + 1)
                gating(p, 0, c0, 1)
                dve.wait_ge(ln_rt_ready, p + 1)
                dve.wait_ge(layer_loaded, 16 * (l + 1))
                link(V.reciprocal(ln_rs, ln_rt))
                for t in range(TT):
                    ins = V.scalar_tensor_tensor(gvc[:, t, :], gvc[:, t, :], ln_rs[:, t:t + 1], row("ln_g"), ALU.mult,
                                                 ALU.mult)
                link(ins)
                for t in range(TT):
                    ins = V.tensor_tensor(lnv[:, t, :], gvc[:, t, :], row("ln_b"), ALU.add)
                ins.then_inc(lnv_ready, 1)
                dve.wait_ge(conv_done, p + 1)
                for c in range(KB):
                    ins = V.scalar_tensor_tensor(y[:, c, :], u[:, c, :], col(f"conv_bias{l}", c),
                                                 PS[:, [TURN, MISC][c // 2], (c % 2) * T:(c % 2 + 1) * T], ALU.mult, ALU.add)
                link(ins)
                link(V.tensor_tensor(y[:, :, :], y[:, :, :], hy[:, 0:4, :], ALU.mult))
                gating(p, 1, c0)
                dve.wait_ge(mixed, p + 1)
                bias = row("mix_bias").rearrange("p (k o t) -> p k o t", k=KB, o=1).to_broadcast([P, KB, TT, P])
                link(V.tensor_tensor(y[:, :, :].rearrange("p k (c t) -> p k c t", c=TT),
                                     PS[:, SCORES:SCORES + 2, :].rearrange("p b (k c t) -> p (b k) c t", c=TT, t=P),
                                     bias, ALU.add))
                link(V.tensor_tensor(y[:, :, :], y[:, :, :], gu[:, :, :], ALU.mult))
                V.memset(signal[:, 0:1], 0.0).then_inc(merge_free, 2)
                gating(p, 2, c0)
                V.memset(signal[:, 1:2], 0.0).then_inc(merge_free, 1)
                each, per = (5, MERGE_TURN) if p == 1 else (3, 9)
                with dve.Fori(0, 4) as i:
                    for b in range(3):
                        c = start[f"pass{p}_merge"] + each * b
                        for j in range(-1, each - 1):
                            split(c + j + RING, i, per)
                            if p == 1 and j == 2:
                                ada_piece(c + 1, ADA_TURNS, b, (6, 7), i)
                        dve.wait_ge(sel_ready, i * 3 + (12 * p + b + 1))
                        m = merged.rearrange("p k t -> p (k t)")[:, bass.ds(i * 512, 512)]
                        V.tensor_tensor(m if b == 0 else term, sel[:, b, :], PS[:, 2 * b, :], ALU.mult).then_inc(merge_free, 1)
                        if b >= 1:
                            dve.wait_ge(merge_free, i * 3 + (15 * p + 3 + b + 1))
                            if b == 2:
                                dve.wait_ge(merge_added, i * 2 + (8 * p + 1))
                            V.tensor_tensor(m, m, term, ALU.add).then_inc(merge_added, 1)
                    if p == 1:
                        ada_take(ADA_TURNS, 7, i)
                for kk in range(KD):
                    dve.wait_ge(m_hi, KD * p + kk + 1)
                    hi, lo = merged_parts(p)
                    V.tensor_tensor(lo[:, kk, :], merged[:, kk, :], f32(hi[:, kk, :]), ALU.subtract).then_inc(m_lo, 1)
                    if kk == 1:
                        split(start[f"pass{p}_wo"] - 1 + RING)

            def take_branch_sum(p, j):
                c = start[f"pass{p}_wo"] + 2 * j
                split(c + RING)
                dve.wait_ge(w_used, c + 2)
                V.tensor_copy(branch_out[:, 2 * j:2 * j + 2, :],
                              PS[:, 4 + j % 2, :].rearrange("p (k t) -> p k t", k=2)).then_inc(src_ready, 1)
                split(c + 1 + RING)

            def sums_and_norm(p, nid, nid_lo, src, g, shift, hi=h_hi, lo=h_lo):
                for j in range(4):
                    take_branch_sum(p, j)
                    if j == 0:
                        norm_rstd(nid)
                    if j < 3:
                        norm_split(nid_lo, src, g, shift, hi, lo, *BEHIND_SUMS[j])

            def rope_copy(n, bank, c, scaled=False):
                dve.wait_ge(w_used, c + 2)
                if n >= 2:
                    dve.wait_ge(rope_rot, n - 1)
                if scaled:
                    ins = V.tensor_tensor(rope_raw[:, n % 2, :].rearrange("p (k t) -> p k t", k=2),
                                          PS[:, bank, :].rearrange("p (k t) -> p k t", k=2), rstd_pair, ALU.mult)
                else:
                    ins = V.tensor_copy(rope_raw[:, n % 2, :], PS[:, bank, :])
                ins.then_inc(rope_in, 1)
                dve.wait_ge(rope_in, n + 1)

            def gained(nid_lo, gains, makes, hi=h_hi, lo=h_lo, behind=None, lag=1):
                def low(j):
                    for kk in (2 * j, 2 * j + 1):
                        dve.wait_ge(norm_hi, KD * nid_lo + kk + 1)
                        V.scalar_tensor_tensor(lo[:, kk, :], x[:, kk, :], col(gains, kk), f32(hi[:, kk, :]), ALU.mult,
                                               ALU.subtract).then_inc(norm_lo, 1)

                behind = behind or [None] * 4
                for j in range(4):
                    makes(j)
                    if j >= lag:
                        low(j - lag)
                    if j == 3 and lag:
                        low(3)
                    if behind[j] is not None:
                        split(behind[j] + RING)

            def down_sum(n):
                def take(j):
                    if j < 3:
                        dve.wait_ge(down_done, 3 * n + j + 1)
                    else:
                        dve.wait_ge(w_used, start[f"ffn{n}"] + FFN_SLOTS)
                    s = slice(2 * j, 2 * j + 2)
                    V.scalar_tensor_tensor(x[:, s, :], PS[:, 4 + j, :].rearrange("p (k t) -> p k t", k=2), 0.5, x[:, s, :],
                                           ALU.mult, ALU.add).then_inc(src_ready, 1)
                return take

            def banks_free(sets, which=0):
                V.memset(signal[:, which:which + 1], 0.0).then_inc(gu_free, sets)

            def ffn(n, nid=None):
                c0 = start[f"ffn{n}"]

                def post(c, s, i, pr, nid=None):
                    b = FPAIRS * n + pr + 1

                    def two(t):
                        return t.rearrange("p (k t) -> p k t", k=2)

                    split(c + RING, i, 12)
                    if nid is not None:
                        split(c + 1 + RING, i, 12)
                        norm_rstd(nid)
                    dve.wait_ge(w_used, at(c + 2, i, 12))
                    V.tensor_tensor(two(gate_in[:, s, :]), two(PS[:, 2 * s, :]), rstd_pair, ALU.mult).then_inc(gate_normed, 1)
                    if nid is None:
                        split(c + 1 + RING, i, 12)
                    dve.wait_ge(silu_ready, at(b, i, 2))
                    link_at(V.tensor_tensor(two(silu[:, s, :]), two(silu[:, s, :]), rstd_pair, ALU.mult), b, i)
                    split(c + 2 + RING, i, 12)
                    dve.wait_ge(w_used, at(c + 4, i, 12))
                    V.tensor_tensor(act_f, silu[:, s, :], PS[:, 2 * s + 1, :], ALU.mult).then_inc(gu_free, 1)
                    dve.wait_ge(gu_free, at(13 * n + 2 + pr + 1, i, 2))
                    hi = act_hi[:, s, :, :].rearrange("p f t -> p (f t)")
                    lo = act_lo[:, s, :, :].rearrange("p f t -> p (f t)")
                    V.tensor_copy(hi, act_f).then_inc(act_hi_ready, 1)
                    dve.wait_ge(act_hi_ready, at(b, i, 2))
                    V.tensor_tensor(lo, act_f, f32(hi), ALU.subtract).then_inc(act_ready, 1)
                    split(c + 3 + RING, i, 12)

                def link_at(ins, b, i):
                    ins.then_inc(silu_scaled, 1)
                    dve.wait_ge(silu_scaled, at(b, i, 2))

                def downs(c, i):
                    for f in range(2):
                        split(c + f + RING, i, 12)

                post(c0, 0, None, 0, nid)
                with dve.Fori(0, 4) as i:
                    for e in range(2):
                        c = c0 + 4 + 6 * e
                        post(c, (1 + e) % 2, i, 1 + e)
                        downs(c + 4, i)
                for pr in (9, 10):
                    c = c0 + 4 + 6 * (pr - 1)
                    post(c, pr % 2, None, pr)
                    downs(c + 4, None)
                split(c0 + FFN_SLOTS - 2 + RING)
            def softmax2(n, unit, table):
                b = unit % 2
                dve.wait_ge(sc2_done, 8 * n + unit + 1)
                bias = const(table).rearrange("p (o s) -> p o s", o=1).to_broadcast([P, 2, SEG])
                V.scalar_tensor_tensor(biased[:, b, :, :], PS[:, SCORES:SCORES + 2, 0:SEG], HD ** -0.5, bias, ALU.mult,
                                       ALU.add).then_inc(biased_ready, 1)
                dve.wait_ge(biased_ready, 8 * n + unit + 1)
                V.reduce_max(mx[:, 4 * b:4 * b + 2], biased[:, b, :, 0:P], AX_X)
                link(V.reduce_max(mx[:, 4 * b + 2:4 * b + 4], biased[:, b, :, P:SEG], AX_X))
                V.tensor_scalar(neg_max[:, 4 * b:4 * b + 4], mx[:, 4 * b:4 * b + 4], -1.0, None, ALU.mult).then_inc(nm2_ready, 1)

            def normalize2(n, unit):
                b = unit % 2
                dve.wait_ge(p2_ready, 8 * n + unit + 1)
                link(V.reciprocal(rden[:, 4 * b:4 * b + 4], den[:, 4 * b:4 * b + 4]))
                for h in range(2):
                    m = 4 * b + h
                    V.tensor_scalar(probs2[:, b, h, 0:P], probs2[:, b, h, 0:P], rden[:, m:m + 1], None, ALU.mult)
                    ins = V.tensor_scalar(probs2[:, b, h, P:SEG], probs2[:, b, h, P:SEG], rden[:, m + 2:m + 3], None, ALU.mult)
                ins.then_inc(p2n_ready, 1)

            def heads_low(n, unit):
                dve.wait_ge(o2_hi, 8 * n + unit + 1)
                V.tensor_tensor(g_lo[:, unit, :], PS[:, 6, 0:T], f32(g_hi[:, unit, :]), ALU.subtract).then_inc(o2_ready, 1)

            def attention_a(c0, n0, table):
                for unit in range(-3, 9):
                    ahead, nxt = unit + 3, unit + 1
                    if 0 <= nxt < 8:
                        softmax2(0, nxt, table)
                    if 1 <= ahead <= 8:
                        split(c0 + 2 * ahead - 1 + RING)
                        rope_turn(n0 + ahead - 1, qk[:, ahead - 1:ahead + KD:KD, :], "cos_b", "sin_b")
                    if ahead < 8:
                        split(c0 + 2 * ahead + RING)
                    if 0 <= unit < 8:
                        normalize2(0, unit)
                    if unit >= 1:
                        heads_low(0, unit - 1)
                    if ahead < 8:
                        rope_copy(n0 + ahead, ahead % 2, c0 + 2 * ahead, True)

            def attention_b(c0, n0, table):
                for unit in range(-5, 9):
                    ahead, nxt = unit + 5, unit + 1
                    if 0 <= nxt < 8:
                        softmax2(1, nxt, table)
                    if 0 <= unit < 8:
                        normalize2(1, unit)
                    if ahead < 8:
                        split(c0 + ahead + RING)
                        if ahead % 2 == 1:
                            rope_copy(n0 + ahead // 2, (ahead // 2) % 2, c0 + ahead - 1, True)
                    if 2 <= ahead <= 8 and ahead % 2 == 0:
                        rope_turn(n0 + ahead // 2 - 1, q[:, ahead - 2:ahead, :], "cos_b", "sin_b")
                    if unit >= 1:
                        heads_low(1, unit - 1)

            def rstd_columns(turn):
                dve.wait_ge(rstd_turned, turn + 1)
                link(V.tensor_copy(rstd_tok, PS[:, 6, 0:TT]))

            def take_normed_values(c, bank, dst):
                dve.wait_ge(w_used, c + 2)
                for t in range(TT):
                    ins = V.tensor_scalar(dst[:, t, :], PS[:, bank, t * T:(t + 1) * T], rstd_tok[:, t:t + 1], None, ALU.mult)
                ins.then_inc(qkv_evac, 1)

            def out_sum(name):
                def take(j):
                    c0 = start[name]
                    s = slice(2 * j, 2 * j + 2)
                    split(c0 + 2 * j + RING)
                    dve.wait_ge(w_used, c0 + 2 * j + 2)
                    V.tensor_tensor(x[:, s, :], x[:, s, :], PS[:, 4 + j % 2, :].rearrange("p (k t) -> p k t", k=2),
                                    ALU.add).then_inc(src_ready, 1)
                return take

            def out_behind(name):
                return [start[name] + 2 * j + 1 for j in range(4)]

            def ffn_behind(n):
                return [None, None, None, start[f"ffn{n}"] + FFN_SLOTS - 1]

            def pairs_of(t):
                return [t[:, 2 * j:2 * j + 2, :] for j in range(4)]

            V.memset(ones[:, :], 1.0 / D)
            V.memset(zeros[:, :], 0.0)
            V.memset(eps[:, :], EPS).then_inc(ones_ready, 1)
            dve.wait_ge(cond_act, 1)
            cond = c_act[:, :].rearrange("p (k w) -> p k w", w=2)
            V.tensor_copy(c_parts[:, :, 0:2], cond).then_inc(cond_hi, 1)
            dve.wait_ge(cond_hi, 1)
            V.tensor_tensor(c_parts[:, :, 2:4], cond, f32(c_parts[:, :, 0:2]), ALU.subtract).then_inc(cond_ready, 1)
            modulation(0)
            sine_args(0)
            ada_take(0, 1)
            modulation(1)
            sine_args(1)
            ada_take(1, 1)
            modulation(2)
            filter_taps(0)
            ada_take(2, 1)
            lambdas()
            modulation(3)
            filter_spectrum(0)
            ada_take(3, 1)
            mod_vectors(0)
            filter_taps(1)
            for c in range(RING):
                split(c)
            norm_rstd(0)
            norm_split(0, cx, lambda kk: gain[:, 0, kk, 1:2], lambda kk: mod[:, 0, kk, 1:2])
            filter_spectrum(1)
            keys_queries(0)
            run_pass(0)
            sums_and_norm(0, 2, 1, x, lambda kk: gain[:, 0, kk, 0:1], lambda kk: mod[:, 0, kk, 0:1])
            keys_queries(1, behind_second=(0, 1))
            run_pass(1)
            mod_vectors(1)
            sums_and_norm(1, 4, 2, cx, lambda kk: gain[:, 1, kk, 1:2], lambda kk: mod[:, 1, kk, 1:2], g_hi, g_lo)
            c = start["ctx_k"]
            splits(c)
            post = post_norm_pairs(1, 3)
            post(0)
            post(1)
            split(c + 2 + RING)
            post(2)
            post(3)
            split(c + 3 + RING)
            splits(c + 4)
            norm_rstd(5)
            for j in range(3):
                norm_split(3, x, lambda kk: gain[:, 1, kk, 0:1], lambda kk: mod[:, 1, kk, 0:1], h_hi, h_lo, *BEHIND_SUMS[j])
                if j == 0:
                    split(c + 6 + RING)
            split(c + 7 + RING)
            keys_queries(2)
            run_pass(2)
            for j in range(4):
                take_branch_sum(2, j)
            post = post_norm_pairs(2, 6)
            banks_free(2)
            gained(4, "ffn10", post)
            ffn(0, 7)
            gained(5, "mix0", down_sum(0), behind=ffn_behind(0))
            c = start["vqk0"]
            splits(c)
            norm_rstd(8)
            rstd_signal()
            splits(c + 2)
            rstd_columns(0)
            for j in range(4):
                if j >= 2:
                    split(c + 2 * j + RING)
                take_normed_values(c + 2 * j, j, v2[:, :, j * T:(j + 1) * T])
                if j >= 2:
                    split(c + 2 * j + 1 + RING)
            attention_a(c + 8, 8, "bias_dilated")
            banks_free(2)
            gained(6, "ffn20", out_sum("wo0"), behind=out_behind("wo0"), lag=0)
            ffn(1, 9)
            gained(7, "kv_norm", down_sum(1), kv_hi, kv_lo, ffn_behind(1))
            c = start["kv"]
            splits(c)
            norm_rstd(10)
            rstd_signal()
            for j in range(4):
                rope_copy(16 + j, j, c + 2 * j, True)
                if j >= 1:
                    splits(c + 2 * j)
                    rope_turn(16 + j - 1, pairs_of(k)[j - 1], "cos_b", "sin_b")
            gained(8, "ffn11", lambda j: None)
            rstd_columns(1)
            for j in range(4):
                split(c + 8 + 2 * j + RING)
                take_normed_values(c + 8 + 2 * j, j, v2[:, :, j * T:(j + 1) * T])
                split(c + 8 + 2 * j + 1 + RING)
                if j == 0:
                    rope_turn(19, pairs_of(k)[3], "cos_b", "sin_b")
                if j % 2 == 1:
                    banks_free(1, j // 2)
            ffn(2)
            gained(9, "mix1", down_sum(2), behind=ffn_behind(2))
            norm_rstd(12)
            attention_b(start["q1"], 20, "bias_causal")
            banks_free(2)
            gained(10, "ffn21", out_sum("wo1"), behind=out_behind("wo1"), lag=0)
            ffn(3, 13)
            for j in range(4):
                down_sum(3)(j)
            norm_rstd(14)
            for kk in range(KD):
                V.scalar_tensor_tensor(normed[:, kk, :], x[:, kk, :], col("final_norm", kk), rstd, ALU.mult,
                                       ALU.mult).then_inc(out_ready, 1)


OUT_EVENT = [0, 2, 4]
BEHIND_SUMS = [(0, 2), (2, 5), (5, 8)]
MS_ORDER = [0, 2, 1, 4, 3] + list(range(5, 11)) + [12, 13, 14]


def constants():
    f = np.float32
    t = np.arange(T)
    out = {"ident": np.eye(P)}

    def rotary(width, ang_of, perm_name, cos_name, sin_name):
        cos, sin, perm = np.ones((P, T)), np.zeros((P, T)), np.zeros((P, P))
        for i in range(P):
            found = ang_of(i % width)
            if found is None:
                continue
            ang, first, half = found
            cos[i], sin[i] = np.cos(ang), np.sin(ang)
            if first:
                perm[i + half, i] = -1.0
            else:
                perm[i - half, i] = 1.0
        out[perm_name], out[cos_name], out[sin_name] = perm, cos, sin

    nf = SUB // 4

    def axial(i):
        axis, rest = divmod(i, 2 * nf)
        half, fr = divmod(rest, nf)
        inv = f(10000.0) ** (-np.arange(nf, dtype=f) / f(nf))
        pos = (t // 64 if axis == 0 else t % 64).astype(f)
        return (pos * inv[fr]).astype(f), half == 0, nf

    def partial(i):
        half_dim = HD // 8
        if i >= 2 * half_dim:
            return None
        half, fr = divmod(i, half_dim)
        inv = f(500000.0) ** (-np.arange(half_dim, dtype=f) / f(half_dim))
        return (t.astype(f) * inv[fr]).astype(f), half == 0, half_dim

    rotary(SUB, axial, "perm_a", "cos_a", "sin_a")
    rotary(HD, partial, "perm_b", "cos_b", "sin_b")

    diff = t[:, None] - t[None, :]
    causal = diff >= 0
    count = sum((causal & (diff <= w) & (diff % d == 0)).astype(int) for w, d in ((128, 1), (512, 4), (2048, 16)))
    for name, n in (("bias_dilated", count), ("bias_causal", causal.astype(int))):
        b = np.where(n > 0, np.log(np.maximum(n, 1)), -1e30)
        out[name] = np.concatenate([b[0:P, 0:P], b[P:T, :]], axis=1)

    def tiled(m):
        return m.reshape(-1, P, m.shape[1]).transpose(1, 0, 2).reshape(P, -1)

    w = np.pi * np.outer(t, t) / T
    sign = np.where(t % 2 == 0, 1.0, -1.0)
    out["dft_cos"] = tiled(np.cos(w))
    s = -np.sin(w)
    out["dft_sin_k"] = tiled(s)
    s = s.copy()
    s[:, 0] = sign
    out["dft_sin_u"] = tiled(s)
    ny = np.cos(w)[:, 0:P].copy()
    ny[:, 0] = sign
    out["dft_nyq"] = tiled(ny)
    weight = np.where(t == 0, 1.0, 2.0)[:, None] / (2 * T)
    re, im = weight * np.cos(w), -weight * np.sin(w)
    im[0, :] = sign / (2 * T)
    out["idft"] = tiled(np.concatenate([re, im], axis=0))
    lin = np.linspace(0.0, 1.0, T)
    lo, hi = math.log(1e-2) / 1.5, math.log(1e-2) / 0.3
    out["decay"] = tiled(np.exp(-lin[:, None] * np.abs(np.linspace(lo, hi, BR))[None, :]))
    wpos = (2.0 * math.pi / T) * t[None, :]
    bands = np.linspace(1e-4, 15, 16)[:, None]
    z = np.concatenate([lin[None, :], np.cos(bands * wpos), -np.sin(bands * wpos)], axis=0)
    out["filter_z"] = np.tile(np.concatenate([z, np.zeros((64 - 33, T))], axis=0), (DEPTH, 1))
    return [np.ascontiguousarray(np.concatenate([out[n].astype(f) for n, _ in part], axis=1))
            for part in (CONSTS, FILTER_CONSTS)]


def pack(inputs):
    g = {n: np.asarray(a) for n, a in inputs.items()}
    slots = []

    def tiles(w, lo=0, hi=None):
        w = w[:, lo:hi]
        for c in range(0, w.shape[1], P):
            slots.append(w[:, c:c + P].reshape(KD, P, P).transpose(1, 0, 2).reshape(P, SLOT))

    def token(w, lo=0, hi=None):
        w = w[:, lo:hi]
        for c in range(0, w.shape[1], T):
            for r in range(0, D, D // 2):
                slots.append(w[r:r + D // 2, c:c + T].reshape(4, P, T).transpose(1, 0, 2).reshape(P, SLOT))

    for l in range(DEPTH):
        token(g["ada_w"][l])
        w = g["w_in"][l]
        for c in range(0, 512, T):
            tiles(w, c, c + T)
            tiles(w, 1024 + c, 1024 + c + T)
        token(w, 512, 1024)
        tiles(w, 2048, 3584)
        tiles(w, 4096, 4608)
        token(w, 4608, 5120)
        tiles(w, 1536, 2048)
        tiles(w, 3584, 4096)
        tiles(w, 5120, 5632)
        for c in range(0, D, T):
            for b in range(3):
                slots.append(g["w_branch"][l, b][:, c:c + T].reshape(KB, P, T).transpose(1, 0, 2).reshape(P, SLOT))
                tiles(w, 5632 + b * D + c, 5632 + b * D + c + T)
        tiles(g["w_out"][l])

    def ffn(n, l):
        gate, up, down = (g[f"ffn{n}_w_{x}_2"][l] for x in ("gate", "up", "down"))
        for p in range(FPAIRS + 1):
            if p < FPAIRS:
                tiles(gate, 2 * P * p, 2 * P * (p + 1))
                tiles(up, 2 * P * p, 2 * P * (p + 1))
            if p >= 1:
                for f in (2 * p - 2, 2 * p - 1):
                    slots.append(down[f * P:(f + 1) * P, :])

    ffn(1, 0)
    token(g["a_w_qkv_2"][0], 2 * D, 3 * D)
    for c in range(0, D, P):
        tiles(g["a_w_qkv_2"][0], c, c + P)
        tiles(g["a_w_qkv_2"][0], D + c, D + c + P)
    tiles(g["a_w_o_2"][0])
    ffn(2, 0)
    tiles(g["kv_w_2"], 0, D)
    token(g["kv_w_2"], D, 2 * D)
    ffn(1, 1)
    tiles(g["b_w_q_2"][0])
    tiles(g["b_w_o_2"][0])
    ffn(2, 1)
    weights = np.stack(slots)

    def column(v):
        return v.reshape(-1, P).T

    def padded(v, rows):
        return np.concatenate([v, np.zeros((rows - v.shape[0], v.shape[1]), v.dtype)], axis=0)

    cols = {"cond": np.stack([column(g["c"][0]), column(g["c_ctx"])], axis=2).reshape(P, 16),
            "ada_sum": padded(np.tile(np.eye(2, dtype=np.float32), (2, 1)), P),
            "kv_norm": column(g["kv_norm_2"]), "final_norm": column(g["final_norm_2"])}
    for name, v in (("filter_b1", g["hy_f_b1"]), ("filter_b2", g["hy_f_b2"]), ("freq0", g["hy_f_freq"][:, 0]),
                    ("freq1", g["hy_f_freq"][:, 1])):
        cols[name] = v.reshape(P, 1)
    layers, filters, lams = [], [], []
    for l in range(DEPTH):
        cols[f"norm_pre{l}"] = column(g["norm_pre"][l])
        cols[f"norm_post{l}"] = column(g["norm_post"][l])
        cols[f"ada_b{l}"] = column(g["ada_b"][l])
        cols[f"subln{l}"] = column(g["da_subln"][l])
        cols[f"short_w{l}"] = column(g["hy_short_w"][l].reshape(-1))
        cols[f"short_b{l}"] = column(g["hy_short_b"][l])
        cols[f"conv_bias{l}"] = column(g["hy_bias"][l])
        cols[f"ffn1{l}"] = column(g["ffn1_norm_2"][l])
        cols[f"mix{l}"] = column(g["mix_norm_2"][l])
        cols[f"ffn2{l}"] = column(g["ffn2_norm_2"][l])
        mix_bias = np.repeat(g["gm_bs"][l].reshape(KB, 2, 1, P), SUB, axis=2).reshape(KB, P, P)
        layers.append(np.concatenate([np.broadcast_to(g["gm_ln_g"][l], (P, BR)), np.broadcast_to(g["gm_ln_b"][l], (P, BR)),
                                      mix_bias.transpose(1, 0, 2).reshape(P, -1),
                                      g["gm_ws"][l].transpose(2, 0, 1).reshape(P, -1)], axis=1))
        filters.append(np.concatenate([padded(g["hy_f_w1"][l], 64), g["hy_f_w2"][l], g["hy_f_w3"][l]], axis=1))
        lams.append(np.broadcast_to(g["da_lambda"][l].reshape(-1), (P, 4 * SUB)))

    consts, filter_consts = constants()

    def stream(a):
        return np.ascontiguousarray(a[0].T.reshape(KD, P, T).transpose(1, 0, 2))

    return {"weights": weights, "x_in": stream(g["x"]), "ctx_in": stream(g["ctx"]),
            "cols_in": np.ascontiguousarray(np.concatenate([cols[n] for n, _ in COLUMNS], axis=1)),
            "consts_in": consts, "filter_consts_in": filter_consts, "layer_in": np.stack(layers), "filter_in": np.concatenate(filters, axis=0),
            "lam_in": np.stack(lams)}


def kernel(**inputs):
    import concourse.bacc as bacc
    from concourse.bass_utils import run_bass_kernel_spmd

    nc = bacc.Bacc("TRN2", target_bir_lowering=False, num_devices=1)
    arrays = pack(inputs)
    aps = {n: nc.dram_tensor(n, a.shape, mybir.dt.from_np(a.dtype), kind="ExternalInput").ap()
           for n, a in arrays.items()}
    out = nc.dram_tensor("out", (P, KD, T), F32, kind="ExternalOutput").ap()
    build(nc, out=out, **aps)
    r = run_bass_kernel_spmd(nc, [arrays], core_ids=[0])
    res = np.asarray(r.results[0]["out"])
    return np.ascontiguousarray(res.transpose(2, 1, 0).reshape(1, T, D))
```
